# Optimizing a Trainium2 kernel written in Bass

```python
import math
import jax
import jax.numpy as jnp
from jax import lax
import numpy as np

D_MODEL = 1024
BATCH = 1
SEQ = 1024
DEPTH = 1

GRID_W = 64
CTX_LEN = 256

RET_HEADS = 4
RET_DV = D_MODEL // (2 * RET_HEADS)
RET_DK = RET_DV // 2
HG_HEADS = 4
HG_DV = D_MODEL // (2 * HG_HEADS)
HG_DK = HG_DV
RET_QK_W = RET_HEADS * RET_DK
RET_V_W = RET_HEADS * RET_DV
HG_K_W = HG_HEADS * HG_DK
HG_V_W = HG_HEADS * HG_DV
PROJ_WIDTHS = (RET_QK_W, RET_QK_W, RET_V_W, RET_V_W, HG_K_W, HG_K_W, HG_K_W, HG_V_W, HG_V_W)
PROJ_W = sum(PROJ_WIDTHS)

CHUNK = 64
ROPE_BASE = 10000.0
EPS = 1e-6

N_EXPERTS = 32
TOP_K = 4
D_FF = D_MODEL
SWIGLU_LIMIT = 7.0
SWIGLU_ALPHA = 1.702
MOE_BLOCK = 128

kernel_name = "hybrid_retention_hgrn2_moe_dit"

def _rms(x):
    xf = x.astype(jnp.float32)
    return xf * lax.rsqrt(jnp.mean(xf * xf, axis=-1, keepdims=True) + EPS)

def rms_norm(x, w):
    return _rms(x) * w.astype(jnp.float32)

def to_heads(t, n_heads):
    b, n, _ = t.shape
    return t.reshape(b, n, n_heads, -1).transpose(0, 2, 1, 3)

def from_heads(t):
    b, h, n, d = t.shape
    return t.transpose(0, 2, 1, 3).reshape(b, n, h * d)

def axial_rope_tables(row, col):
    n_freq = RET_DK // 4
    inv = ROPE_BASE ** (-jnp.arange(n_freq, dtype=jnp.float32) / n_freq)
    ang = jnp.concatenate([row[:, None] * inv, col[:, None] * inv], axis=-1)
    return jnp.cos(ang), jnp.sin(ang)

def apply_rope(t, cos, sin):
    half = t.shape[-1] // 2
    t1, t2 = t[..., :half], t[..., half:]
    return jnp.concatenate([t1 * cos - t2 * sin, t1 * sin + t2 * cos], axis=-1)

def chunk_recurrence(q, k, v, log_a, s0):
    B, H, N, dk = q.shape
    dv = v.shape[-1]
    nc = N // CHUNK

    def to_chunks(t):
        return t.astype(jnp.float32).reshape(B, H, nc, CHUNK, t.shape[-1]).transpose(2, 0, 1, 3, 4)

    causal = jnp.tril(jnp.ones((CHUNK, CHUNK), dtype=bool))[:, :, None]

    def step(state, blk):
        qc, kc, vc, la = blk
        b = jnp.cumsum(la, axis=2)
        rel = b[:, :, :, None, :] - b[:, :, None, :, :]
        decay = jnp.exp(jnp.where(causal, rel, -jnp.inf))
        if la.shape[-1] == 1:
            scores = jnp.einsum('bhtd,bhsd->bhts', qc, kc) * decay[..., 0]
        else:
            scores = jnp.einsum('bhtsd,bhsd->bhts', qc[:, :, :, None, :] * decay, kc)
        out = (jnp.einsum('bhts,bhsv->bhtv', scores, vc)
               + jnp.einsum('bhtd,bhdv->bhtv', qc * jnp.exp(b), state))
        b_end = b[:, :, -1:, :]
        new_state = (jnp.exp(b_end[:, :, 0, :])[..., None] * state
                     + jnp.einsum('bhsd,bhsv->bhdv', kc * jnp.exp(b_end - b), vc))
        return new_state, out

    state, out = lax.scan(step, s0, (to_chunks(q), to_chunks(k), to_chunks(v), to_chunks(log_a)))
    return out.transpose(1, 2, 0, 3, 4).reshape(B, H, N, dv), state

def _flip(t):
    return jnp.flip(t, axis=2)

def bidirectional_scan(c_fwd, c_bwd, x_fwd, x_bwd):
    B, H, _, dk = c_fwd[0].shape
    dv = c_fwd[2].shape[-1]
    s0 = jnp.zeros((B, H, dk, dv), jnp.float32)
    oc_f, sc_f = chunk_recurrence(*c_fwd, s0)
    oc_b, sc_b = chunk_recurrence(*tuple(_flip(t) for t in c_bwd), s0)
    ox_f, _ = chunk_recurrence(*x_fwd, sc_f)
    ox_b, _ = chunk_recurrence(*tuple(_flip(t) for t in x_bwd), sc_b)
    return ox_f + _flip(ox_b), oc_f + _flip(oc_b)

def hybrid_mixer(u_x, u_c, w_in_l, w_out_l, lb_l, hg_norm_w_l, cos, sin, ctx_out):
    B, N, _ = u_x.shape
    C = u_c.shape[1]
    split_pts = [int(p) for p in np.cumsum(PROJ_WIDTHS)[:-1]]
    px = jnp.split(u_x @ w_in_l, split_pts, axis=-1)
    pc = jnp.split(u_c @ w_in_l, split_pts, axis=-1)

    hidx = jnp.arange(RET_HEADS, dtype=jnp.float32)
    lg_f = jnp.log1p(-(2.0 ** (-5.0 - 2.0 * hidx)))
    lg_b = jnp.log1p(-(2.0 ** (-6.0 - 2.0 * hidx)))

    def ret_qkv(p, rope):
        q = to_heads(p[0], RET_HEADS)
        k = to_heads(p[1], RET_HEADS) * (RET_DK ** -0.5)
        if rope:
            q = apply_rope(q, cos, sin)
            k = apply_rope(k, cos, sin)
        return q, k, to_heads(p[2], RET_HEADS)

    def dec(lg, n):
        return jnp.broadcast_to(lg[None, :, None, None], (B, RET_HEADS, n, 1))

    rqx, rkx, rvx = ret_qkv(px, True)
    rqc, rkc, rvc = ret_qkv(pc, False)
    ret_x, ret_c = bidirectional_scan((rqc, rkc, rvc, dec(lg_f, C)), (rqc, rkc, rvc, dec(lg_b, C)),
                                      (rqx, rkx, rvx, dec(lg_f, N)), (rqx, rkx, rvx, dec(lg_b, N)))

    def hg_dir(p, z, lb):
        q = jax.nn.silu(to_heads(p[4], HG_HEADS))
        lbh = lb.reshape(1, HG_HEADS, 1, HG_DK)
        f = lbh + (1.0 - lbh) * jax.nn.sigmoid(to_heads(z, HG_HEADS).astype(jnp.float32))
        return q, 1.0 - f, to_heads(p[7], HG_HEADS), jnp.log(f)

    hg_x, hg_c = bidirectional_scan(hg_dir(pc, pc[5], lb_l[0]), hg_dir(pc, pc[6], lb_l[1]),
                                    hg_dir(px, px[5], lb_l[0]), hg_dir(px, px[6], lb_l[1]))

    def merge(o_ret, o_hg, p):
        a = from_heads(_rms(o_ret)) * jax.nn.silu(p[3])
        b = from_heads(rms_norm(o_hg, hg_norm_w_l)) * jax.nn.silu(p[8])
        return jnp.concatenate([a, b], axis=-1) @ w_out_l

    y_x = merge(ret_x, hg_x, px)
    if ctx_out:
        return y_x, merge(ret_c, hg_c, pc)
    return y_x, None

def moe_ffn(h, router_w, router_b, w1, b1, w2, b2):
    T, D = h.shape
    logits = (h @ router_w + router_b).astype(jnp.float32)
    top_logit, top_idx = lax.top_k(logits, TOP_K)
    gates = jax.nn.softmax(top_logit, axis=-1)
    A = T * TOP_K
    flat_e = top_idx.reshape(A)
    flat_tok = jnp.arange(A, dtype=jnp.int32) // TOP_K
    order = jnp.argsort(flat_e)
    se, stok, sg = flat_e[order], flat_tok[order], gates.reshape(A)[order]
    counts = jnp.bincount(flat_e, length=N_EXPERTS)
    padded = (counts + MOE_BLOCK - 1) // MOE_BLOCK * MOE_BLOCK
    start = jnp.cumsum(counts) - counts
    pend = jnp.cumsum(padded)
    pstart = pend - padded
    dest = pstart[se] + jnp.arange(A, dtype=jnp.int32) - start[se]
    n_blocks = -(-A // MOE_BLOCK) + N_EXPERTS
    R = n_blocks * MOE_BLOCK
    row_tok = jnp.full((R,), T, jnp.int32).at[dest].set(stok)
    row_gate = jnp.zeros((R,), jnp.float32).at[dest].set(sg)
    block_e = jnp.minimum(jnp.searchsorted(pend, jnp.arange(n_blocks, dtype=jnp.int32) * MOE_BLOCK,
                                           side='right'), N_EXPERTS - 1)
    h_pad = jnp.concatenate([h, jnp.zeros((1, D), h.dtype)], axis=0)
    xb = h_pad[row_tok].reshape(n_blocks, MOE_BLOCK, D)

    def run_block(args):
        xblk, e = args
        hu = xblk @ w1[e] + b1[e]
        x_glu = jnp.minimum(hu[:, :D_FF], SWIGLU_LIMIT)
        x_lin = jnp.clip(hu[:, D_FF:], -SWIGLU_LIMIT, SWIGLU_LIMIT)
        act = x_glu * jax.nn.sigmoid(SWIGLU_ALPHA * x_glu) * (x_lin + 1.0)
        return act @ w2[e] + b2[e]

    yb = lax.map(run_block, (xb, block_e))
    y = jnp.zeros((T + 1, D), jnp.float32).at[row_tok].add(yb.reshape(R, D) * row_gate[:, None])
    return y[:T]

def setup_inputs(seed: int = 0) -> dict:
    key = jax.random.key(seed)
    ks = jax.random.split(key, 20)
    f32 = jnp.float32
    sd = D_MODEL ** -0.5
    nrm = lambda k, s: jax.random.normal(k, s, f32)
    return {
        "x": nrm(ks[0], (BATCH, SEQ, D_MODEL)),
        "c": nrm(ks[1], (BATCH, D_MODEL)),
        "ctx": nrm(ks[2], (BATCH, CTX_LEN, D_MODEL)),
        "c_ctx": nrm(ks[3], (D_MODEL,)),
        "w_ada": nrm(ks[4], (DEPTH, D_MODEL, 6 * D_MODEL)) * sd,
        "b_ada": nrm(ks[5], (DEPTH, 6 * D_MODEL)) * 0.02,
        "norm_mix_w": 1.0 + 0.02 * nrm(ks[6], (DEPTH, D_MODEL)),
        "norm_ffn_w": 1.0 + 0.02 * nrm(ks[7], (DEPTH, D_MODEL)),
        "w_in": nrm(ks[8], (DEPTH, D_MODEL, PROJ_W)) * sd,
        "w_out": nrm(ks[9], (DEPTH, D_MODEL, D_MODEL)) * sd,
        "hg_lb": nrm(ks[10], (DEPTH + 1, 2, HG_K_W)) * 0.5,
        "hg_norm_w": 1.0 + 0.02 * nrm(ks[11], (DEPTH, HG_DV)),
        "router_w": nrm(ks[12], (DEPTH, D_MODEL, N_EXPERTS)) * sd,
        "router_b": nrm(ks[13], (DEPTH, N_EXPERTS)) * 0.01,
        "w1": nrm(ks[14], (DEPTH, N_EXPERTS, D_MODEL, 2 * D_FF)) * sd,
        "b1": nrm(ks[15], (DEPTH, N_EXPERTS, 2 * D_FF)) * 0.02,
        "w2": nrm(ks[16], (DEPTH, N_EXPERTS, D_FF, D_MODEL)) * (D_FF ** -0.5),
        "b2": nrm(ks[17], (DEPTH, N_EXPERTS, D_MODEL)) * 0.02,
        "norm_final_w": 1.0 + 0.02 * nrm(ks[18], (D_MODEL,)),
    }

def reference(x, c, ctx, c_ctx, w_ada, b_ada, norm_mix_w, norm_ffn_w, w_in, w_out, hg_lb,
              hg_norm_w, router_w, router_b, w1, b1, w2, b2, norm_final_w):
    B, N, D = x.shape
    C = ctx.shape[1]
    ROWS = N // GRID_W
    row = jnp.repeat(jnp.arange(ROWS, dtype=jnp.float32), GRID_W)
    col = jnp.tile(jnp.arange(GRID_W, dtype=jnp.float32), ROWS)
    cos, sin = axial_rope_tables(row, col)
    lb_all = jnp.cumsum(jax.nn.softmax(hg_lb.astype(jnp.float32), axis=0), axis=0)
    s_c = jax.nn.silu(c.astype(jnp.float32))
    s_cc = jax.nn.silu(c_ctx.astype(jnp.float32))
    h_lat, h_ctx = x, ctx
    for l in range(DEPTH):
        last = l == DEPTH - 1
        sh1, sc1, g1, sh2, sc2, g2 = jnp.split(s_c @ w_ada[l] + b_ada[l], 6, axis=-1)
        csh1, csc1, cg1, csh2, csc2, cg2 = jnp.split(s_cc @ w_ada[l] + b_ada[l], 6, axis=-1)
        u_x = rms_norm(h_lat, norm_mix_w[l]) * (1.0 + sc1[:, None]) + sh1[:, None]
        u_c = rms_norm(h_ctx, norm_mix_w[l]) * (1.0 + csc1) + csh1
        y_x, y_c = hybrid_mixer(u_x, u_c, w_in[l], w_out[l], lb_all[l], hg_norm_w[l], cos, sin,
                                not last)
        h_lat = h_lat + g1[:, None] * y_x
        v_x = (rms_norm(h_lat, norm_ffn_w[l]) * (1.0 + sc2[:, None]) + sh2[:, None]).reshape(B * N, D)
        if last:
            y = moe_ffn(v_x, router_w[l], router_b[l], w1[l], b1[l], w2[l], b2[l])
        else:
            h_ctx = h_ctx + cg1 * y_c
            v_c = (rms_norm(h_ctx, norm_ffn_w[l]) * (1.0 + csc2) + csh2).reshape(B * C, D)
            y_all = moe_ffn(jnp.concatenate([v_c, v_x], axis=0), router_w[l], router_b[l],
                            w1[l], b1[l], w2[l], b2[l])
            h_ctx = h_ctx + cg2 * y_all[:B * C].reshape(B, C, D)
            y = y_all[B * C:]
        h_lat = h_lat + g2[:, None] * y.reshape(B, N, D)
    return rms_norm(h_lat, norm_final_w)


_drawn_inputs = setup_inputs


def setup_inputs(seed=0):
    import zlib

    import numpy as np

    out = dict(_drawn_inputs(seed))
    spreads = {}
    factors = {'hg_lb': 2.714,
     'hg_norm_w': 2.982,
     'router_b': 2.855,
     'b1': 6.587,
     'b2': 8.0,
     'norm_final_w': 2.874}
    for name, (base, spread) in spreads.items():
        noise = np.random.default_rng([zlib.crc32(name.encode()), seed]).standard_normal(out[name].shape)
        drawn = base * np.exp(spread * noise) if base else spread * noise
        out[name] = jnp.asarray(drawn.astype(out[name].dtype))
    for name, factor in factors.items():
        out[name] = (out[name] * factor).astype(out[name].dtype)
    return out
```

```python
from contextlib import ExitStack

import numpy as np

import concourse.bass as bass
from concourse import mybir

F32 = mybir.dt.float32
F32R = mybir.dt.float32r
U32 = mybir.dt.uint32
I32 = mybir.dt.int32
ALU = mybir.AluOpType
ACT = mybir.ActivationFunctionType
AX = mybir.AxisListType

P = 128
D = 1024
KT = D // P
CTX, SEQ = 256, 1024
CT, LT = CTX // P, SEQ // P
NT = CT + LT
N = CTX + SEQ
HEADS = 4
RDK = 64
HALF = RDK // 2
ADA = 6 * D
NE = 32
TOPK = 4
EPS = 1e-6
CAP = 256
LIMIT = 7.0
PARTS = SEQ // CAP
UNITS = NE + TOPK * SEQ // CAP
SLOTS = 4
WSLOT = 2048
LEVELS = [64, 32, 16, 8, 4, 2, 1]
FINE = LEVELS[2:]
O_RQ, O_RK, O_RV, O_RG, O_HQ, O_ZF, O_ZB, O_HV, O_HG = 0, 256, 512, 1024, 1536, 2048, 2560, 3072, 3584


def constants():
    p = np.arange(P)
    f = np.float32
    out = {"ident": np.eye(P, dtype=f)}
    t = np.arange(SEQ)
    inv = 10000.0 ** (-np.arange(RDK // 4) / (RDK // 4))
    ang = np.concatenate([(t // 64)[:, None] * inv, (t % 64)[:, None] * inv], 1)
    out["cos"] = np.cos(ang).astype(f).reshape(LT, P, HALF).transpose(1, 0, 2).reshape(P, LT * HALF)
    out["sin"] = np.sin(ang).astype(f).reshape(LT, P, HALF).transpose(1, 0, 2).reshape(P, LT * HALF)
    h = np.arange(HEADS)
    gf = 1.0 - 2.0 ** (-5.0 - 2.0 * h)
    gb = 1.0 - 2.0 ** (-6.0 - 2.0 * h)
    s, q = p[:, None], p[None, :]
    dec = [RDK ** -0.5 * (np.where(q >= s, gf[i] ** np.maximum(q - s, 0), 0) + np.where(q <= s, gb[i] ** np.maximum(s - q, 0), 0)) for i in h]
    out["retdecay"] = np.stack(dec).astype(f)
    col = np.stack([np.stack([gf[i] ** (p + 1), gb[i] ** (P - p), RDK ** -0.5 * gf[i] ** (P - 1 - p), RDK ** -0.5 * gb[i] ** p,
                              np.where(p < RDK, gf[i] ** P, gb[i] ** P)], 1) for i in h])
    out["retcols"] = col.astype(f)
    masks = [(s == q) | (s // 32 != q // 32)]
    for hl in FINE:
        masks.append((s // (2 * hl) == q // (2 * hl)) & (s // hl != q // hl))
    out["masks"] = np.stack(masks, 1).astype(f).reshape(P, -1)
    out["scanmask"] = np.tile((np.arange(N) % P != 0).astype(f)[None], (P, 1))
    out["earlier"] = (s < q).astype(f)
    out["tokens"] = (np.arange(LT)[None] * P + p[:, None]).astype(f)
    out["experts"] = np.tile(np.arange(NE, dtype=f)[None], (P, 1))
    place = np.arange(NE * SEQ)
    out["empty_lists"] = np.stack([SEQ + place % CAP, 0 * place], 1).astype(f)
    out["spare_rows"] = np.zeros((CAP, D), f)
    e, part = np.arange(NE)[:, None], CAP * np.arange(PARTS)[None]
    out["unit_ids"] = np.concatenate([0 * e + np.arange(UNITS)[None], e, 0 * e + part, e * SEQ + part], 1).astype(f)
    return out


def alone(engine, passed):
    engine.sem_inc(passed, 1)


class Steps:

    def __init__(self, engine, sem, base=0):
        self.engine, self.sem, self.base, self.n = engine, sem, base, 0

    def did(self, ins):
        self.n += 1
        ins.then_inc(self.sem, 1)
        return self.n

    def wait(self, n=None):
        self.engine.wait_ge(self.sem, self.base + (self.n if n is None else n))

    def link(self, ins):
        self.did(ins)
        self.wait()


class Machine:

    def __init__(self, nc, ctx):
        self.nc, self.ctx, self.sems = nc, ctx, []

    def sb(self, name, shape, dt=F32):
        return self.ctx.enter_context(self.nc.sbuf_tensor(name, shape, dt))

    def sb_twice(self, name, shape):
        at = -(-self.nc.sbuf_base // 32) * 32
        x = self.sb(name, shape)
        return x, self.nc.alloc_sbuf_tensor_at(name + "_r", shape, F32R, offset=at)

    def ps(self, name, shape=(P, 512), dt=F32):
        return self.ctx.enter_context(self.nc.psum_tensor(name, list(shape), dt))

    def sem(self, name):
        self.sems.append(self.ctx.enter_context(self.nc.semaphore(name)))
        return self.sems[-1]

    def clear(self):
        with self.nc.Block() as block:
            @block.gpsimd
            def _(g):
                for x in self.sems:
                    g.sem_clear(x)


def modulate(nc, m, dram, keep):
    with ExitStack() as ctx:
        t = Machine(nc, ctx)
        xt = t.sb("xt", [P, NT, D])
        acc = t.sb("acc", [P, 4 * D])
        rows = t.sb("rows", [48, P])
        cols = t.sb("cols", [P, 48])
        sc = t.sb("sc", [P, 2, KT])
        scs = t.sb("scs", [P, 2, KT])
        square = t.sb("square", [P, D])
        ms = t.sb("ms", [P, NT])
        rstd = t.sb("rstd", [P, NT])
        acol = t.sb("acol", [P, KT, 2])
        bcol = t.sb("bcol", [P, KT, 2])
        lbd = t.sb("lbd", [P, 8])
        ones = t.sb("ones", [P, 1])
        arow = t.sb("arow", [1, 4 * D])
        tp = [t.ps(f"tp{i}") for i in range(4)]
        pa = t.ps("pa")
        pr = [t.ps(f"pr{i}") for i in range(2)]
        x_in = [t.sem(f"x_in{i}") for i in range(NT)]
        c_in = t.sem("c_in")
        acc_in = t.sem("acc_in")
        zeroed = t.sem("zeroed")
        squared = t.sem("squared")
        ms_ready = t.sem("ms_ready")
        root_ready = t.sem("root_ready")
        normed = t.sem("normed")
        turned = t.sem("turned")
        evacuated = t.sem("evacuated")
        cols_turned = t.sem("cols_turned")
        cols_ready = t.sem("cols_ready")
        silu_part = t.sem("silu_part")
        s_ready = t.sem("s_ready")
        ada_cols = t.sem("ada_cols")
        dve = t.sem("mod_dve")
        acc_done = t.sem("acc_done")
        row_summed = t.sem("row_summed")
        row_ready = t.sem("row_ready")
        row_out = t.sem("row_out")
        lb_part = t.sem("lb_part")
        slots, landed, released = keep["slots"], keep["landed"], keep["released"]
        uT, lb, oml = keep["uT"], keep["lb"], keep["oml"]
        ident = keep["ident"]
        ctx.callback(t.clear)
        block = ctx.enter_context(nc.Block())

        @block.sync
        def _(sp):
            sp.dma_start(dram["lists"], dram["empty_lists"]).then_inc(keep["emptied"], 16)
            sp.dma_start(dram["sum"][SEQ:, :], dram["spare_rows"]).then_inc(keep["emptied"], 16)
            sp.dma_start(ident[:], dram["ident"]).then_inc(keep["const_in"], 16)
            sp.dma_start(rows[0:16, :], dram["b_ada"][0, 0:2 * D].rearrange("(r p) -> r p", p=P)).then_inc(c_in, 16)
            sp.dma_start(rows[16:24, :], dram["norm_mix_w"][0].rearrange("(r p) -> r p", p=P)).then_inc(c_in, 16)
            sp.dma_start(rows[24:40, :], dram["hg_lb"].rearrange("a b (r p) -> (a b r) p", p=P)).then_inc(c_in, 16)
            sp.dma_start(sc[:, 0, :], dram["c"][0].rearrange("(p k) -> p k", k=KT)).then_inc(c_in, 16)
            sp.dma_start(sc[:, 1, :], dram["c_ctx"].rearrange("(p k) -> p k", k=KT)).then_inc(c_in, 16)
            sp.wait_ge(zeroed, 1)
            sp.dma_start(acc[0:1, :], dram["b_ada"][0:1, 2 * D:]).then_inc(acc_in, 16)
            for i in range(NT):
                src = dram["ctx"][0] if i < CT else dram["x"][0]
                r = i if i < CT else i - CT
                sp.dma_start(xt[:, i, :], src[r * P:(r + 1) * P, :]).then_inc(x_in[i], 16)
            wa = dram["w_ada"][0].rearrange("(p k) n -> p k n", k=KT)
            for n in range(3 * KT):
                g, k = n // KT, n % KT
                if n >= SLOTS:
                    sp.wait_ge(released[n % SLOTS], n // SLOTS)
                sp.dma_start(slots[n % SLOTS][:], wa[:, k, g * WSLOT:(g + 1) * WSLOT]).then_inc(landed[n % SLOTS], 16)
            sp.wait_ge(row_ready, 8)
            sp.dma_start(dram["ada_rows"], arow[:]).then_inc(row_out, 16)
            sp.wait_ge(row_out, 16)

        @block.scalar
        def _(act):
            act.wait_ge(c_in, 80)
            act.activation(scs[:], sc[:], ACT.Sigmoid).then_inc(silu_part, 1)
            act.wait_ge(cols_ready, 1)
            act.wait_ge(lb_part, 1)
            act.activation(lb[:], lbd[:], ACT.Sigmoid).then_inc(keep["lb_ready"], 1)
            for i in range(NT):
                act.wait_ge(x_in[i], 16)
                if i:
                    act.wait_ge(squared, i)
                act.activation(square[:], xt[:, i, :], ACT.Square, accum_out=ms[:, i:i + 1]).then_inc(squared, 1)
            act.wait_ge(ms_ready, 1)
            act.activation(rstd[:], ms[:], ACT.Sqrt).then_inc(root_ready, 1)
            for i in range(NT):
                for b in range(2):
                    n = 2 * i + b
                    act.wait_ge(turned, n + 1)
                    act.activation(uT[:, 4 * b:4 * b + 4, i * P:(i + 1) * P], tp[n % 4][:].rearrange("p (k t) -> p k t", k=4), ACT.Copy).then_inc(evacuated, 1)

        @block.vector
        def _(v):
            c = Steps(v, dve)
            v.memset(acc[:], 0.0).then_inc(zeroed, 1)
            v.memset(ones[:], 1.0).then_inc(zeroed, 1)
            v.wait_ge(silu_part, 1)
            v.tensor_tensor(sc[:], sc[:], scs[:], ALU.mult).then_inc(s_ready, 1)
            v.wait_ge(cols_turned, 1)
            v.tensor_copy(cols[:, 0:40], pa[:, 64:104]).then_inc(cols_ready, 1)
            v.wait_ge(cols_ready, 1)
            v.tensor_tensor(lbd[:], cols[:, 24:32], cols[:, 32:40], ALU.subtract).then_inc(lb_part, 1)
            v.wait_ge(keep["lb_ready"], 1)
            v.tensor_scalar(oml[:], lb[:], -1.0, 1.0, ALU.mult, ALU.add).then_inc(keep["lb_ready"], 1)
            v.wait_ge(squared, NT)
            v.tensor_scalar(ms[:], ms[:], 1.0 / D, EPS, ALU.mult, ALU.add).then_inc(ms_ready, 1)
            v.wait_ge(root_ready, 1)
            c.link(v.reciprocal(rstd[:], rstd[:]))
            for i in range(NT):
                v.tensor_scalar(xt[:, i, :], xt[:, i, :], rstd[:, i:i + 1], None, ALU.mult).then_inc(normed, 1)
            v.wait_ge(ada_cols, 1)
            pv = pa[:, 0:32].rearrange("p (j b) -> p j b", b=2)
            bias = cols[:, 0:16]
            c.link(v.tensor_tensor(bcol[:], pv[:, 0:8, :], bias[:, 0:8].unsqueeze(2).to_broadcast((P, 8, 2)), ALU.add))
            c.link(v.tensor_tensor(acol[:], pv[:, 8:16, :], bias[:, 8:16].unsqueeze(2).to_broadcast((P, 8, 2)), ALU.add))
            c.link(v.tensor_scalar(acol[:], acol[:], 1.0, None, ALU.add))
            c.link(v.tensor_tensor(acol[:], acol[:], cols[:, 16:24].unsqueeze(2).to_broadcast((P, 8, 2)), ALU.mult))
            v.wait_ge(evacuated, 2 * NT)
            for k in range(KT):
                for b, (a, z) in enumerate([(CTX, N), (0, CTX)]):
                    v.tensor_scalar(uT[:, k, a:z], uT[:, k, a:z], acol[:, k, b:b + 1], bcol[:, k, b:b + 1], ALU.mult, ALU.add).then_inc(keep["u_ready"], 1)
            v.wait_ge(acc_in, 16)
            for n in range(KT, 3 * KT):
                g, k = n // KT - 1, n % KT
                v.wait_ge(landed[n % SLOTS], 16 * (n // SLOTS + 1))
                if k:
                    v.wait_ge(released[(n - 1) % SLOTS], (n - 1) // SLOTS + 1)
                a = acc[:, g * WSLOT:(g + 1) * WSLOT]
                v.scalar_tensor_tensor(a, slots[n % SLOTS][:], sc[:, 0, k:k + 1], a, ALU.mult, ALU.add).then_inc(released[n % SLOTS], 1)
            for j in range(8):
                v.wait_ge(row_summed, j + 1)
                v.tensor_copy(arow[:, j * 512:(j + 1) * 512], pr[j % 2][0:1, :]).then_inc(row_ready, 1)

        @block.tensor
        def _(pe):
            pe.wait_ge(keep["const_in"], 16)
            pe.wait_ge(c_in, 80)
            pe.transpose(pa[:, 64:104], rows[0:40, :], ident[0:40, 0:40]).then_inc(cols_turned, 1)
            pe.wait_ge(s_ready, 1)
            pe.wait_ge(cols_ready, 1)
            for k in range(KT):
                pe.wait_ge(landed[k % SLOTS], 16 * (k // SLOTS + 1))
                for j in range(16):
                    mm = pe.matmul(pa[:, 2 * j:2 * j + 2], slots[k % SLOTS][:, j * P:(j + 1) * P], sc[:, :, k],
                                   start=(k == 0 and j == 0), stop=(k == KT - 1), skip_group_check=True)
                mm.then_inc(released[k % SLOTS], 1)
            pe.matmul(pa[:, 504:505], ident[:], ident[:, 0:1], start=True, stop=True, skip_group_check=True).then_inc(ada_cols, 1)
            for i in range(NT):
                pe.wait_ge(normed, i + 1)
                for b in range(2):
                    n = 2 * i + b
                    if n >= 4:
                        pe.wait_ge(evacuated, n - 3)
                    for k in range(4):
                        tt = pe.transpose(tp[n % 4][:, k * P:(k + 1) * P], xt[:, i, (4 * b + k) * P:(4 * b + k + 1) * P], ident[:])
                    tt.then_inc(turned, 1)
            pe.wait_ge(zeroed, 2)
            for j in range(8):
                n = 3 * KT - 1 if j >= 4 else 2 * KT - 1
                pe.wait_ge(released[n % SLOTS], n // SLOTS + 1)
                if j >= 2:
                    pe.wait_ge(row_ready, j - 1)
                pe.matmul(pr[j % 2][0:1, :], ones[:], acc[:, j * 512:(j + 1) * 512], start=True, stop=True).then_inc(row_summed, 1)


def project(pe, out, uT, tile, w, cols):
    for k in range(KT):
        mm = pe.matmul(out, uT[:, k, tile * P:(tile + 1) * P], w[:, k, cols], start=(k == 0), stop=(k == KT - 1))
    return mm


def retention(nc, m, dram, keep):
    with ExitStack() as ctx:
        t = Machine(nc, ctx)
        vqk = t.sb("r_vqk", [P, NT, 256])
        sig = t.sb("r_sig", [P, LT, P])
        gate = t.sb("r_gate", [P, LT, P])
        qk = t.sb("r_qk", [P, LT, P])
        rot = t.sb("r_rot", [P, 4, LT, 2, HALF])
        kd = t.sb("r_kd", [P, NT, P])
        qd = t.sb("r_qd", [P, LT, P])
        qT = t.sb("r_qT", [RDK, LT, P])
        kT = t.sb("r_kT", [RDK, LT, P])
        qdT = t.sb("r_qdT", [P, LT, P])
        state = t.sb("r_state", [P, LT + 1, P])
        st = t.sb("r_st", [P, LT, P])
        o = t.sb("r_o", [P, LT, P])
        sq = t.sb("r_sq", [P, P])
        ms = t.sb("r_ms", [P, LT])
        cos = t.sb("r_cos", [P, LT, HALF])
        sin = t.sb("r_sin", [P, LT, HALF])
        decay = t.sb("r_decay", [P, P])
        dcol = t.sb("r_dcol", [P, 5])
        pj = [t.ps(f"r_pj{i}") for i in range(2)]
        tb = [t.ps(f"r_tb{i}") for i in range(2)]
        pu = [t.ps(f"r_pu{i}") for i in range(3)]
        po1 = t.ps("r_po1")
        po = [pu[2], po1]
        trig_in = t.sem("r_trig_in")
        decay_in = t.sem("r_decay_in")
        s_passed = t.sem("r_s_passed")
        vqk_done, vqk_ready = t.sem("r_vqk_done"), t.sem("r_vqk_ready")
        g_done, g_sig, gate_ready = t.sem("r_g_done"), t.sem("r_g_sig"), t.sem("r_gate_ready")
        dve = t.sem("r_dve")
        rotated = t.sem("r_rotated")
        decayed = t.sem("r_decayed")
        u_done = t.sem("r_u_done")
        turned, qT_ready, kT_ready, qdT_ready = t.sem("r_turned"), t.sem("r_qT_ready"), t.sem("r_kT_ready"), t.sem("r_qdT_ready")
        s_done, st_ready = t.sem("r_s_done"), t.sem("r_st_ready")
        o_done, squared, ms_ready, root_ready, o_ready, o_out = (t.sem("r_" + x) for x in ("o_done", "squared", "ms_ready", "root_ready", "o_ready", "o_out"))
        slots, landed, released = keep["slots"], keep["landed"], keep["released"]
        uT, ident = keep["uT"], keep["ident"]
        w0 = slots[0][:].rearrange("p (k n) -> p k n", k=KT)
        w1 = slots[1][:].rearrange("p (k n) -> p k n", k=KT)
        base = 3 * KT // SLOTS
        win = dram["w_in"][0].rearrange("(k p) n -> p k n", p=P)
        L0, L1 = 16 * base, 16 * base
        STATES_AT = 10 + 4 + 2 * (LT - 1)
        DVE_STEPS = STATES_AT + 1
        ctx.callback(t.clear)
        block = ctx.enter_context(nc.Block())

        @block.sync
        def _(sp):
            sp.wait_ge(released[0], base)
            sp.wait_ge(released[1], base)
            sp.dma_start(cos[:].rearrange("p a b -> p (a b)"), dram["cos"]).then_inc(trig_in, 16)
            sp.dma_start(sin[:].rearrange("p a b -> p (a b)"), dram["sin"]).then_inc(trig_in, 16)
            with sp.Fori(0, HEADS) as h:
                at_v, at_q, at_k = sp.snap(h * P + O_RV), sp.snap(h * RDK + O_RQ), sp.snap(h * RDK + O_RK)
                at_g, at_o = sp.snap(h * P + O_RG), sp.snap(h * P)
                sp.wait_ge(vqk_done, h * 5)
                alone(sp, s_passed)
                sp.dma_start(w0[:, :, 0:128], win[:, :, bass.ds(at_v, P)]).then_inc(landed[0], 16)
                sp.dma_start(w0[:, :, 128:192], win[:, :, bass.ds(at_q, RDK)]).then_inc(landed[0], 16)
                sp.dma_start(w0[:, :, 192:256], win[:, :, bass.ds(at_k, RDK)]).then_inc(landed[0], 16)
                sp.wait_ge(g_done, h * 2)
                alone(sp, s_passed)
                sp.dma_start(w1[:, :, 0:128], win[:, :, bass.ds(at_g, P)]).then_inc(landed[1], 16)
                sp.wait_ge(st_ready, h * 2)
                alone(sp, s_passed)
                sp.dma_start(decay[:], dram["retdecay"][bass.ds(h, 1), :, :].rearrange("a s t -> (a s) t")).then_inc(decay_in, 16)
                sp.dma_start(dcol[:], dram["retcols"][bass.ds(h, 1), :, :].rearrange("a s t -> (a s) t")).then_inc(decay_in, 16)
                sp.wait_ge(o_ready, h * LT + LT)
                alone(sp, s_passed)
                sp.dma_start(dram["merged"].rearrange("(i p) n -> p i n", p=P)[:, :, bass.ds(at_o, P)], o[:]).then_inc(o_out, 16)
            sp.wait_ge(o_out, 16 * HEADS)

        @block.tensor
        def _(pe):
            pe.wait_ge(keep["u_ready"], 2 * KT)
            with pe.Fori(0, HEADS) as h:
                pe.wait_ge(landed[0], h * 48 + (L0 + 48))
                pe.wait_ge(gate_ready, h * 2)
                for g in range(NT // 2):
                    if g >= 2:
                        pe.wait_ge(vqk_ready, h * 5 + (g - 1))
                    for i in range(2):
                        mm = project(pe, pj[g % 2][:, i * 256:(i + 1) * 256], uT, 2 * g + i, w0, slice(0, 256))
                    mm.then_inc(vqk_done, 1)
                pe.wait_ge(landed[1], h * 16 + (L1 + 16))
                for g in range(2):
                    pe.wait_ge(vqk_ready, h * 5 + (4 + g))
                    for i in range(4):
                        mm = project(pe, pj[(g + 1) % 2][:, i * P:(i + 1) * P], uT, CT + 4 * g + i, w1, slice(0, 128))
                    mm.then_inc(g_done, 1)
                for n in range(4):
                    src = qk if n < 2 else qd
                    pe.wait_ge(rotated if n < 2 else decayed, h + 1)
                    if n == 2:
                        pe.wait_ge(qT_ready, h * 2 + 1)
                        pe.wait_ge(kT_ready, h * 2 + 1)
                    if n == 3:
                        pe.wait_ge(qT_ready, h * 2 + 2)
                        pe.wait_ge(kT_ready, h * 2 + 2)
                    for i in range(4):
                        tt = pe.transpose(tb[n % 2][:, i * P:(i + 1) * P], src[:, 4 * (n % 2) + i, :], ident[:])
                    tt.then_inc(turned, 1)
                pe.wait_ge(decayed, h + 1)
                pe.wait_ge(o_ready, h * LT)
                for g in range(3):
                    for i in range(4 if g < 2 else 2):
                        mm = pe.matmul(pu[g][:, i * P:(i + 1) * P], kd[:, 4 * g + i, :], vqk[:, 4 * g + i, 0:P], start=True, stop=True)
                    mm.then_inc(u_done, 1)
                pe.wait_ge(dve, h * DVE_STEPS + STATES_AT)
                for g in range(2):
                    pe.wait_ge(qT_ready, h * 2 + (g + 1))
                    pe.wait_ge(kT_ready, h * 2 + (g + 1))
                    for i in range(4):
                        mm = pe.matmul(pu[g][:, i * P:(i + 1) * P], kT[:, 4 * g + i, :], qT[:, 4 * g + i, :], start=True, stop=True)
                    mm.then_inc(s_done, 1)
                for g in range(2):
                    pe.wait_ge(qdT_ready, h * 2 + (g + 1))
                    pe.wait_ge(st_ready, h * 2 + (g + 1))
                    for i in range(4):
                        j = 4 * g + i
                        pe.matmul(po[g][:, i * P:(i + 1) * P], st[:, j, :], vqk[:, CT + j, 0:P], start=True, stop=False)
                        mm = pe.matmul(po[g][:, i * P:(i + 1) * P], qdT[:, j, :], state[:, j, :], start=False, stop=True)
                    mm.then_inc(o_done, 1)

        @block.scalar
        def _(act):
            with act.Fori(0, HEADS) as h:
                act.wait_ge(o_done, h * 2)
                for g in range(NT // 2):
                    act.wait_ge(vqk_done, h * 5 + (g + 1))
                    act.activation(vqk[:, 2 * g:2 * g + 2, :], pj[g % 2][:].rearrange("p (i n) -> p i n", i=2), ACT.Copy).then_inc(vqk_ready, 1)
                for g in range(2):
                    act.wait_ge(g_done, h * 2 + (g + 1))
                    act.activation(sig[:, 4 * g:4 * g + 4, :], pj[(g + 1) % 2][:].rearrange("p (i n) -> p i n", i=4), ACT.Sigmoid).then_inc(g_sig, 1)
                for g in range(2):
                    act.wait_ge(turned, h * 4 + (g + 1))
                    act.activation(qT[:, 4 * g:4 * g + 4, :], tb[g][0:RDK, :].rearrange("p (i n) -> p i n", i=4), ACT.Copy).then_inc(qT_ready, 1)
                for g in range(2):
                    act.wait_ge(turned, h * 4 + (g + 3))
                    act.activation(qdT[:, 4 * g:4 * g + 4, :], tb[g][:].rearrange("p (i n) -> p i n", i=4), ACT.Copy).then_inc(qdT_ready, 1)
                for g in range(2):
                    act.wait_ge(o_done, h * 2 + (g + 1))
                    for i in range(4):
                        j = 4 * g + i
                        if j:
                            act.wait_ge(squared, h * LT + j)
                        act.activation(sq[:], po[g][:, i * P:(i + 1) * P], ACT.Square, accum_out=ms[:, j:j + 1]).then_inc(squared, 1)
                act.wait_ge(ms_ready, h + 1)
                act.activation(ms[:], ms[:], ACT.Sqrt).then_inc(root_ready, 1)

        @block.vector
        def _(v):
            v.wait_ge(trig_in, 32)
            with v.Fori(0, HEADS) as h:
                c = Steps(v, dve, h * DVE_STEPS)
                v.wait_ge(vqk_ready, h * 5 + 5)
                a = vqk[:, CT:NT, P:].rearrange("p i (q f d) -> p i q f d", q=2, f=2)
                q4 = qk[:].rearrange("p i (q f d) -> p i q f d", q=2, f=2)
                cb = cos[:].unsqueeze(2).to_broadcast((P, LT, 2, HALF))
                sb = sin[:].unsqueeze(2).to_broadcast((P, LT, 2, HALF))
                c.did(v.tensor_tensor(rot[:, 0], a[:, :, :, 0, :], cb, ALU.mult))
                c.did(v.tensor_tensor(rot[:, 1], a[:, :, :, 1, :], sb, ALU.mult))
                c.did(v.tensor_tensor(rot[:, 2], a[:, :, :, 0, :], sb, ALU.mult))
                c.link(v.tensor_tensor(rot[:, 3], a[:, :, :, 1, :], cb, ALU.mult))
                c.did(v.tensor_tensor(q4[:, :, :, 0, :], rot[:, 0], rot[:, 1], ALU.subtract))
                v.tensor_tensor(q4[:, :, :, 1, :], rot[:, 2], rot[:, 3], ALU.add).then_inc(rotated, 1)
                v.wait_ge(rotated, h + 1)
                c.wait()
                v.wait_ge(decay_in, h * 32 + 32)
                for b in range(2):
                    c.did(v.tensor_scalar(kd[:, 0:CT, b * RDK:(b + 1) * RDK], vqk[:, 0:CT, 192:256], dcol[:, 2 + b:3 + b], None, ALU.mult))
                    c.did(v.tensor_scalar(kd[:, CT:, b * RDK:(b + 1) * RDK], qk[:, :, RDK:], dcol[:, 2 + b:3 + b], None, ALU.mult))
                    if b == 0:
                        c.did(v.tensor_scalar(qd[:, :, 0:RDK], qk[:, :, 0:RDK], dcol[:, 0:1], None, ALU.mult))
                v.tensor_scalar(qd[:, :, RDK:], qk[:, :, 0:RDK], dcol[:, 1:2], None, ALU.mult).then_inc(decayed, 1)
                for g in range(2):
                    v.wait_ge(g_sig, h * 2 + (g + 1))
                    v.tensor_tensor(gate[:, 4 * g:4 * g + 4, :], pj[(g + 1) % 2][:].rearrange("p (i n) -> p i n", i=4), sig[:, 4 * g:4 * g + 4, :], ALU.mult).then_inc(gate_ready, 1)
                for g in range(2):
                    v.wait_ge(turned, h * 4 + (g + 1))
                    v.tensor_copy(kT[:, 4 * g:4 * g + 4, :], tb[g][RDK:, :].rearrange("p (i n) -> p i n", i=4)).then_inc(kT_ready, 1)
                v.wait_ge(u_done, h * 3 + 3)
                U = lambda b, i: pu[i // 4][b * RDK:(b + 1) * RDK, (i % 4) * P:(i % 4 + 1) * P]
                S = lambda b, j: state[b * RDK:(b + 1) * RDK, j, :]
                g0, g1 = dcol[0:RDK, 4:5], dcol[RDK:, 4:5]
                c.did(v.tensor_copy(S(0, LT), U(0, 0)))
                c.link(v.tensor_copy(S(1, LT), U(1, 1)))
                c.did(v.scalar_tensor_tensor(S(0, 0), S(0, LT), g0, U(0, 1), ALU.mult, ALU.add))
                c.link(v.scalar_tensor_tensor(S(1, LT - 1), S(1, LT), g1, U(1, 0), ALU.mult, ALU.add))
                for j in range(LT - 1):
                    n = LT - 1 - j
                    c.did(v.scalar_tensor_tensor(S(0, j + 1), S(0, j), g0, U(0, CT + j), ALU.mult, ALU.add))
                    c.link(v.scalar_tensor_tensor(S(1, n - 1), S(1, n), g1, U(1, CT + n), ALU.mult, ALU.add))
                assert c.n == STATES_AT
                for g in range(2):
                    v.wait_ge(s_done, h * 2 + (g + 1))
                    v.tensor_tensor(st[:, 4 * g:4 * g + 4, :], pu[g][:].rearrange("p (i n) -> p i n", i=4), decay[:].unsqueeze(1).to_broadcast((P, 4, P)), ALU.mult).then_inc(st_ready, 1)
                v.wait_ge(squared, h * LT + LT)
                v.tensor_scalar(ms[:], ms[:], 1.0 / P, EPS, ALU.mult, ALU.add).then_inc(ms_ready, 1)
                v.wait_ge(root_ready, h + 1)
                c.link(v.reciprocal(ms[:], ms[:]))
                v.wait_ge(o_out, h * 16)
                for j in range(LT):
                    v.scalar_tensor_tensor(o[:, j, :], po[j // 4][:, (j % 4) * P:(j % 4 + 1) * P], ms[:, j:j + 1], gate[:, j, :], ALU.mult, ALU.mult).then_inc(o_ready, 1)
                assert c.n == DVE_STEPS


def hgrn2(nc, m, dram, keep):
    with ExitStack() as ctx:
        t = Machine(nc, ctx)
        HT = LT // 2
        HN = HT * P
        NL = len(LEVELS)
        NM = len(FINE) + 1
        key = [t.sb(f"h_key{d}", [P, N]) for d in range(2)]
        cum = [t.sb(f"h_cum{d}", [P, N]) for d in range(2)]
        cumb = t.sb("h_cumb", [P, N])
        scan = t.sb("h_scan", [P, N])
        sigq = t.sb("h_sigq", [P, SEQ])
        q = t.sb("h_q", [P, SEQ])
        qdec = [t.sb(f"h_qdec{d}", [P, SEQ]) for d in range(2)]
        kdec = [t.sb(f"h_kdec{d}", [P, N]) for d in range(2)]
        wk = t.sb("h_wk", [P, NL + 1, HN])
        wq = t.sb("h_wq", [P, NL, HN])
        val = t.sb("h_val", [P, NT, P])
        gate = t.sb("h_gate", [P, LT, P])
        sigg = t.sb("h_sigg", [P, LT, P])
        ktok = [t.sb(f"h_ktok{d}", [P, NT, P]) for d in range(2)]
        state = [t.sb(f"h_state{d}", [P, LT + 1, P]) for d in range(2)]
        total = t.sb("h_total", [P, 2, NT])
        st = [t.sb(f"h_st{i}", [P, P]) for i in range(2)]
        o = sigg
        sq = t.sb("h_sq", [P, P])
        ms = t.sb("h_ms", [P, LT])
        bound = t.sb("h_bound", [P, HEADS, 2, 3])
        bnd = t.sb("h_bnd", [P, 2, 3])
        masks = t.sb("h_masks", [P, NM, P])
        picked = t.sb("h_picked", [P, NM, P])
        nw = t.sb("h_nw", [P, P])
        pj = [t.ps(f"h_pj{i}") for i in range(2)]
        ps = [t.ps(f"h_ps{i}") for i in range(4)]
        po = t.ps("h_po")
        tb = [t.ps("h_tb"), po]
        names = """const_in dve bounds z_done z_sig logf q_done q_sig q_ready v_done v_ready g_done g_sig gate_ready
        cumulated keys_ready pool_sub exped dec_ready turned ktok_ready u_done lev_sub lev_exp lev_ready s_done
         st_ready o_done squared ms_ready root_ready o_ready o_out s_passed""".split()
        S = {x: t.sem("h_" + x) for x in names}
        slots, landed = keep["slots"], keep["landed"]
        uT, ident = keep["uT"], keep["ident"]
        W = [slots[i][:].rearrange("p (k n) -> p k n", k=KT) for i in range(3)]
        b0 = 3 * KT // SLOTS
        L = [16 * (b0 + 3 * HEADS), 16 * (b0 + HEADS), 16 * b0]
        win = dram["w_in"][0].rearrange("(k p) n -> p k n", p=P)
        RNG = [(0, CTX), (CTX, CTX + 512), (CTX + 512, N)]
        FREE_AT = 1 + 3 * NL + 2
        U_FREE = [FREE_AT + 2, FREE_AT + 6]
        STATES_AT = 1 + 3 * NL + 2 * (LT + 1)
        PICKED = [STATES_AT + 2 * (j + 1) for j in range(HT)]
        PICKED += [PICKED[-1] + 3 * NL + 2] + [PICKED[-1] + 3 * NL + 3 + 2 * (j + 1) for j in range(HT - 1)]
        STEPS = PICKED[-1] + 1
        ctx.callback(t.clear)
        block = ctx.enter_context(nc.Block())

        @block.sync
        def _(sp):
            sp.dma_start(masks[:].rearrange("p a b -> p (a b)"), dram["masks"]).then_inc(S["const_in"], 16)
            sp.dma_start(scan[:], dram["scanmask"]).then_inc(S["const_in"], 16)
            sp.dma_start(nw[:], dram["hg_norm_w"].to_broadcast((P, P))).then_inc(S["const_in"], 16)
            with sp.Fori(0, HEADS) as h:
                at = [sp.snap(h * P + x) for x in (O_ZF, O_ZB, O_HQ, O_HV, O_HG)]
                at_o = sp.snap(h * P + HEADS * P)
                sp.wait_ge(S["z_done"], h * 6)
                alone(sp, S["s_passed"])
                sp.dma_start(W[0][:, :, 0:P], win[:, :, bass.ds(at[0], P)]).then_inc(landed[0], 16)
                sp.dma_start(W[0][:, :, P:], win[:, :, bass.ds(at[1], P)]).then_inc(landed[0], 16)
                sp.wait_ge(S["v_done"], h * 3)
                alone(sp, S["s_passed"])
                sp.dma_start(W[1][:, :, 0:P], win[:, :, bass.ds(at[2], P)]).then_inc(landed[1], 16)
                sp.dma_start(W[1][:, :, P:], win[:, :, bass.ds(at[3], P)]).then_inc(landed[1], 16)
                sp.wait_ge(S["g_done"], h * 2)
                alone(sp, S["s_passed"])
                sp.dma_start(W[2][:, :, 0:P], win[:, :, bass.ds(at[4], P)]).then_inc(landed[2], 16)
                sp.wait_ge(S["o_ready"], h * LT + LT)
                alone(sp, S["s_passed"])
                sp.dma_start(dram["merged"].rearrange("(i p) n -> p i n", p=P)[:, :, bass.ds(at_o, P)], o[:]).then_inc(S["o_out"], 16)
            sp.wait_ge(S["o_out"], 16 * HEADS)

        @block.tensor
        def _(pe):
            with pe.Fori(0, HEADS) as h:
                pe.wait_ge(S["gate_ready"], h * 2)
                pe.wait_ge(landed[0], h * 32 + (L[0] + 32))
                for d in range(2):
                    for j, (a, z) in enumerate(RNG):
                        n = 3 * d + j
                        if n >= 2:
                            pe.wait_ge(S["z_sig"], h * 6 + (n - 1))
                        for k in range(KT):
                            mm = pe.matmul(pj[n % 2][:, 0:z - a], W[0][:, k, d * P:(d + 1) * P], uT[:, k, a:z], start=(k == 0), stop=(k == KT - 1))
                        mm.then_inc(S["z_done"], 1)
                pe.wait_ge(landed[1], h * 32 + (L[1] + 32))
                for j in range(2):
                    pe.wait_ge(S["z_sig"], h * 6 + (5 + j))
                    for k in range(KT):
                        mm = pe.matmul(pj[j][:], W[1][:, k, 0:P], uT[:, k, RNG[j + 1][0]:RNG[j + 1][1]], start=(k == 0), stop=(k == KT - 1))
                    mm.then_inc(S["q_done"], 1)
                for g in range(3):
                    if g < 2:
                        pe.wait_ge(S["q_ready"], h * 2 + (g + 1))
                    else:
                        pe.wait_ge(S["v_ready"], h * 3 + 1)
                    for i in range(min(4, NT - 4 * g)):
                        mm = project(pe, pj[g % 2][:, i * P:(i + 1) * P], uT, 4 * g + i, W[1], slice(P, 2 * P))
                    mm.then_inc(S["v_done"], 1)
                pe.wait_ge(landed[2], h * 16 + (L[2] + 16))
                for g in range(2):
                    pe.wait_ge(S["v_ready"], h * 3 + (g + 2))
                    for i in range(4):
                        mm = project(pe, pj[(g + 1) % 2][:, i * P:(i + 1) * P], uT, CT + 4 * g + i, W[2], slice(0, P))
                    mm.then_inc(S["g_done"], 1)
                for d in range(2):
                    pe.wait_ge(S["dec_ready"], h * 4 + (d + 1))
                    pe.wait_ge(S["o_ready"], h * LT)
                    for g in range(3):
                        n = 3 * d + g
                        if n >= 2:
                            pe.wait_ge(S["ktok_ready"], h * 6 + (n - 1))
                        for i in range(min(4, NT - 4 * g)):
                            c = 4 * g + i
                            tt = pe.transpose(tb[n % 2][:, i * P:(i + 1) * P], kdec[d][:, c * P:(c + 1) * P], ident[:])
                        tt.then_inc(S["turned"], 1)
                for d in range(2):
                    for g in range(3):
                        bank = (3 * d + g) % 4
                        if 3 * d + g < 4:
                            pe.wait_ge(S["st_ready"], h * LT)
                        else:
                            pe.wait_ge(S["dve"], h * STEPS + U_FREE[bank])
                        pe.wait_ge(S["ktok_ready"], h * 6 + (3 * d + g + 1))
                        for i in range(min(4, NT - 4 * g)):
                            c = 4 * g + i
                            mm = pe.matmul(ps[bank][:, i * P:(i + 1) * P], ktok[d][:, c, :], val[:, c, :], start=True, stop=True)
                        mm.then_inc(S["u_done"], 1)
                pe.wait_ge(S["dve"], h * STEPS + STATES_AT)

                def scores(half, i):
                    j = HT * half + i
                    bank = ps[2 * (j % 2)], ps[2 * (j % 2) + 1]
                    if j >= 2:
                        pe.wait_ge(S["dve"], h * STEPS + PICKED[j - 2])
                    if i == 0:
                        pe.wait_ge(S["lev_ready"], h * 2 + (half + 1))
                    c = slice(i * P, (i + 1) * P)
                    pe.matmul(bank[0][:, 0:P], wk[:, NL, c], q[:, j * P:(j + 1) * P], start=True, stop=True)
                    for l, hl in enumerate(LEVELS[:2]):
                        for a in range(0, P, 2 * hl):
                            for key_at, query_at in ((a, a + hl), (a + hl, a)):
                                pe.matmul(bank[0][key_at:key_at + hl, query_at:query_at + hl], wk[:, l, i * P + key_at:i * P + key_at + hl],
                                          wq[:, l, i * P + query_at:i * P + query_at + hl], start=True, stop=True)
                    for r in range(1, NM):
                        mm = pe.matmul(bank[r // 4][:, (r % 4) * P:(r % 4 + 1) * P], wk[:, r + 1, c], wq[:, r + 1, c], start=True, stop=True)
                    mm.then_inc(S["s_done"], 1)

                def output(j):
                    pe.wait_ge(S["st_ready"], h * LT + (j + 1))
                    if j == HT:
                        pe.wait_ge(S["o_ready"], h * LT + HT)
                    out = po[:, (j % HT) * P:(j % HT + 1) * P]
                    pe.matmul(out, st[j % 2][:], val[:, CT + j, :], start=True, stop=False)
                    for d in range(2):
                        mm = pe.matmul(out, qdec[d][:, j * P:(j + 1) * P], state[d][:, j, :], start=False, stop=(d == 1))
                    mm.then_inc(S["o_done"], 1)

                pe.wait_ge(S["dec_ready"], h * 4 + 4)
                for j in range(LT):
                    scores(j // HT, j % HT)
                    if j:
                        output(j - 1)
                output(LT - 1)

        @block.scalar
        def _(act):
            with act.Fori(0, HEADS) as h:
                act.wait_ge(S["bounds"], h + 1)
                act.wait_ge(S["lev_ready"], h * 2)
                for d in range(2):
                    for j, (a, z) in enumerate(RNG):
                        n = 3 * d + j
                        act.wait_ge(S["z_done"], h * 6 + (n + 1))
                        act.activation(key[d][:, a:z], pj[n % 2][:, 0:z - a], ACT.Sigmoid).then_inc(S["z_sig"], 1)
                for j in range(2):
                    act.wait_ge(S["q_done"], h * 2 + (j + 1))
                    act.activation(sigq[:, j * 512:(j + 1) * 512], pj[j][:], ACT.Sigmoid).then_inc(S["q_sig"], 1)
                for d in range(2):
                    act.wait_ge(S["z_sig"], h * 6 + (3 * d + 3))
                    act.activation(cum[d][:], key[d][:], ACT.Ln, scale=bnd[:, d, 1:2], bias=bnd[:, d, 0:1]).then_inc(S["logf"], 1)
                act.wait_ge(S["o_done"], h * LT)
                for g in range(3):
                    act.wait_ge(S["v_done"], h * 3 + (g + 1))
                    n = min(4, NT - 4 * g)
                    act.activation(val[:, 4 * g:4 * g + n, :], pj[g % 2][:, 0:n * P].rearrange("p (i n) -> p i n", i=n), ACT.Copy).then_inc(S["v_ready"], 1)
                act.wait_ge(S["o_out"], h * 16)
                for g in range(2):
                    act.wait_ge(S["g_done"], h * 2 + (g + 1))
                    act.activation(sigg[:, 4 * g:4 * g + 4, :], pj[(g + 1) % 2][:].rearrange("p (i n) -> p i n", i=4), ACT.Sigmoid).then_inc(S["g_sig"], 1)
                act.wait_ge(S["pool_sub"], h * 3 + 1)
                act.activation(kdec[0][:], kdec[0][:], ACT.Exp).then_inc(S["exped"], 1)
                act.wait_ge(S["pool_sub"], h * 3 + 2)
                act.activation(kdec[1][:], cum[1][:], ACT.Exp).then_inc(S["exped"], 1)
                act.activation(qdec[0][:], cum[0][:, CTX:], ACT.Exp).then_inc(S["exped"], 1)
                act.wait_ge(S["pool_sub"], h * 3 + 3)
                act.activation(qdec[1][:], qdec[1][:], ACT.Exp).then_inc(S["exped"], 1)
                act.activation(total[:, 0, :], cum[0][:].rearrange("p (i n) -> p i n", n=P)[:, :, P - 1], ACT.Exp).then_inc(S["exped"], 1)
                act.activation(total[:, 1, :], cumb[:].rearrange("p (i n) -> p i n", n=P)[:, :, P - 1], ACT.Exp).then_inc(S["exped"], 1)
                def levels(half):
                    for l in range(NL):
                        act.wait_ge(S["lev_sub"], h * (8 * NL) + (half * 4 * NL + 4 * l + 4))
                        for x in (wk, wq):
                            act.activation(x[:, l, :], x[:, l, :], ACT.Exp).then_inc(S["lev_exp"], 1)

                def turned_keys():
                    for n in range(6):
                        d, g = n // 3, n % 3
                        m_ = min(4, NT - 4 * g)
                        act.wait_ge(S["turned"], h * 6 + (n + 1))
                        act.activation(ktok[d][:, 4 * g:4 * g + m_, :], tb[n % 2][:, 0:m_ * P].rearrange("p (i n) -> p i n", i=m_), ACT.Copy).then_inc(S["ktok_ready"], 1)

                def square(half):
                    act.wait_ge(S["o_done"], h * LT + (half + 1) * HT)
                    for j in range(half * HT, half * HT + HT):
                        if j:
                            act.wait_ge(S["squared"], h * LT + j)
                        act.activation(sq[:], po[:, (j % HT) * P:(j % HT + 1) * P], ACT.Square, accum_out=ms[:, j:j + 1]).then_inc(S["squared"], 1)
                    act.wait_ge(S["ms_ready"], h * 2 + (half + 1))
                    act.activation(ms[:, half * HT:(half + 1) * HT], ms[:, half * HT:(half + 1) * HT], ACT.Sqrt).then_inc(S["root_ready"], 1)

                levels(0)
                turned_keys()
                levels(1)
                square(0)
                square(1)

        @block.gpsimd
        def _(g):
            with g.Fori(0, HEADS) as h:
                c3 = lambda x, a=0, z=N: x[:, a:z].rearrange("p (i n) -> p i n", n=P)
                g.wait_ge(S["cumulated"], h * 2 + 1)
                g.wait_ge(S["u_done"], h * 6)
                g.tensor_tensor(c3(kdec[0]), c3(cum[0])[:, :, P - 1:P].to_broadcast((P, NT, P)), c3(cum[0]), ALU.subtract).then_inc(S["pool_sub"], 1)
                g.wait_ge(S["cumulated"], h * 2 + 2)
                g.tensor_tensor(cum[1][:], cumb[:], cum[1][:], ALU.subtract).then_inc(S["pool_sub"], 1)
                g.wait_ge(S["pool_sub"], h * 3 + 2)
                g.tensor_tensor(c3(qdec[1], 0, SEQ), c3(cumb, CTX)[:, :, P - 1:P].to_broadcast((P, LT, P)), c3(cum[1], CTX), ALU.subtract).then_inc(S["pool_sub"], 1)
                for half in range(2):
                    g.wait_ge(S["s_done"], h * LT + half * HT)
                    for l, hl in enumerate(LEVELS):
                        nb = HN // (2 * hl)
                        view = lambda x: x.rearrange("p (b f n) -> p b f n", f=2, n=hl)
                        fwd, bwd = (view(cum[d][:, CTX + half * HN:CTX + (half + 1) * HN]) for d in range(2))
                        k4, q4 = view(wk[:, l, :]), view(wq[:, l, :])
                        mf = fwd[:, :, 0, hl - 1:hl].to_broadcast((P, nb, hl))
                        mb = bwd[:, :, 1, 0:1].to_broadcast((P, nb, hl))
                        for out, x, y in ((k4[:, :, 0], mf, fwd[:, :, 0]), (k4[:, :, 1], bwd[:, :, 1], mb),
                                          (q4[:, :, 0], mb, bwd[:, :, 0]), (q4[:, :, 1], fwd[:, :, 1], mf)):
                            g.tensor_tensor(out, x, y, ALU.subtract).then_inc(S["lev_sub"], 1)

        @block.vector
        def _(v):
            v.wait_ge(keep["lb_ready"], 2)
            c = Steps(v, S["bounds"])
            for n, (src, sign) in enumerate([(keep["lb"], 1.0), (keep["oml"], 1.0), (keep["oml"], -1.0)]):
                v.tensor_scalar(bound[:, :, :, n], src[:].rearrange("p (d h) -> p h d", d=2), sign, None, ALU.mult).then_inc(keep["bound_part"], 1)
            v.wait_ge(keep["bound_part"], 3)
            v.wait_ge(S["const_in"], 48)
            with v.Fori(0, HEADS) as h:
                c = Steps(v, S["dve"], h * STEPS)
                v.wait_ge(S["logf"], h * 2)
                v.tensor_copy(bnd[:], bound[:, bass.ds(h, 1), :, :].rearrange("p a d n -> p (a d) n")).then_inc(S["bounds"], 1)
                v.wait_ge(S["bounds"], h + 1)
                for j in range(2):
                    v.wait_ge(S["q_sig"], h * 2 + (j + 1))
                    v.tensor_tensor(q[:, j * 512:(j + 1) * 512], pj[j][:], sigq[:, j * 512:(j + 1) * 512], ALU.mult).then_inc(S["q_ready"], 1)
                v.wait_ge(S["logf"], h * 2 + 1)
                v.tensor_tensor_scan(cum[0][:], scan[:], cum[0][:], 0.0, ALU.mult, ALU.add).then_inc(S["cumulated"], 1)
                v.wait_ge(S["logf"], h * 2 + 2)
                v.tensor_tensor_scan(cumb[:], scan[:], cum[1][:], 0.0, ALU.mult, ALU.add).then_inc(S["cumulated"], 1)
                for d in range(2):
                    v.tensor_scalar(key[d][:], key[d][:], bnd[:, d, 2:3], bnd[:, d, 1:2], ALU.mult, ALU.add).then_inc(S["keys_ready"], 1)
                for g in range(2):
                    v.wait_ge(S["g_sig"], h * 2 + (g + 1))
                    v.tensor_tensor(gate[:, 4 * g:4 * g + 4, :], pj[(g + 1) % 2][:].rearrange("p (i n) -> p i n", i=4), sigg[:, 4 * g:4 * g + 4, :], ALU.mult).then_inc(S["gate_ready"], 1)
                v.wait_ge(S["gate_ready"], h * 2 + 2)
                c.link(v.tensor_tensor(gate[:], gate[:], nw[:].unsqueeze(1).to_broadcast((P, LT, P)), ALU.mult))
                v.wait_ge(S["keys_ready"], h * 2 + 2)
                v.wait_ge(S["q_ready"], h * 2 + 2)
                for n, (buf, by) in enumerate([(kdec[0], key[0]), (kdec[1], key[1]), (qdec[0], q), (qdec[1], q)]):
                    v.wait_ge(S["exped"], h * 6 + (n + 1))
                    v.tensor_tensor(buf[:], buf[:], by[:], ALU.mult).then_inc(S["dec_ready"], 1)

                def levels(half):
                    lo = half * HN
                    v.wait_ge(S["s_done"], h * LT + half * HT)
                    k0, k1 = (key[d][:, CTX + lo:CTX + lo + HN] for d in range(2))
                    c.did(v.tensor_tensor(wk[:, NL, :], k0, k1, ALU.add))
                    for l, hl in enumerate(LEVELS):
                        view = lambda x: x.rearrange("p (b f n) -> p b f n", f=2, n=hl)
                        k4 = view(wk[:, l, :])
                        v.wait_ge(S["lev_exp"], h * (4 * NL) + (half * 2 * NL + 2 * l + 1))
                        c.did(v.tensor_tensor(k4[:, :, 0], k4[:, :, 0], view(k0)[:, :, 0], ALU.mult))
                        c.did(v.tensor_tensor(k4[:, :, 1], k4[:, :, 1], view(k1)[:, :, 1], ALU.mult))
                        v.wait_ge(S["lev_exp"], h * (4 * NL) + (half * 2 * NL + 2 * l + 2))
                        x = v.tensor_tensor(wq[:, l, :], wq[:, l, :], q[:, lo:lo + HN], ALU.mult)
                        if l < NL - 1:
                            c.did(x)
                        else:
                            x.then_inc(S["lev_ready"], 1)

                def states():
                    v.wait_ge(S["exped"], h * 6 + 6)
                    v.wait_ge(S["o_done"], h * LT)
                    U = lambda i: ps[i // 4][:, (i % 4) * P:(i % 4 + 1) * P]
                    v.wait_ge(S["u_done"], h * 6 + 3)
                    c.link(v.tensor_copy(state[0][:, LT, :], U(0)))
                    c.link(v.scalar_tensor_tensor(state[0][:, 0, :], state[0][:, LT, :], total[:, 0, 1:2], U(1), ALU.mult, ALU.add))
                    for j in range(LT - 1):
                        c.link(v.scalar_tensor_tensor(state[0][:, j + 1, :], state[0][:, j, :], total[:, 0, CT + j:CT + j + 1], U(CT + j), ALU.mult, ALU.add))
                    v.wait_ge(S["u_done"], h * 6 + 6)
                    U = lambda i: ps[(3 + i // 4) % 4][:, (i % 4) * P:(i % 4 + 1) * P]
                    c.link(v.tensor_copy(state[1][:, LT, :], U(1)))
                    c.link(v.scalar_tensor_tensor(state[1][:, LT - 1, :], state[1][:, LT, :], total[:, 1, 0:1], U(0), ALU.mult, ALU.add))
                    for j in range(LT - 1, 0, -1):
                        c.link(v.scalar_tensor_tensor(state[1][:, j - 1, :], state[1][:, j, :], total[:, 1, CT + j:CT + j + 1], U(CT + j), ALU.mult, ALU.add))

                def pick(j):
                    v.wait_ge(S["s_done"], h * LT + (j + 1))
                    c.did(v.tensor_tensor(picked[:, 0:4, :], ps[2 * (j % 2)][:].rearrange("p (r n) -> p r n", r=4), masks[:, 0:4, :], ALU.mult))
                    c.link(v.tensor_tensor(picked[:, 4:NM, :], ps[2 * (j % 2) + 1][:, 0:(NM - 4) * P].rearrange("p (r n) -> p r n", n=P), masks[:, 4:NM, :], ALU.mult))
                    if j >= 2:
                        v.wait_ge(S["o_done"], h * LT + (j - 1))
                    v.tensor_reduce(st[j % 2][:], picked[:].rearrange("p r n -> p n r"), AX.X, ALU.add).then_inc(S["st_ready"], 1)
                    v.wait_ge(S["st_ready"], h * LT + (j + 1))
                    assert c.n == PICKED[j], (c.n, j)

                def finish(half):
                    sl = slice(half * HT, half * HT + HT)
                    v.wait_ge(S["squared"], h * LT + (half + 1) * HT)
                    v.tensor_scalar(ms[:, sl], ms[:, sl], 1.0 / P, EPS, ALU.mult, ALU.add).then_inc(S["ms_ready"], 1)
                    v.wait_ge(S["root_ready"], h * 2 + (half + 1))
                    c.link(v.reciprocal(ms[:, sl], ms[:, sl]))
                    for j in range(half * HT, half * HT + HT):
                        v.scalar_tensor_tensor(o[:, j, :], po[:, (j % HT) * P:(j % HT + 1) * P], ms[:, j:j + 1], gate[:, j, :], ALU.mult, ALU.mult).then_inc(S["o_ready"], 1)

                levels(0)
                states()
                assert c.n == STATES_AT, c.n
                for j in range(HT):
                    pick(j)
                levels(1)
                pick(HT)
                finish(0)
                for j in range(HT + 1, LT):
                    pick(j)
                finish(1)
                assert c.n == STEPS, c.n


def route(nc, m, dram, keep):
    with ExitStack() as ctx:
        t = Machine(nc, ctx)
        g1, g2 = t.sb("o_g1", [P, D]), t.sb("o_g2", [P, D])
        scale, shift = t.sb("o_scale", [P, D]), t.sb("o_shift", [P, D])
        fw = t.sb("o_fw", [P, D])
        rw = t.sb("o_rw", [P, KT, NE])
        rb = t.sb("o_rb", [P, NE])
        b2 = t.sb("o_b2", [NE, D])
        earlier = t.sb("o_earlier", [P, P])
        tokens = t.sb("o_tokens", [P, LT])
        experts = t.sb("o_experts", [P, NE])
        base = t.sb("o_base", [P, NE])
        ones = t.sb("o_ones", [P, P])
        mt = t.sb("o_mt", [P, D])
        x = t.sb("o_x", [P, D])
        mT = t.sb("o_mT", [P, KT, P])
        h_ = t.sb("o_h", [P, D])
        sq = t.sb("o_sq", [P, D])
        ms = t.sb("o_ms", [P, 1])
        vv = t.sb("o_v", [P, D])
        vT = t.sb("o_vT", [P, KT, P])
        out = t.sb("o_out", [P, D])
        n_parts = t.sb("o_n_parts", [NE, 1])
        lg = t.sb("o_lg", [P, NE])
        top = t.sb("o_top", [P, 8])
        topi = t.sb("o_topi", [P, 8], U32)
        topf = t.sb("o_topf", [P, TOPK])
        nmax = t.sb("o_nmax", [P, 1])
        ex = t.sb("o_ex", [P, TOPK])
        den = t.sb("o_den", [P, 1])
        pairs = t.sb("o_pairs", [P, TOPK, 2])
        hot = t.sb("o_hot", [P, TOPK, NE])
        pick = t.sb("o_pick", [P, TOPK, NE])
        sel = t.sb("o_sel", [P, NE])
        seen = t.sb("o_seen", [P, NE])
        dense = t.sb("o_dense", [P, NE])
        denseT = t.sb("o_denseT", [NE, P])
        place = t.sb("o_place", [P, NE])
        dest = t.sb("o_dest", [P, TOPK])
        desti = t.sb("o_desti", [P, TOPK], U32)
        cnt = t.sb("o_cnt", [NE, 2])
        more = t.sb("o_more", [NE, 3, PARTS])
        units = t.sb("o_units", [NE, 4, UNITS])
        mine = t.sb("o_mine", [NE, PARTS, UNITS])
        iota = t.sb("o_iota", [NE, UNITS + 1 + 2 * PARTS])
        tb = [t.ps(f"o_tb{i}") for i in range(2)]
        py = [t.ps(f"o_py{i}") for i in range(2)]
        pl, pp, pd = t.ps("o_pl"), t.ps("o_pp"), t.ps("o_pd")
        names = """const_in dve merged_in x_in turned mT_ready y_done h_ready squared ms_ready root_ready v_ready v_out
        vT_ready logits_done lg_ready top_ready exped sel_ready placed_done dense_ready denseT_done denseT_ready bias_done out_ready
        sum_out dest_ready scattered seen_ready counted unit_step units_done v_passed g_passed s_passed""".split()
        S = {n: t.sem("o_" + n) for n in names}
        slots, landed, ident = keep["slots"], keep["landed"], keep["ident"]
        W = [slots[i][:].rearrange("p (k n) -> p k n", k=KT) for i in range(4)]
        ctx.callback(t.clear)
        block = ctx.enter_context(nc.Block())
        NCONST = 12
        STEPS = 21

        @block.sync
        def _(sp):
            wo = dram["w_out"][0].rearrange("(k p) n -> p k n", p=P)
            for j in range(4):
                sp.dma_start(W[j], wo[:, :, j * 256:(j + 1) * 256]).then_inc(S["const_in"], 16)
            for n, dst in enumerate((g1, shift, scale, g2)):
                sp.dma_start(dst[:], dram["ada_rows"][:, n * D:(n + 1) * D].to_broadcast((P, D))).then_inc(S["const_in"], 16)
            sp.dma_start(fw[:], dram["norm_ffn_w"].to_broadcast((P, D))).then_inc(S["const_in"], 16)
            sp.dma_start(rw[:], dram["router_w"][0].rearrange("(k p) e -> p k e", p=P)).then_inc(S["const_in"], 16)
            sp.dma_start(rb[:], dram["router_b"].to_broadcast((P, NE))).then_inc(S["const_in"], 16)
            sp.dma_start(b2[:], dram["b2"][0]).then_inc(S["const_in"], 16)
            sp.dma_start(earlier[:], dram["earlier"]).then_inc(S["const_in"], 16)
            sp.dma_start(tokens[:], dram["tokens"]).then_inc(S["const_in"], 16)
            sp.dma_start(experts[:], dram["experts"]).then_inc(S["const_in"], 16)
            sp.dma_start(iota[:], dram["unit_ids"]).then_inc(S["const_in"], 16)
            with sp.Fori(0, LT) as i:
                at = sp.snap(i * P)
                sp.wait_ge(S["turned"], i * 4)
                alone(sp, S["s_passed"])
                sp.dma_start(mt[:], dram["merged"][bass.ds(at, P), :]).then_inc(S["merged_in"], 16)
                sp.wait_ge(S["h_ready"], i)
                alone(sp, S["s_passed"])
                sp.dma_start(x[:], dram["x"][0][bass.ds(at, P), :]).then_inc(S["x_in"], 16)
                sp.wait_ge(S["v_ready"], i + 1)
                alone(sp, S["s_passed"])
                sp.dma_start(dram["v_rows"][bass.ds(at, P), :], vv[:]).then_inc(S["v_out"], 16)
                sp.wait_ge(S["out_ready"], i + 1)
                alone(sp, S["s_passed"])
                sp.dma_start(dram["sum"][bass.ds(at, P), :], out[:]).then_inc(S["sum_out"], 16)
            sp.wait_ge(S["v_out"], 16 * LT)
            sp.wait_ge(S["sum_out"], 16 * LT)

        @block.tensor
        def _(pe):
            pe.wait_ge(S["const_in"], 16 * (NCONST + 4))
            with pe.Fori(0, LT) as i:
                for n in range(2):
                    if n == 0:
                        pe.wait_ge(S["merged_in"], i * 16 + 16)
                        pe.wait_ge(S["vT_ready"], i * 2)
                    for k in range(4):
                        tt = pe.transpose(tb[n][:, k * P:(k + 1) * P], mt[:, (4 * n + k) * P:(4 * n + k + 1) * P], ident[:])
                    tt.then_inc(S["turned"], 1)
                pe.wait_ge(S["mT_ready"], i * 2 + 2)
                pe.wait_ge(S["out_ready"], i)
                for j in range(4):
                    for k in range(KT):
                        mm = pe.matmul(py[j // 2][:, (j % 2) * 256:(j % 2 + 1) * 256], mT[:, k, :], W[j][:, k, :], start=(k == 0), stop=(k == KT - 1))
                mm.then_inc(S["y_done"], 1)
                pe.wait_ge(S["v_ready"], i + 1)
                for n in range(2):
                    for k in range(4):
                        tt = pe.transpose(tb[n][:, k * P:(k + 1) * P], vv[:, (4 * n + k) * P:(4 * n + k + 1) * P], ident[:])
                    tt.then_inc(S["turned"], 1)
                pe.wait_ge(S["vT_ready"], i * 2 + 2)
                for k in range(KT):
                    mm = pe.matmul(pl[:, 0:NE], vT[:, k, :], rw[:, k, :], start=(k == 0), stop=(k == KT - 1))
                mm.then_inc(S["logits_done"], 1)
                pe.wait_ge(S["sel_ready"], i + 1)
                pe.matmul(pp[:, 0:NE], earlier[:], sel[:], start=True, stop=False)
                pe.matmul(pp[:, 0:NE], ones[:], seen[:], start=False, stop=True).then_inc(S["placed_done"], 1)
                pe.wait_ge(S["dense_ready"], i + 1)
                pe.transpose(pd[0:NE, 0:P], dense[:], ident[:]).then_inc(S["denseT_done"], 1)
                pe.wait_ge(S["denseT_ready"], i + 1)
                for n in range(2):
                    mm = pe.matmul(py[n][:], denseT[:], b2[:, n * 512:(n + 1) * 512], start=True, stop=True)
                mm.then_inc(S["bias_done"], 1)
            pe.wait_ge(S["seen_ready"], LT + 1)
            pe.matmul(pl[0:NE, 0:1], seen[:], ones[:, 0:1], start=True, stop=True).then_inc(S["counted"], 1)
            pe.wait_ge(S["unit_step"], 2)
            pe.matmul(pl[0:NE, 0:1], earlier[0:NE, 0:NE], n_parts[:], start=True, stop=True).then_inc(S["counted"], 1)
            pe.wait_ge(S["unit_step"], 3)
            pe.matmul(pl[0:1, 0:4 * UNITS], ones[0:NE, 0:1], units[:].rearrange("e a u -> e (a u)"), start=True, stop=True).then_inc(S["counted"], 1)

        @block.scalar
        def _(act):
            with act.Fori(0, LT) as i:
                for n in range(2):
                    act.wait_ge(S["turned"], i * 4 + (n + 1))
                    act.activation(mT[:, 4 * n:4 * n + 4, :], tb[n][:].rearrange("p (k n) -> p k n", k=4), ACT.Copy).then_inc(S["mT_ready"], 1)
                act.wait_ge(S["h_ready"], i + 1)
                act.activation(sq[:], h_[:], ACT.Square, accum_out=ms[:]).then_inc(S["squared"], 1)
                act.wait_ge(S["ms_ready"], i + 1)
                act.activation(ms[:], ms[:], ACT.Sqrt).then_inc(S["root_ready"], 1)
                for n in range(2):
                    act.wait_ge(S["turned"], i * 4 + (n + 3))
                    act.activation(vT[:, 4 * n:4 * n + 4, :], tb[n][:].rearrange("p (k n) -> p k n", k=4), ACT.Copy).then_inc(S["vT_ready"], 1)
                act.wait_ge(S["top_ready"], i + 1)
                act.activation(ex[:], top[:, 0:TOPK], ACT.Exp, bias=nmax[:], accum_out=den[:]).then_inc(S["exped"], 1)
                act.wait_ge(S["denseT_done"], i + 1)
                act.activation(denseT[:], pd[0:NE, 0:P], ACT.Copy).then_inc(S["denseT_ready"], 1)

        @block.vector
        def _(v):
            v.memset(ones[:], 1.0).then_inc(S["seen_ready"], 1)
            v.memset(seen[:], 0.0).then_inc(S["unit_step"], 1)
            v.wait_ge(S["const_in"], 16 * (NCONST + 4))
            c = Steps(v, S["dve"])
            c.did(v.tensor_scalar(base[:], experts[:], float(SEQ), None, ALU.mult))
            c.link(v.scalar_tensor_tensor(scale[:], scale[:], 1.0, fw[:], ALU.add, ALU.mult))
            with v.Fori(0, LT) as i:
                c = Steps(v, S["dve"], i * STEPS + 2)
                v.wait_ge(S["y_done"], i + 1)
                v.wait_ge(S["x_in"], i * 16 + 16)
                for n in range(2):
                    c.did(v.tensor_tensor(h_[:, n * 512:(n + 1) * 512], py[n][:], g1[:, n * 512:(n + 1) * 512], ALU.mult))
                c.wait()
                v.tensor_tensor(h_[:], h_[:], x[:], ALU.add).then_inc(S["h_ready"], 1)
                v.wait_ge(S["squared"], i + 1)
                v.tensor_scalar(ms[:], ms[:], 1.0 / D, EPS, ALU.mult, ALU.add).then_inc(S["ms_ready"], 1)
                v.wait_ge(S["root_ready"], i + 1)
                c.link(v.reciprocal(ms[:], ms[:]))
                v.wait_ge(S["v_out"], i * 16)
                c.link(v.scalar_tensor_tensor(vv[:], h_[:], ms[:], scale[:], ALU.mult, ALU.mult))
                v.tensor_tensor(vv[:], vv[:], shift[:], ALU.add).then_inc(S["v_ready"], 1)
                v.wait_ge(S["logits_done"], i + 1)
                c.did(v.tensor_tensor(lg[:], pl[:, 0:NE], rb[:], ALU.add))
                c.wait()
                alone(v, S["v_passed"])
                c.did(v.max(out=top[:], in_=lg[:]))
                c.wait()
                alone(v, S["v_passed"])
                c.did(v.max_index(out=topi[:], in_max=top[:], in_values=lg[:]))
                v.tensor_scalar(nmax[:], top[:, 0:1], -1.0, None, ALU.mult).then_inc(S["top_ready"], 1)
                c.wait()
                c.link(v.tensor_copy(topf[:], topi[:, 0:TOPK]))
                for k in range(TOPK):
                    c.did(v.tensor_scalar(hot[:, k, :], experts[:], topf[:, k:k + 1], None, ALU.is_equal))
                c.wait()
                v.tensor_reduce(sel[:], hot[:].rearrange("p k e -> p e k"), AX.X, ALU.add).then_inc(S["sel_ready"], 1)
                v.wait_ge(S["exped"], i + 1)
                v.wait_ge(S["scattered"], i * 64)
                c.link(v.reciprocal(den[:], den[:]))
                c.did(v.tensor_copy(pairs[:, :, 0], tokens[:, bass.ds(i, 1)].to_broadcast((P, TOPK))))
                c.link(v.tensor_scalar(pairs[:, :, 1], ex[:], den[:], None, ALU.mult))
                c.link(v.tensor_tensor(pick[:], hot[:], pairs[:, :, 1:2].to_broadcast((P, TOPK, NE)), ALU.mult))
                v.tensor_reduce(dense[:], pick[:].rearrange("p k e -> p e k"), AX.X, ALU.add).then_inc(S["dense_ready"], 1)
                v.wait_ge(S["placed_done"], i + 1)
                v.wait_ge(S["dense_ready"], i + 1)
                v.wait_ge(S["seen_ready"], i + 1)
                v.tensor_tensor(seen[:], seen[:], sel[:], ALU.add).then_inc(S["seen_ready"], 1)
                c.link(v.tensor_tensor(place[:], pp[:, 0:NE], base[:], ALU.add))
                c.link(v.tensor_tensor(pick[:], hot[:], place[:].unsqueeze(1).to_broadcast((P, TOPK, NE)), ALU.mult))
                c.link(v.tensor_reduce(dest[:], pick[:], AX.X, ALU.add))
                v.tensor_copy(desti[:], dest[:]).then_inc(S["dest_ready"], 1)
                v.wait_ge(S["bias_done"], i + 1)
                v.wait_ge(S["sum_out"], i * 16)
                for n in range(2):
                    c.did(v.tensor_tensor(out[:, n * 512:(n + 1) * 512], py[n][:], g2[:, n * 512:(n + 1) * 512], ALU.mult))
                c.wait()
                v.tensor_tensor(out[:], out[:], h_[:], ALU.add).then_inc(S["out_ready"], 1)
                assert c.n == STEPS, c.n
            c = Steps(v, S["dve"], LT * STEPS + 2)
            ids = iota[:, UNITS:UNITS + 1]
            begin, begin_all = iota[:, UNITS + 1:UNITS + 1 + PARTS], iota[:, UNITS + 1 + PARTS:]
            v.wait_ge(S["counted"], 1)
            c.link(v.tensor_copy(cnt[:, 0:1], pl[0:NE, 0:1]))
            c.link(v.tensor_tensor(more[:, 1, :], cnt[:, 0:1].to_broadcast((NE, PARTS)), begin, ALU.subtract))
            c.link(v.tensor_scalar(more[:, 0, :], more[:, 1, :], 0.0, None, ALU.is_gt))
            v.tensor_reduce(n_parts[:], more[:, 0, :], AX.X, ALU.add).then_inc(S["unit_step"], 1)
            v.wait_ge(S["unit_step"], 2)
            v.wait_ge(S["counted"], 2)
            c.link(v.tensor_copy(cnt[:, 1:2], pl[0:NE, 0:1]))
            c.link(v.tensor_tensor(more[:, 2, :], cnt[:, 1:2].to_broadcast((NE, PARTS)), iota[:, 0:PARTS], ALU.add))
            for j in range(PARTS):
                c.did(v.tensor_scalar(mine[:, j, :], iota[:, 0:UNITS], more[:, 2, j:j + 1], more[:, 0, j:j + 1], ALU.is_equal, ALU.mult))
            c.wait()
            c.link(v.tensor_reduce(keep["own"][0:NE], mine[:].rearrange("e j u -> e u j"), AX.X, ALU.add))
            c.did(v.tensor_copy(keep["own"][NE:], keep["own"][0:NE]))
            c.did(v.tensor_scalar(units[:, 0, :], keep["own"][0:NE], ids, None, ALU.mult))
            c.did(v.tensor_scalar(units[:, 2, :], iota[:, 0:UNITS], 0.0, n_parts[:], ALU.is_equal, ALU.mult))
            c.did(v.tensor_scalar(units[:, 1, :], mine[:, 0, :], more[:, 1, 0:1], None, ALU.mult))
            c.link(v.tensor_scalar(units[:, 3, :], mine[:, 0, :], begin_all[:, 0:1], None, ALU.mult))
            for j in range(1, PARTS):
                c.did(v.scalar_tensor_tensor(units[:, 1, :], mine[:, j, :], more[:, 1, j:j + 1], units[:, 1, :], ALU.mult, ALU.add))
                c.link(v.scalar_tensor_tensor(units[:, 3, :], mine[:, j, :], begin_all[:, j:j + 1], units[:, 3, :], ALU.mult, ALU.add))
            v.sem_inc(S["unit_step"], 1)
            v.wait_ge(S["counted"], 3)
            v.tensor_copy(keep["units"][:], pl[0:1, 0:4 * UNITS]).then_inc(S["units_done"], 1)
            v.wait_ge(S["units_done"], 1)

        @block.gpsimd
        def _(g):
            g.wait_ge(keep["emptied"], 32)
            with g.Fori(0, LT) as i:
                g.wait_ge(S["dest_ready"], i + 1)
                alone(g, S["g_passed"])
                for k in range(TOPK):
                    g.indirect_dma_start(dram["lists"], bass.IndirectOffsetOnAxis(ap=desti[:, k:k + 1], axis=0), pairs[:, k, :], None).then_inc(S["scattered"], 16)
            g.wait_ge(S["scattered"], 16 * TOPK * LT)


def experts(nc, m, dram, keep):
    with ExitStack() as ctx:
        t = Machine(nc, ctx)
        NB = CAP // P
        PIECES, RING = 12, 4
        KH = KT // 2
        more = [t.sb_twice(f"e_slot{i}", [P, WSLOT]) for i in range(SLOTS, PIECES)]
        raw = keep["slots"] + [x[0] for x in more]
        wlo = keep["slots_r"] + [x[1] for x in more]
        whi = [t.sb(f"e_whi{i}", [P, WSLOT], F32R) for i in range(RING)]
        xhi, xlo = t.sb("e_xhi", [P, KT, CAP], F32R), t.sb("e_xlo", [P, KT, CAP], F32R)
        ahi, alo = t.sb("e_ahi", [P, KT, CAP], F32R), t.sb("e_alo", [P, KT, CAP], F32R)
        xg = [t.sb(f"e_xg{i}", [P, D]) for i in range(NB)]
        yo = t.sb("e_yo", [P, NB, D])
        glu, lin, sig = (t.sb("e_" + n, [P, NB, 256]) for n in ("glu", "lin", "sig"))
        act_rows = [t.sb(f"e_act{i}", [P, NB, 256]) for i in range(2)]
        g2 = t.sb("e_g2", [P, D])
        spark = t.sb("e_spark", [1, 1])
        b1 = t.sb("e_b1", [2 * NE, 2 * D], F32R)
        pick = t.sb("e_pick", [2 * NE, P], F32R)
        lists = t.sb("e_lists", [P, NB, 2])
        idx_next = t.sb("e_idx_next", [P, NB], U32)
        idx_mid, gate_mid = t.sb("e_idx_mid", [P, NB], U32), t.sb("e_gate_mid", [P, NB])
        idx_now = t.sb("e_idx_now", [P, NB], U32)
        hb = [t.ps(f"e_hb{i}", [P, NB, 512]) for i in range(2)]
        yb = [t.ps("e_yb", [P, NB, 512]), hb[1]]
        tb = [t.ps(f"e_tb{i}") for i in range(2)]
        names = """const_in set b1_high b1_ready lists_in mid_ready next_ready now_ready pick_ready gates_ready whi_made wlo_dve wlo_pool
        piece_done glu_ready hid_taken sig_made lin_ready act_ready turned hi_made lo_made y_taken scattered
        g_passed a_passed s_passed""".split()
        S = {n: t.sem("e_" + n) for n in names}
        w_in = [t.sem(f"e_w_in{i}") for i in range(PIECES)]
        gath = [t.sem(f"e_gath{i}") for i in range(NB)]
        ident, U, own = keep["ident"], keep["units"], keep["own"]
        FIRST, GROUPS = 4, 8
        ACT_GROUP, ROW_GROUP = [0, 1, 2, 3], [4, 5, 6, 7]
        ctx.callback(t.clear)
        block = ctx.enter_context(nc.Block())

        def units_of(e):
            return e.snap(e.value_load(U[0:1, 2 * UNITS:2 * UNITS + 1], min_val=1, max_val=UNITS - 1))

        def expert_of(e, u):
            return e.value_load(U[0:1, bass.ds(u, 1)], min_val=0, max_val=NE - 1)

        def count_of(e, u):
            return e.value_load(U[0:1, bass.ds(u + UNITS, 1)], min_val=0, max_val=SEQ)

        def by_pool(i):
            return i % 3 == 2

        def wait_rest(e, i, u):
            if by_pool(i):
                e.wait_ge(S["wlo_pool"], u * (PIECES // 3) + (i + 1) // 3)
            else:
                e.wait_ge(S["wlo_dve"], u * (PIECES - PIECES // 3) + (i + 1 - (i + 1) // 3))

        def rest(e, i, u, done):
            e.wait_ge(S["whi_made"], u * PIECES + (i + 1))
            e.tensor_tensor(wlo[i % PIECES][:], raw[i % PIECES][:], whi[i % RING][:].bitcast(F32), ALU.subtract).then_inc(done, 1)

        @block.sync
        def _(sp):
            sp.dma_start(g2[:], dram["ada_rows"][:, 3 * D:].to_broadcast((P, D))).then_inc(S["const_in"], 16)
            for i in range(2):
                sp.dma_start(yo[i * NE:(i + 1) * NE].rearrange("p b n -> p (b n)"), dram["b1"][0]).then_inc(S["const_in"], 16)

            def load(i, e):
                w = (dram["w1"] if i < 8 else dram["w2"])[0][bass.ds(e, 1), :, :].rearrange("a (k p) n -> p (a k) n", p=P)[:, i % 2 * KH:(i % 2 + 1) * KH, :]
                to = raw[i][:].rearrange("p (k n) -> p k n", k=KH)
                if i < 8:
                    for f in range(2):
                        col = f * D + i // 2 * 256
                        sp.dma_start(to[:, :, f * 256:(f + 1) * 256], w[:, :, col:col + 256]).then_inc(w_in[i], 16)
                else:
                    col = (i // 2 - 4) * 512
                    sp.dma_start(to, w[:, :, col:col + 512]).then_inc(w_in[i], 32)

            n_units = units_of(sp)
            e0 = expert_of(sp, 0)
            for i in range(PIECES):
                load(i, e0)
            with sp.Fori(0, n_units) as u:
                en = expert_of(sp, u + 1)
                for i in range(PIECES):
                    sp.wait_ge(S["piece_done"], u * PIECES + (i + 1))
                    alone(sp, S["s_passed"])
                    load(i, en)
            for i in range(PIECES):
                sp.wait_ge(w_in[i], n_units * 32 + 32)
                alone(sp, S["s_passed"])

        @block.gpsimd
        def _(g):
            g.wait_ge(S["set"], NB)

            def load_lists(u):
                at = g.value_load(U[0:1, bass.ds(u + 3 * UNITS, 1)], min_val=0, max_val=NE * SEQ - CAP)
                g.dma_start(lists[:], dram["lists"][bass.ds(at, CAP), :].rearrange("(b p) c -> p b c", p=P)).then_inc(S["lists_in"], 16)

            def gather(b):
                g.indirect_dma_start(xg[b][:], None, dram["v_rows"], bass.IndirectOffsetOnAxis(ap=idx_next[:, b:b + 1], axis=0),
                                     bounds_check=SEQ - 1, oob_is_err=False).then_inc(gath[b], 16)

            n_units = units_of(g)
            load_lists(0)
            g.wait_ge(S["next_ready"], 1)
            for b in range(NB):
                gather(b)
            for i in range(RING):
                if by_pool(i):
                    rest(g, i, 0, S["wlo_pool"])
            with g.Fori(0, n_units) as u:
                g.wait_ge(S["mid_ready"], u + 1)
                alone(g, S["g_passed"])
                load_lists(u + 1)
                pieces = [i for i in range(RING, PIECES + RING) if by_pool(i)]
                rest(g, pieces[0], u, S["wlo_pool"])
                g.wait_ge(S["next_ready"], u + 2)
                g.wait_ge(S["turned"], u * GROUPS + FIRST)
                alone(g, S["g_passed"])
                for b in range(NB):
                    gather(b)
                for i in pieces[1:]:
                    rest(g, i, u, S["wlo_pool"])
                cnt = count_of(g, u)
                g.wait_ge(S["scattered"], u * (16 * NB))
                g.wait_ge(S["y_taken"], u * 2 + 2)
                g.wait_ge(S["now_ready"], u + 1)
                alone(g, S["g_passed"])

                def scatter(nb):
                    for b in range(nb):
                        n = 1 if b < nb - 1 else 1 + NB - nb
                        g.indirect_dma_start(dram["sum"], bass.IndirectOffsetOnAxis(ap=idx_now[:, b:b + 1], axis=0), yo[:, b, :], None,
                                             compute_op=ALU.add).then_inc(S["scattered"], 16 * n)

                with g.If(cnt > P):
                    scatter(2)
                with g.Else():
                    scatter(1)
            g.wait_ge(S["scattered"], n_units * (16 * NB))
            alone(g, S["g_passed"])

        def by_size(e, cnt, body):
            with e.If(cnt > P):
                body(2)
            with e.Else():
                body(1)

        @block.tensor
        def _(pe):
            n_units = units_of(pe)

            def turn_rows(g, base, loads):
                r = g - ROW_GROUP[0] if base is not None else g
                b, hf = r // 2, r % 2
                if hf == 0:
                    pe.wait_ge(gath[b], loads)
                if base is not None:
                    pe.wait_ge(S["lo_made"], base + (g - 1))
                elif g >= 2:
                    pe.wait_ge(S["lo_made"], g - 1)
                for k in range(4):
                    tt = pe.transpose(tb[g % 2][:, k * P:(k + 1) * P], xg[b][:, (4 * hf + k) * P:(4 * hf + k + 1) * P], ident[:])
                tt.then_inc(S["turned"], 1)

            for g in range(FIRST):
                turn_rows(g, None, 16)
            pe.wait_ge(S["b1_ready"], 1)
            with pe.Fori(0, n_units) as u:
                cnt = count_of(pe, u)
                base = u * GROUPS + FIRST

                def turn_act(p, nb):
                    g = ACT_GROUP[p]
                    pe.wait_ge(S["act_ready"], u * 4 + (p + 1))
                    pe.wait_ge(S["lo_made"], base + (g - 1))
                    for b in range(nb):
                        for q in range(2):
                            tt = pe.transpose(tb[g % 2][:, (2 * b + q) * P:(2 * b + q + 1) * P], act_rows[p % 2][:, b, q * P:(q + 1) * P], ident[:])
                    tt.then_inc(S["turned"], 1)

                def products(out, hi, lo, nb, i):
                    wait_rest(pe, i, u)
                    wh, wl = whi[i % RING][:], wlo[i][:]
                    for b in range(nb):
                        c = slice(b * P, (b + 1) * P)
                        for k in range(KH):
                            w, kk = slice(k * 512, (k + 1) * 512), i % 2 * KH + k
                            pe.matmul(out[:, b, :], hi[:, kk, c], wh[:, w], start=(i >= 8 and kk == 0), stop=False)
                            pe.matmul(out[:, b, :], hi[:, kk, c], wl[:, w], start=False, stop=False)
                            mm = pe.matmul(out[:, b, :], lo[:, kk, c], wh[:, w], start=False, stop=(kk == KT - 1))
                    mm.then_inc(S["piece_done"], 1)

                def body(nb):
                    pe.wait_ge(S["pick_ready"], u + 1)
                    for p in range(4):
                        if p == 0:
                            pe.wait_ge(S["lo_made"], base)
                            pe.wait_ge(S["hid_taken"], u * 4)
                        elif p == 1:
                            pe.wait_ge(S["y_taken"], u * 2)
                        else:
                            pe.wait_ge(S["hid_taken"], u * 4 + (p - 1))
                        out = hb[p % 2]
                        for b in range(nb):
                            pe.matmul(out[:, b, :], pick[:], b1[:].rearrange("e (f n) -> e f n", f=2)[:, :, p * 256:(p + 1) * 256], start=True, stop=False)
                        products(out, xhi, xlo, nb, 2 * p)
                        products(out, xhi, xlo, nb, 2 * p + 1)
                        if 1 <= p < 3:
                            turn_act(p - 1, nb)
                    pe.wait_ge(S["lo_made"], base + (ACT_GROUP[1] + 1))
                    products(yb[0], ahi, alo, nb, 8)
                    turn_act(2, nb)
                    turn_act(3, nb)
                    turn_rows(ROW_GROUP[0], base, u * 16 + 32)
                    pe.wait_ge(S["lo_made"], base + (ACT_GROUP[3] + 1))
                    products(yb[0], ahi, alo, nb, 9)
                    turn_rows(ROW_GROUP[1], base, u * 16 + 32)
                    turn_rows(ROW_GROUP[2], base, u * 16 + 32)
                    products(yb[1], ahi, alo, nb, 10)
                    turn_rows(ROW_GROUP[3], base, u * 16 + 32)
                    products(yb[1], ahi, alo, nb, 11)

                by_size(pe, cnt, body)

        @block.scalar
        def _(act):
            act.wait_ge(S["const_in"], 48)
            act.activation(b1[:], yo[0:2 * NE].rearrange("p b n -> p (b n)"), ACT.Copy).then_inc(S["b1_high"], 1)
            n_units = units_of(act)

            def high(i, u, ahead=True):
                act.wait_ge(w_in[i % PIECES], (u + i // PIECES) * 32 + 32)
                if ahead:
                    act.wait_ge(S["piece_done"], u * PIECES + (i - RING + 1))
                act.activation(whi[i % RING][:], raw[i % PIECES][:], ACT.Copy).then_inc(S["whi_made"], 1)

            def high_rows(r, parity, count):
                act.wait_ge(S["turned"], count)
                b, hf = r // 2, r % 2
                act.activation(xhi[:, 4 * hf:4 * hf + 4, b * P:(b + 1) * P], tb[parity][:].rearrange("p (k n) -> p k n", k=4), ACT.Copy).then_inc(S["hi_made"], 1)

            for r in range(FIRST):
                high_rows(r, r % 2, r + 1)
            for i in range(RING):
                high(i, 0, ahead=False)
            with act.Fori(0, n_units) as u:
                cnt = count_of(act, u)
                base = u * GROUPS + FIRST

                def high_act(p, nb):
                    g = ACT_GROUP[p]
                    act.wait_ge(S["turned"], base + (g + 1))
                    act.activation(ahi[:, 2 * p:2 * p + 2, 0:nb * P].rearrange("p q (b n) -> p b q n", b=nb),
                                   tb[g % 2][:, 0:nb * 256].rearrange("p (b q n) -> p b q n", b=nb, q=2), ACT.Copy).then_inc(S["hi_made"], 1)

                def body(nb):
                    act.wait_ge(S["a_passed"], u)
                    act.activation(spark[:], ident[0:1, 0:1], ACT.Sigmoid).then_inc(S["a_passed"], 1)
                    for p in range(4):
                        high(2 * p + RING, u)
                        act.wait_ge(S["glu_ready"], u * 4 + (p + 1))
                        act.activation(sig[:, 0:nb], glu[:, 0:nb], ACT.Sigmoid, scale=1.702).then_inc(S["sig_made"], 1)
                        if 1 <= p < 3:
                            high_act(p - 1, nb)
                        high(2 * p + RING + 1, u)
                    rows = lambda r: high_rows(r, ROW_GROUP[r] % 2, base + (ROW_GROUP[r] + 1))
                    high_act(2, nb)
                    high_act(3, nb)
                    rows(0)
                    high(8 + RING, u)
                    rows(1)
                    rows(2)
                    high(9 + RING, u)
                    rows(3)
                    high(10 + RING, u)
                    high(11 + RING, u)

                by_size(act, cnt, body)

        @block.vector
        def _(v):
            for x in xg:
                v.memset(x[:], 0.0).then_inc(S["set"], 1)
            v.wait_ge(S["b1_high"], 1)
            lo_rows = slice(NE, 2 * NE)
            v.tensor_tensor(b1[lo_rows], yo[lo_rows].rearrange("p b n -> p (b n)"), b1[lo_rows].bitcast(F32), ALU.subtract).then_inc(S["b1_ready"], 1)
            n_units = units_of(v)

            def next_index(loads):
                v.wait_ge(S["lists_in"], loads)
                v.tensor_copy(idx_next[:], lists[:, :, 0]).then_inc(S["next_ready"], 1)

            def low_rows(r, parity, count):
                v.wait_ge(S["hi_made"], count)
                b, hf = r // 2, r % 2
                to = (slice(None), slice(4 * hf, 4 * hf + 4), slice(b * P, (b + 1) * P))
                v.tensor_tensor(xlo[to], tb[parity][:].rearrange("p (k n) -> p k n", k=4), xhi[to].bitcast(F32), ALU.subtract).then_inc(S["lo_made"], 1)

            next_index(16)
            for r in range(FIRST):
                low_rows(r, r % 2, r + 1)
            for i in range(RING):
                if not by_pool(i):
                    rest(v, i, 0, S["wlo_dve"])
            v.tensor_copy(pick[:], own[:, 0:1].to_broadcast((2 * NE, P))).then_inc(S["pick_ready"], 1)
            with v.Fori(0, n_units) as u:
                cnt = count_of(v, u)
                base = u * GROUPS + FIRST
                v.wait_ge(S["next_ready"], u + 1)
                v.wait_ge(S["now_ready"], u)
                v.wait_ge(S["y_taken"], u * 2)
                v.tensor_copy(gate_mid[:], lists[:, :, 1]).then_inc(S["gates_ready"], 1)
                v.tensor_copy(idx_mid[:], idx_next[:]).then_inc(S["mid_ready"], 1)

                def low_act(p, nb):
                    g = ACT_GROUP[p]
                    v.wait_ge(S["hi_made"], base + (g + 1))
                    to = lambda x: x[:, 2 * p:2 * p + 2, 0:nb * P].rearrange("p q (b n) -> p b q n", b=nb)
                    v.tensor_tensor(to(alo), tb[g % 2][:, 0:nb * 256].rearrange("p (b q n) -> p b q n", b=nb, q=2), to(ahi).bitcast(F32),
                                    ALU.subtract).then_inc(S["lo_made"], 1)

                def rest_ahead(i):
                    if not by_pool(i + RING):
                        rest(v, i + RING, u, S["wlo_dve"])

                def body(nb):
                    for p in range(4):
                        g_, l_, s_ = glu[:, 0:nb], lin[:, 0:nb], sig[:, 0:nb]
                        h = hb[p % 2][:, 0:nb]
                        n = u * 4 + (p + 1)
                        rest_ahead(2 * p)
                        v.wait_ge(S["piece_done"], u * PIECES + (2 * p + 2))
                        v.tensor_scalar(g_, h[:, :, 0:256], LIMIT, None, ALU.min).then_inc(S["glu_ready"], 1)
                        v.tensor_scalar(l_, h[:, :, 256:512], LIMIT, -LIMIT, ALU.min, ALU.max).then_inc(S["hid_taken"], 1)
                        v.wait_ge(S["hid_taken"], n)
                        v.wait_ge(S["glu_ready"], n)
                        v.scalar_tensor_tensor(l_, l_, 1.0, g_, ALU.add, ALU.mult).then_inc(S["lin_ready"], 1)
                        v.wait_ge(S["lin_ready"], n)
                        v.wait_ge(S["sig_made"], n)
                        v.tensor_tensor(act_rows[p % 2][:, 0:nb], l_, s_, ALU.mult).then_inc(S["act_ready"], 1)
                        v.wait_ge(S["act_ready"], n)
                        if p == 0:
                            next_index(u * 16 + 32)
                        if 1 <= p < 3:
                            low_act(p - 1, nb)
                        rest_ahead(2 * p + 1)
                    rows = lambda r: low_rows(r, ROW_GROUP[r] % 2, base + (ROW_GROUP[r] + 1))

                    def take(j):
                        v.wait_ge(S["piece_done"], u * PIECES + (10 + 2 * j))
                        for b in range(nb):
                            x = v.scalar_tensor_tensor(yo[:, b, j * 512:(j + 1) * 512], yb[j][:, b, :], gate_mid[:, b:b + 1], g2[:, j * 512:(j + 1) * 512], ALU.mult, ALU.mult)
                        x.then_inc(S["y_taken"], 1)

                    v.tensor_copy(pick[:], own[:, bass.ds(u + 1, 1)].to_broadcast((2 * NE, P))).then_inc(S["pick_ready"], 1)
                    low_act(2, nb)
                    low_act(3, nb)
                    rows(0)
                    rest_ahead(8)
                    v.wait_ge(S["scattered"], u * (16 * NB))
                    v.wait_ge(S["mid_ready"], u + 1)
                    v.tensor_copy(idx_now[:], idx_mid[:]).then_inc(S["now_ready"], 1)
                    v.wait_ge(S["gates_ready"], u + 1)
                    rows(1)
                    rows(2)
                    take(0)
                    rest_ahead(9)
                    rows(3)
                    rest_ahead(10)
                    take(1)
                    rest_ahead(11)

                by_size(v, cnt, body)


def finish(nc, m, dram, keep):
    with ExitStack() as ctx:
        t = Machine(nc, ctx)
        x = t.sb("f_x", [P, LT, D])
        sq = t.sb("f_sq", [P, D])
        nw = t.sb("f_nw", [P, D])
        ms = t.sb("f_ms", [P, LT])
        w_in, squared, ms_ready, root_ready, inv_ready, ready, out = (t.sem("f_" + n) for n in ("w_in", "squared", "ms_ready", "root_ready", "inv_ready", "ready", "out"))
        x_in = [t.sem(f"f_x_in{i}") for i in range(LT)]
        ctx.callback(t.clear)
        block = ctx.enter_context(nc.Block())

        @block.sync
        def _(sp):
            for i in range(LT):
                sp.dma_start(x[:, i, :], dram["sum"][i * P:(i + 1) * P, :]).then_inc(x_in[i], 16)
            sp.dma_start(nw[:], dram["norm_final_w"].rearrange("(a n) -> a n", a=1).to_broadcast((P, D))).then_inc(w_in, 16)
            for i in range(LT):
                sp.wait_ge(ready, i + 1)
                sp.dma_start(dram["out"][0, i * P:(i + 1) * P, :], x[:, i, :]).then_inc(out, 16)
            sp.wait_ge(out, 16 * LT)

        @block.scalar
        def _(act):
            for i in range(LT):
                act.wait_ge(x_in[i], 16)
                if i:
                    act.wait_ge(squared, i)
                act.activation(sq[:], x[:, i, :], ACT.Square, accum_out=ms[:, i:i + 1]).then_inc(squared, 1)
            for i in range(LT):
                act.wait_ge(ms_ready, i + 1)
                act.activation(ms[:, i:i + 1], ms[:, i:i + 1], ACT.Sqrt).then_inc(root_ready, 1)

        @block.vector
        def _(v):
            v.wait_ge(w_in, 16)
            for i in range(LT):
                r = ms[:, i:i + 1]
                v.wait_ge(squared, i + 1)
                v.tensor_scalar(r, r, 1.0 / D, EPS, ALU.mult, ALU.add).then_inc(ms_ready, 1)
            for i in range(LT):
                r = ms[:, i:i + 1]
                v.wait_ge(root_ready, i + 1)
                v.reciprocal(r, r).then_inc(inv_ready, 1)
                v.wait_ge(inv_ready, i + 1)
                v.scalar_tensor_tensor(x[:, i, :], x[:, i, :], r, nw[:], ALU.mult, ALU.mult).then_inc(ready, 1)


IN = ["x", "c", "ctx", "c_ctx", "w_ada", "b_ada", "norm_mix_w", "norm_ffn_w", "w_in", "w_out", "hg_lb",
      "hg_norm_w", "router_w", "router_b", "w1", "b1", "w2", "b2", "norm_final_w"]


def build(nc, dram, stages=99):
    with ExitStack() as ctx:
        m = Machine(nc, ctx)
        dram["ada_rows"] = nc.dram_tensor("ada_rows", [1, 4 * D], F32, kind="Internal").ap()
        dram["v_rows"] = nc.dram_tensor("v_rows", [SEQ, D], F32, kind="Internal").ap()
        dram["sum"] = nc.dram_tensor("sum", [SEQ + CAP, D], F32, kind="Internal").ap()
        dram["lists"] = nc.dram_tensor("lists", [NE * SEQ, 2], F32, kind="Internal").ap()
        dram["merged"] = nc.dram_tensor("merged", [SEQ, D], F32, kind="Internal").ap()
        slots = [m.sb_twice(f"slot{i}", [P, WSLOT]) for i in range(SLOTS)]
        keep = dict(
            slots=[x[0] for x in slots], slots_r=[x[1] for x in slots],
            landed=[m.sem(f"landed{i}") for i in range(SLOTS)], released=[m.sem(f"released{i}") for i in range(SLOTS)],
            ident=m.sb("ident", [P, P]), const_in=m.sem("const_in"),
            lb=m.sb("lb", [P, 8]), oml=m.sb("oml", [P, 8]), lb_ready=m.sem("lb_ready"), emptied=m.sem("emptied"), bound_part=m.sem("bound_part"), u_ready=m.sem("u_ready"),
        )
        with ExitStack() as mix:
            keep["uT"] = Machine(nc, mix).sb("uT", [P, KT, N])
            modulate(nc, m, dram, keep)
            if stages >= 1:
                retention(nc, m, dram, keep)
            if stages >= 2:
                hgrn2(nc, m, dram, keep)
        keep["units"] = m.sb("units", [1, 4 * UNITS], I32)
        keep["own"] = m.sb("own", [2 * NE, UNITS])
        if stages >= 3:
            route(nc, m, dram, keep)
        if stages >= 4:
            experts(nc, m, dram, keep)
            finish(nc, m, dram, keep)


def kernel(**inputs):
    import concourse.bacc as bacc
    from concourse.bass_utils import run_bass_kernel_spmd

    nc = bacc.Bacc("TRN2", target_bir_lowering=False, num_devices=1)
    arrays, dram = {}, {}
    for prefix, names, source in (("in_", IN, inputs), ("c_", None, constants())):
        for name in names or source:
            a = np.ascontiguousarray(source[name])
            arrays[prefix + name] = a
            dram[name] = nc.dram_tensor(prefix + name, list(a.shape), mybir.dt.from_np(a.dtype), kind="ExternalInput").ap()
    dram["out"] = nc.dram_tensor("out", [1, SEQ, D], F32, kind="ExternalOutput").ap()
    build(nc, dram)
    r = run_bass_kernel_spmd(nc, [arrays], core_ids=[0])
    return r.results[0]["out"]
```

```python
from contextlib import ExitStack

import numpy as np

import concourse.bass as bass
from concourse import mybir

F32 = mybir.dt.float32
F32R = mybir.dt.float32r
U32 = mybir.dt.uint32
I32 = mybir.dt.int32
ALU = mybir.AluOpType
ACT = mybir.ActivationFunctionType
AX = mybir.AxisListType

P = 128
D = 1024
KT = D // P
CTX, SEQ = 256, 1024
CT, LT = CTX // P, SEQ // P
NT = CT + LT
N = CTX + SEQ
HEADS = 4
RDK = 64
HALF = RDK // 2
ADA = 6 * D
NE = 32
TOPK = 4
EPS = 1e-6
CAP = 256
LIMIT = 7.0
PARTS = SEQ // CAP
UNITS = NE + TOPK * SEQ // CAP
SLOTS = 4
WSLOT = 2048
TASKS = NT + LT // 2
LEVELS = [64, 32, 16, 8, 4, 2, 1]
FINE = LEVELS[2:]
O_RQ, O_RK, O_RV, O_RG, O_HQ, O_ZF, O_ZB, O_HV, O_HG = 0, 256, 512, 1024, 1536, 2048, 2560, 3072, 3584


def constants():
    p = np.arange(P)
    f = np.float32
    out = {"ident": np.eye(P, dtype=f)}
    t = np.arange(SEQ)
    inv = 10000.0 ** (-np.arange(RDK // 4) / (RDK // 4))
    ang = np.concatenate([(t // 64)[:, None] * inv, (t % 64)[:, None] * inv], 1)
    out["cos"] = np.cos(ang).astype(f).reshape(LT, P, HALF).transpose(1, 0, 2).reshape(P, LT * HALF)
    out["sin"] = np.sin(ang).astype(f).reshape(LT, P, HALF).transpose(1, 0, 2).reshape(P, LT * HALF)
    h = np.arange(HEADS)
    gf = 1.0 - 2.0 ** (-5.0 - 2.0 * h)
    gb = 1.0 - 2.0 ** (-6.0 - 2.0 * h)
    s, q = p[:, None], p[None, :]
    dec = [RDK ** -0.5 * (np.where(q >= s, gf[i] ** np.maximum(q - s, 0), 0) + np.where(q <= s, gb[i] ** np.maximum(s - q, 0), 0)) for i in h]
    out["retdecay"] = np.stack(dec).astype(f)
    col = np.stack([np.stack([gf[i] ** (p + 1), gb[i] ** (P - p), RDK ** -0.5 * gf[i] ** (P - 1 - p), RDK ** -0.5 * gb[i] ** p,
                              np.where(p < RDK, gf[i] ** P, gb[i] ** P)], 1) for i in h])
    out["retcols"] = col.astype(f)
    masks = [(s == q) | (s // 32 != q // 32)]
    for hl in FINE:
        masks.append((s // (2 * hl) == q // (2 * hl)) & (s // hl != q // hl))
    out["masks"] = np.stack(masks, 1).astype(f).reshape(P, -1)
    out["scanmask"] = np.tile((np.arange(N) % P != 0).astype(f)[None], (P, 1))
    out["earlier"] = (s < q).astype(f)
    out["tokens"] = (np.arange(LT)[None] * P + p[:, None]).astype(f)
    out["experts"] = np.tile(np.arange(NE, dtype=f)[None], (P, 1))
    place = np.arange(NE * SEQ)
    out["empty_lists"] = np.stack([SEQ + place % CAP, 0 * place], 1).astype(f)
    out["spare_rows"] = np.zeros((CAP, D), f)
    e, part = np.arange(NE)[:, None], CAP * np.arange(PARTS)[None]
    out["unit_ids"] = np.concatenate([0 * e + np.arange(UNITS)[None], e, 0 * e + part, e * SEQ + part], 1).astype(f)
    return out


def alone(engine, passed):
    engine.sem_inc(passed, 1)


class Steps:

    def __init__(self, engine, sem, base=0):
        self.engine, self.sem, self.base, self.n = engine, sem, base, 0

    def did(self, ins):
        self.n += 1
        ins.then_inc(self.sem, 1)
        return self.n

    def wait(self, n=None):
        self.engine.wait_ge(self.sem, self.base + (self.n if n is None else n))

    def link(self, ins):
        self.did(ins)
        self.wait()


class Machine:

    def __init__(self, nc, ctx):
        self.nc, self.ctx, self.sems = nc, ctx, []

    def sb(self, name, shape, dt=F32):
        return self.ctx.enter_context(self.nc.sbuf_tensor(name, shape, dt))

    def sb_twice(self, name, shape):
        at = -(-self.nc.sbuf_base // 32) * 32
        x = self.sb(name, shape)
        return x, self.nc.alloc_sbuf_tensor_at(name + "_r", shape, F32R, offset=at)

    def ps(self, name, shape=(P, 512), dt=F32):
        return self.ctx.enter_context(self.nc.psum_tensor(name, list(shape), dt))

    def sem(self, name):
        self.sems.append(self.ctx.enter_context(self.nc.semaphore(name)))
        return self.sems[-1]

    def clear(self):
        with self.nc.Block() as block:
            @block.gpsimd
            def _(g):
                for x in self.sems:
                    g.sem_clear(x)


def modulate(nc, m, dram, keep):
    with ExitStack() as ctx:
        t = Machine(nc, ctx)
        xt = t.sb("xt", [P, NT, D])
        acc = t.sb("acc", [P, 4 * D])
        rows = t.sb("rows", [48, P])
        cols = t.sb("cols", [P, 48])
        sc = t.sb("sc", [P, 2, KT])
        scs = t.sb("scs", [P, 2, KT])
        square = t.sb("square", [P, D])
        ms = t.sb("ms", [P, NT])
        rstd = t.sb("rstd", [P, NT])
        acol = t.sb("acol", [P, KT, 2])
        bcol = t.sb("bcol", [P, KT, 2])
        lbd = t.sb("lbd", [P, 8])
        ones = t.sb("ones", [P, 1])
        arow = t.sb("arow", [1, 4 * D])
        tp = [t.ps(f"tp{i}") for i in range(4)]
        pa = t.ps("pa")
        pr = [t.ps(f"pr{i}") for i in range(2)]
        x_in = [t.sem(f"x_in{i}") for i in range(NT)]
        c_in = t.sem("c_in")
        acc_in = t.sem("acc_in")
        zeroed = t.sem("zeroed")
        squared = t.sem("squared")
        ms_ready = t.sem("ms_ready")
        root_ready = t.sem("root_ready")
        normed = t.sem("normed")
        turned = t.sem("turned")
        evacuated = t.sem("evacuated")
        cols_turned = t.sem("cols_turned")
        cols_ready = t.sem("cols_ready")
        silu_part = t.sem("silu_part")
        s_ready = t.sem("s_ready")
        ada_cols = t.sem("ada_cols")
        dve = t.sem("mod_dve")
        row_summed = t.sem("row_summed")
        row_ready = t.sem("row_ready")
        row_out = t.sem("row_out")
        lb_part = t.sem("lb_part")
        slots, landed, released = keep["slots"], keep["landed"], keep["released"]
        uT, lb, oml = keep["uT"], keep["lb"], keep["oml"]
        ident = keep["ident"]
        others = [(g, k) for g in (1, 2) for k in range(KT)]
        PLAN = [(0, n // 3) if n % 3 == 0 else others[n - n // 3 - 1] for n in range(3 * KT)]
        ctx.callback(t.clear)
        block = ctx.enter_context(nc.Block())

        @block.sync
        def _(sp):
            sp.dma_start(dram["lists"], dram["empty_lists"]).then_inc(keep["emptied"], 16)
            sp.dma_start(dram["sum"][SEQ:, :], dram["spare_rows"]).then_inc(keep["emptied"], 16)
            sp.dma_start(ident[:], dram["ident"]).then_inc(keep["const_in"], 16)
            sp.dma_start(rows[0:16, :], dram["b_ada"][0, 0:2 * D].rearrange("(r p) -> r p", p=P)).then_inc(c_in, 16)
            sp.dma_start(rows[16:24, :], dram["norm_mix_w"][0].rearrange("(r p) -> r p", p=P)).then_inc(c_in, 16)
            sp.dma_start(rows[24:40, :], dram["hg_lb"].rearrange("a b (r p) -> (a b r) p", p=P)).then_inc(c_in, 16)
            sp.dma_start(sc[:, 0, :], dram["c"][0].rearrange("(p k) -> p k", k=KT)).then_inc(c_in, 16)
            sp.dma_start(sc[:, 1, :], dram["c_ctx"].rearrange("(p k) -> p k", k=KT)).then_inc(c_in, 16)
            sp.wait_ge(zeroed, 1)
            sp.dma_start(acc[0:1, :], dram["b_ada"][0:1, 2 * D:]).then_inc(acc_in, 16)
            for i in range(NT):
                src = dram["ctx"][0] if i < CT else dram["x"][0]
                r = i if i < CT else i - CT
                sp.dma_start(xt[:, i, :], src[r * P:(r + 1) * P, :]).then_inc(x_in[i], 16)
            wa = dram["w_ada"][0].rearrange("(p k) n -> p k n", k=KT)
            for n, (g, k) in enumerate(PLAN):
                if n >= SLOTS:
                    sp.wait_ge(released[n % SLOTS], n // SLOTS)
                sp.dma_start(slots[n % SLOTS][:], wa[:, k, g * WSLOT:(g + 1) * WSLOT]).then_inc(landed[n % SLOTS], 16)
            sp.wait_ge(row_ready, 8)
            sp.dma_start(dram["ada_rows"], arow[:]).then_inc(row_out, 16)
            sp.wait_ge(row_out, 16)

        @block.scalar
        def _(act):
            act.wait_ge(c_in, 80)
            act.activation(scs[:], sc[:], ACT.Sigmoid).then_inc(silu_part, 1)
            act.wait_ge(cols_ready, 1)
            act.wait_ge(lb_part, 1)
            act.activation(lb[:], lbd[:], ACT.Sigmoid).then_inc(keep["lb_ready"], 1)
            for i in range(NT):
                act.wait_ge(x_in[i], 16)
                if i:
                    act.wait_ge(squared, i)
                act.activation(square[:], xt[:, i, :], ACT.Square, accum_out=ms[:, i:i + 1]).then_inc(squared, 1)
            act.wait_ge(ms_ready, 1)
            act.activation(rstd[:], ms[:], ACT.Sqrt).then_inc(root_ready, 1)
            for i in range(NT):
                for b in range(2):
                    n = 2 * i + b
                    act.wait_ge(turned, n + 1)
                    act.activation(uT[:, 4 * b:4 * b + 4, i * P:(i + 1) * P], tp[n % 4][:].rearrange("p (k t) -> p k t", k=4), ACT.Copy).then_inc(evacuated, 1)
            for j in range(8):
                act.wait_ge(row_summed, j + 1)
                act.activation(arow[:, j * 512:(j + 1) * 512], pr[j % 2][0:1, :], ACT.Copy).then_inc(row_ready, 1)

        @block.vector
        def _(v):
            c = Steps(v, dve)
            v.memset(acc[:], 0.0).then_inc(zeroed, 1)
            v.memset(ones[:], 1.0).then_inc(zeroed, 1)
            v.wait_ge(silu_part, 1)
            v.tensor_tensor(sc[:], sc[:], scs[:], ALU.mult).then_inc(s_ready, 1)
            v.wait_ge(cols_turned, 1)
            v.tensor_copy(cols[:, 0:40], pa[:, 64:104]).then_inc(cols_ready, 1)
            v.wait_ge(cols_ready, 1)
            v.tensor_tensor(lbd[:], cols[:, 24:32], cols[:, 32:40], ALU.subtract).then_inc(lb_part, 1)
            v.wait_ge(keep["lb_ready"], 1)
            v.tensor_scalar(oml[:], lb[:], -1.0, 1.0, ALU.mult, ALU.add).then_inc(keep["lb_ready"], 1)
            v.wait_ge(squared, NT)
            v.tensor_scalar(ms[:], ms[:], 1.0 / D, EPS, ALU.mult, ALU.add).then_inc(ms_ready, 1)
            v.wait_ge(root_ready, 1)
            c.link(v.reciprocal(rstd[:], rstd[:]))
            for i in range(NT):
                v.tensor_scalar(xt[:, i, :], xt[:, i, :], rstd[:, i:i + 1], None, ALU.mult).then_inc(normed, 1)
            v.wait_ge(acc_in, 16)
            for n, (g, k) in enumerate(PLAN):
                if g:
                    v.wait_ge(landed[n % SLOTS], 16 * (n // SLOTS + 1))
                    before = [m_ for m_ in range(n) if PLAN[m_][0]]
                    if before:
                        v.wait_ge(released[before[-1] % SLOTS], before[-1] // SLOTS + 1)
                    a = acc[:, (g - 1) * WSLOT:g * WSLOT]
                    v.scalar_tensor_tensor(a, slots[n % SLOTS][:], sc[:, 0, k:k + 1], a, ALU.mult, ALU.add).then_inc(released[n % SLOTS], 1)
            v.wait_ge(ada_cols, 1)
            pv = pa[:, 0:32].rearrange("p (j b) -> p j b", b=2)
            bias = cols[:, 0:16]
            c.link(v.tensor_tensor(bcol[:], pv[:, 0:8, :], bias[:, 0:8].unsqueeze(2).to_broadcast((P, 8, 2)), ALU.add))
            c.link(v.tensor_tensor(acol[:], pv[:, 8:16, :], bias[:, 8:16].unsqueeze(2).to_broadcast((P, 8, 2)), ALU.add))
            c.link(v.tensor_scalar(acol[:], acol[:], 1.0, None, ALU.add))
            c.link(v.tensor_tensor(acol[:], acol[:], cols[:, 16:24].unsqueeze(2).to_broadcast((P, 8, 2)), ALU.mult))
            v.wait_ge(evacuated, 2 * NT)
            for k in range(KT):
                for b, (a, z) in enumerate([(CTX, N), (0, CTX)]):
                    v.tensor_scalar(uT[:, k, a:z], uT[:, k, a:z], acol[:, k, b:b + 1], bcol[:, k, b:b + 1], ALU.mult, ALU.add).then_inc(keep["u_ready"], 1)

        @block.tensor
        def _(pe):
            pe.wait_ge(keep["const_in"], 16)
            pe.wait_ge(c_in, 80)
            pe.transpose(pa[:, 64:104], rows[0:40, :], ident[0:40, 0:40]).then_inc(cols_turned, 1)
            pe.wait_ge(s_ready, 1)
            pe.wait_ge(cols_ready, 1)
            def columns(k):
                n = 3 * k
                pe.wait_ge(landed[n % SLOTS], 16 * (n // SLOTS + 1))
                for j in range(16):
                    mm = pe.matmul(pa[:, 2 * j:2 * j + 2], slots[n % SLOTS][:, j * P:(j + 1) * P], sc[:, :, k],
                                   start=(k == 0 and j == 0), stop=(k == KT - 1), skip_group_check=True)
                mm.then_inc(released[n % SLOTS], 1)

            def turn(i):
                pe.wait_ge(normed, i + 1)
                for b in range(2):
                    n = 2 * i + b
                    if n >= 4:
                        pe.wait_ge(evacuated, n - 3)
                    for k in range(4):
                        tt = pe.transpose(tp[n % 4][:, k * P:(k + 1) * P], xt[:, i, (4 * b + k) * P:(4 * b + k + 1) * P], ident[:])
                    tt.then_inc(turned, 1)

            for k in range(KT):
                columns(k)
                if 1 <= k <= NT // 2:
                    turn(2 * k - 2)
                    turn(2 * k - 1)
            pe.matmul(pa[:, 504:505], ident[:], ident[:, 0:1], start=True, stop=True, skip_group_check=True).then_inc(ada_cols, 1)
            pe.wait_ge(zeroed, 2)
            for j in range(8):
                n = PLAN.index((2 if j >= 4 else 1, KT - 1))
                pe.wait_ge(released[n % SLOTS], n // SLOTS + 1)
                if j >= 2:
                    pe.wait_ge(row_ready, j - 1)
                pe.matmul(pr[j % 2][0:1, :], ones[:], acc[:, j * 512:(j + 1) * 512], start=True, stop=True).then_inc(row_summed, 1)


def project(pe, out, uT, tile, w, cols):
    for k in range(KT):
        mm = pe.matmul(out, uT[:, k, tile * P:(tile + 1) * P], w[:, k, cols], start=(k == 0), stop=(k == KT - 1))
    return mm


def hgrn2(nc, m, dram, keep):
    with ExitStack() as ctx:
        t = Machine(nc, ctx)
        HT = LT // 2
        HN = HT * P
        NL = len(LEVELS)
        NM = len(FINE) + 1
        key = [t.sb(f"h_key{d}", [P, N]) for d in range(2)]
        cum = [t.sb(f"h_cum{d}", [P, N]) for d in range(2)]
        cumb = t.sb("h_cumb", [P, N])
        scan = t.sb("h_scan", [P, N])
        sigq = t.sb("h_sigq", [P, SEQ])
        q = t.sb("h_q", [P, SEQ])
        qdec = [t.sb(f"h_qdec{d}", [P, SEQ]) for d in range(2)]
        kdec = [t.sb(f"h_kdec{d}", [P, N]) for d in range(2)]
        wk = t.sb("h_wk", [P, NL + 1, HN])
        wq = t.sb("h_wq", [P, NL, HN])
        val = t.sb("h_val", [P, NT, P])
        gate = t.sb("h_gate", [P, LT, P])
        sigg = t.sb("h_sigg", [P, LT, P])
        ktok = [t.sb(f"h_ktok{d}", [P, NT, P]) for d in range(2)]
        state = [t.sb(f"h_state{d}", [P, LT + 1, P]) for d in range(2)]
        total = t.sb("h_total", [P, 2, NT])
        st = [t.sb(f"h_st{i}", [P, P]) for i in range(2)]
        o = sigg
        sq = t.sb("h_sq", [P, P])
        ms = t.sb("h_ms", [P, LT])
        stage = [t.sb(f"h_stage{i}", [P, 256]) for i in range(2)]
        bound = t.sb("h_bound", [P, HEADS, 2, 3])
        bnd = t.sb("h_bnd", [P, 2, 3])
        masks = t.sb("h_masks", [P, NM, P])
        picked = t.sb("h_picked", [P, NM, P])
        nw = t.sb("h_nw", [P, P])
        pj = [t.ps(f"h_pj{i}") for i in range(2)]
        ps = [t.ps(f"h_ps{i}") for i in range(4)]
        po = t.ps("h_po")
        tb = [t.ps("h_tb"), po]
        names = """const_in dve bounds z_done z_sig logf q_done q_sig q_ready v_done v_ready g_done g_sig gate_ready
        cumulated keys_ready pool_sub exped dec_ready turned ktok_ready u_done lev_sub lev_exp lev_ready s_done
         st_ready o_done squared ms_ready root_ready o_ready o_out s_passed a_passed task_done task_taken""".split()
        S = {x: t.sem("h_" + x) for x in names}
        slots, landed, released = keep["slots"], keep["landed"], keep["released"]
        staged = [t.sem(f"h_staged{i}") for i in range(2)]
        uT, ident = keep["uT"], keep["ident"]
        W = [slots[i][:].rearrange("p (k n) -> p k n", k=KT) for i in range(4)]
        b0 = 3 * KT // SLOTS
        L = 16 * b0
        win = dram["w_in"][0].rearrange("(k p) n -> p k n", p=P)
        RNG = [(0, CTX), (CTX, CTX + 512), (CTX + 512, N)]
        FREE_AT = 1 + 3 * NL + 2
        U_FREE = [FREE_AT + 2, FREE_AT + 6]
        STATES_AT = 1 + 3 * NL + 2 * (LT + 1)
        PICKED = [STATES_AT + 2 * (j + 1) for j in range(HT)]
        PICKED += [PICKED[-1] + 3 * NL + 2] + [PICKED[-1] + 3 * NL + 3 + 2 * (j + 1) for j in range(HT - 1)]
        STEPS = PICKED[-1] + 1
        ctx.callback(t.clear)
        block = ctx.enter_context(nc.Block())

        @block.sync
        def _(sp):
            for i in range(SLOTS):
                sp.wait_ge(released[i], b0)
            sp.dma_start(masks[:].rearrange("p a b -> p (a b)"), dram["masks"]).then_inc(S["const_in"], 16)
            sp.dma_start(scan[:], dram["scanmask"]).then_inc(S["const_in"], 16)
            sp.dma_start(nw[:], dram["hg_norm_w"].to_broadcast((P, P))).then_inc(S["const_in"], 16)
            with sp.Fori(0, HEADS) as h:
                at = [sp.snap(h * P + x) for x in (O_ZF, O_ZB, O_HQ, O_HV, O_HG)]
                at_r = [sp.snap(h * P + O_RV), sp.snap(h * RDK + O_RQ), sp.snap(h * RDK + O_RK), sp.snap(h * P + O_RG)]
                at_tasks = sp.snap(h * TASKS)
                sp.wait_ge(S["z_done"], h * 6)
                alone(sp, S["s_passed"])
                sp.dma_start(W[0][:, :, 0:P], win[:, :, bass.ds(at[0], P)]).then_inc(landed[0], 16)
                sp.dma_start(W[0][:, :, P:], win[:, :, bass.ds(at[1], P)]).then_inc(landed[0], 16)
                sp.wait_ge(S["v_done"], h * 3)
                alone(sp, S["s_passed"])
                sp.dma_start(W[1][:, :, 0:P], win[:, :, bass.ds(at[2], P)]).then_inc(landed[1], 16)
                sp.dma_start(W[1][:, :, P:], win[:, :, bass.ds(at[3], P)]).then_inc(landed[1], 16)
                sp.wait_ge(S["g_done"], h * 2)
                alone(sp, S["s_passed"])
                sp.dma_start(W[2][:, :, 0:P], win[:, :, bass.ds(at[4], P)]).then_inc(landed[2], 16)
                sp.wait_ge(S["task_done"], h * TASKS)
                alone(sp, S["s_passed"])
                sp.dma_start(W[3][:, :, 0:P], win[:, :, bass.ds(at_r[0], P)]).then_inc(landed[3], 16)
                sp.dma_start(W[3][:, :, P:P + RDK], win[:, :, bass.ds(at_r[1], RDK)]).then_inc(landed[3], 16)
                sp.dma_start(W[3][:, :, P + RDK:], win[:, :, bass.ds(at_r[2], RDK)]).then_inc(landed[3], 16)
                sp.dma_start(W[2][:, :, P:], win[:, :, bass.ds(at_r[3], P)]).then_inc(landed[3], 16)
                for n in range(TASKS):
                    sp.wait_ge(S["task_taken"], h * TASKS + (n + 1))
                    alone(sp, S["s_passed"])
                    sp.dma_start(dram["projected"][bass.ds(at_tasks + n, 1), :, :].rearrange("a p c -> (a p) c"), stage[n % 2][:]).then_inc(staged[n % 2], 16)
            for i in range(2):
                sp.wait_ge(staged[i], 8 * TASKS * HEADS)
            sp.wait_ge(S["o_out"], 16 * HEADS)

        @block.tensor
        def _(pe):
            pe.wait_ge(keep["u_ready"], 2 * KT)
            with pe.Fori(0, HEADS) as h:
                def tasks(ns):
                    for n in ns:
                        if n == 0:
                            pe.wait_ge(landed[3], h * 64 + (L + 64))
                        if n < 2:
                            pe.wait_ge(S["gate_ready"], h * 2 + 2)
                        else:
                            pe.wait_ge(S["task_taken"], h * TASKS + (n - 1))
                        if n < NT:
                            mm = project(pe, pj[n % 2][:, 0:256], uT, n, W[3], slice(0, 256))
                        else:
                            for i in range(2):
                                mm = project(pe, pj[n % 2][:, i * P:(i + 1) * P], uT, CT + 2 * (n - NT) + i, W[2], slice(P, 2 * P))
                        mm.then_inc(S["task_done"], 1)

                pe.wait_ge(S["gate_ready"], h * 2)
                pe.wait_ge(S["task_taken"], h * TASKS)
                pe.wait_ge(landed[0], h * 32 + (L + 32))
                for d in range(2):
                    for j, (a, z) in enumerate(RNG):
                        n = 3 * d + j
                        if n >= 2:
                            pe.wait_ge(S["z_sig"], h * 6 + (n - 1))
                        for k in range(KT):
                            mm = pe.matmul(pj[n % 2][:, 0:z - a], W[0][:, k, d * P:(d + 1) * P], uT[:, k, a:z], start=(k == 0), stop=(k == KT - 1))
                        mm.then_inc(S["z_done"], 1)
                pe.wait_ge(landed[1], h * 32 + (L + 32))
                for j in range(2):
                    pe.wait_ge(S["z_sig"], h * 6 + (5 + j))
                    for k in range(KT):
                        mm = pe.matmul(pj[j][:], W[1][:, k, 0:P], uT[:, k, RNG[j + 1][0]:RNG[j + 1][1]], start=(k == 0), stop=(k == KT - 1))
                    mm.then_inc(S["q_done"], 1)
                for g in range(3):
                    if g < 2:
                        pe.wait_ge(S["q_ready"], h * 2 + (g + 1))
                    else:
                        pe.wait_ge(S["v_ready"], h * 3 + 1)
                    for i in range(min(4, NT - 4 * g)):
                        mm = project(pe, pj[g % 2][:, i * P:(i + 1) * P], uT, 4 * g + i, W[1], slice(P, 2 * P))
                    mm.then_inc(S["v_done"], 1)
                pe.wait_ge(landed[2], h * 16 + (L + 16))
                for g in range(2):
                    pe.wait_ge(S["v_ready"], h * 3 + (g + 2))
                    for i in range(4):
                        mm = project(pe, pj[(g + 1) % 2][:, i * P:(i + 1) * P], uT, CT + 4 * g + i, W[2], slice(0, P))
                    mm.then_inc(S["g_done"], 1)
                tasks(range(0, 2))
                for d in range(2):
                    pe.wait_ge(S["dec_ready"], h * 4 + (d + 1))
                    pe.wait_ge(S["o_ready"], h * LT)
                    for g in range(3):
                        n = 3 * d + g
                        if n == 2:
                            tasks(range(2, 5))
                        if n >= 2:
                            pe.wait_ge(S["ktok_ready"], h * 6 + (n - 1))
                        for i in range(min(4, NT - 4 * g)):
                            c = 4 * g + i
                            tt = pe.transpose(tb[n % 2][:, i * P:(i + 1) * P], kdec[d][:, c * P:(c + 1) * P], ident[:])
                        tt.then_inc(S["turned"], 1)
                for d in range(2):
                    for g in range(3):
                        bank = (3 * d + g) % 4
                        if 3 * d + g < 4:
                            pe.wait_ge(S["st_ready"], h * LT)
                        else:
                            pe.wait_ge(S["dve"], h * STEPS + U_FREE[bank])
                        pe.wait_ge(S["ktok_ready"], h * 6 + (3 * d + g + 1))
                        for i in range(min(4, NT - 4 * g)):
                            c = 4 * g + i
                            mm = pe.matmul(ps[bank][:, i * P:(i + 1) * P], ktok[d][:, c, :], val[:, c, :], start=True, stop=True)
                        mm.then_inc(S["u_done"], 1)
                tasks(range(5, 6))
                pe.wait_ge(S["dve"], h * STEPS + STATES_AT)

                def scores(half, i):
                    j = HT * half + i
                    bank = ps[2 * (j % 2)], ps[2 * (j % 2) + 1]
                    if j >= 2:
                        pe.wait_ge(S["dve"], h * STEPS + PICKED[j - 2])
                    if i == 0:
                        pe.wait_ge(S["lev_ready"], h * 2 + (half + 1))
                    c = slice(i * P, (i + 1) * P)
                    pe.matmul(bank[0][:, 0:P], wk[:, NL, c], q[:, j * P:(j + 1) * P], start=True, stop=True)
                    for l, hl in enumerate(LEVELS[:2]):
                        for a in range(0, P, 2 * hl):
                            for key_at, query_at in ((a, a + hl), (a + hl, a)):
                                pe.matmul(bank[0][key_at:key_at + hl, query_at:query_at + hl], wk[:, l, i * P + key_at:i * P + key_at + hl],
                                          wq[:, l, i * P + query_at:i * P + query_at + hl], start=True, stop=True)
                    for r in range(1, NM):
                        mm = pe.matmul(bank[r // 4][:, (r % 4) * P:(r % 4 + 1) * P], wk[:, r + 1, c], wq[:, r + 1, c], start=True, stop=True)
                    mm.then_inc(S["s_done"], 1)

                def output(j):
                    pe.wait_ge(S["st_ready"], h * LT + (j + 1))
                    if j == HT:
                        pe.wait_ge(S["o_ready"], h * LT + HT)
                    out = po[:, (j % HT) * P:(j % HT + 1) * P]
                    pe.matmul(out, st[j % 2][:], val[:, CT + j, :], start=True, stop=False)
                    for d in range(2):
                        mm = pe.matmul(out, qdec[d][:, j * P:(j + 1) * P], state[d][:, j, :], start=False, stop=(d == 1))
                    mm.then_inc(S["o_done"], 1)

                pe.wait_ge(S["dec_ready"], h * 4 + 4)
                for j in range(LT):
                    if j == HT:
                        tasks(range(6, 12))
                    if j > HT + 1:
                        tasks(range(j + 12 - (HT + 2), j + 13 - (HT + 2)))
                    scores(j // HT, j % HT)
                    if j:
                        output(j - 1)
                output(LT - 1)

        @block.scalar
        def _(act):
            with act.Fori(0, HEADS) as h:
                at_o = act.snap(h * P + HEADS * P)
                act.wait_ge(S["bounds"], h + 1)
                act.wait_ge(S["lev_ready"], h * 2)
                for d in range(2):
                    for j, (a, z) in enumerate(RNG):
                        n = 3 * d + j
                        act.wait_ge(S["z_done"], h * 6 + (n + 1))
                        act.activation(key[d][:, a:z], pj[n % 2][:, 0:z - a], ACT.Sigmoid).then_inc(S["z_sig"], 1)
                for j in range(2):
                    act.wait_ge(S["q_done"], h * 2 + (j + 1))
                    act.activation(sigq[:, j * 512:(j + 1) * 512], pj[j][:], ACT.Sigmoid).then_inc(S["q_sig"], 1)
                for d in range(2):
                    act.wait_ge(S["z_sig"], h * 6 + (3 * d + 3))
                    act.activation(cum[d][:], key[d][:], ACT.Ln, scale=bnd[:, d, 1:2], bias=bnd[:, d, 0:1]).then_inc(S["logf"], 1)
                act.wait_ge(S["o_done"], h * LT)
                for g in range(3):
                    act.wait_ge(S["v_done"], h * 3 + (g + 1))
                    n = min(4, NT - 4 * g)
                    act.activation(val[:, 4 * g:4 * g + n, :], pj[g % 2][:, 0:n * P].rearrange("p (i n) -> p i n", i=n), ACT.Copy).then_inc(S["v_ready"], 1)
                act.wait_ge(S["o_out"], h * 16)
                for g in range(2):
                    act.wait_ge(S["g_done"], h * 2 + (g + 1))
                    act.activation(sigg[:, 4 * g:4 * g + 4, :], pj[(g + 1) % 2][:].rearrange("p (i n) -> p i n", i=4), ACT.Sigmoid).then_inc(S["g_sig"], 1)
                act.wait_ge(S["pool_sub"], h * 3 + 1)
                act.activation(kdec[0][:], kdec[0][:], ACT.Exp).then_inc(S["exped"], 1)
                act.wait_ge(S["pool_sub"], h * 3 + 2)
                act.activation(kdec[1][:], cum[1][:], ACT.Exp).then_inc(S["exped"], 1)
                act.activation(qdec[0][:], cum[0][:, CTX:], ACT.Exp).then_inc(S["exped"], 1)
                act.wait_ge(S["pool_sub"], h * 3 + 3)
                act.activation(qdec[1][:], qdec[1][:], ACT.Exp).then_inc(S["exped"], 1)
                act.activation(total[:, 0, :], cum[0][:].rearrange("p (i n) -> p i n", n=P)[:, :, P - 1], ACT.Exp).then_inc(S["exped"], 1)
                act.activation(total[:, 1, :], cumb[:].rearrange("p (i n) -> p i n", n=P)[:, :, P - 1], ACT.Exp).then_inc(S["exped"], 1)
                def levels(half):
                    for l in range(NL):
                        act.wait_ge(S["lev_sub"], h * (8 * NL) + (half * 4 * NL + 4 * l + 4))
                        for x in (wk, wq):
                            act.activation(x[:, l, :], x[:, l, :], ACT.Exp).then_inc(S["lev_exp"], 1)
                        if half == 1 and l:
                            take(5 + l)

                def turned_keys(groups):
                    for n in groups:
                        d, g = n // 3, n % 3
                        m_ = min(4, NT - 4 * g)
                        act.wait_ge(S["turned"], h * 6 + (n + 1))
                        act.activation(ktok[d][:, 4 * g:4 * g + m_, :], tb[n % 2][:, 0:m_ * P].rearrange("p (i n) -> p i n", i=m_), ACT.Copy).then_inc(S["ktok_ready"], 1)

                def square(half):
                    act.wait_ge(S["o_done"], h * LT + (half + 1) * HT)
                    for j in range(half * HT, half * HT + HT):
                        if j:
                            act.wait_ge(S["squared"], h * LT + j)
                        act.activation(sq[:], po[:, (j % HT) * P:(j % HT + 1) * P], ACT.Square, accum_out=ms[:, j:j + 1]).then_inc(S["squared"], 1)
                    act.wait_ge(S["ms_ready"], h * 2 + (half + 1))
                    act.activation(ms[:, half * HT:(half + 1) * HT], ms[:, half * HT:(half + 1) * HT], ACT.Sqrt).then_inc(S["root_ready"], 1)

                def take(n):
                    act.wait_ge(S["task_done"], h * TASKS + (n + 1))
                    act.wait_ge(staged[n % 2], h * (8 * TASKS) + 16 * (n // 2))
                    act.activation(stage[n % 2][:], pj[n % 2][:, 0:256], ACT.Copy).then_inc(S["task_taken"], 1)

                take(0)
                take(1)
                levels(0)
                turned_keys(range(0, 2))
                for n in range(2, 5):
                    take(n)
                turned_keys(range(2, 6))
                take(5)
                levels(1)
                square(0)
                take(12)
                take(13)
                square(1)
                act.wait_ge(S["o_ready"], h * LT + LT)
                alone(act, S["a_passed"])
                act.dma_start(dram["merged"].rearrange("(i p) n -> p i n", p=P)[:, :, bass.ds(at_o, P)], o[:]).then_inc(S["o_out"], 16)

        @block.gpsimd
        def _(g):
            with g.Fori(0, HEADS) as h:
                c3 = lambda x, a=0, z=N: x[:, a:z].rearrange("p (i n) -> p i n", n=P)
                g.wait_ge(S["cumulated"], h * 2 + 1)
                g.wait_ge(S["u_done"], h * 6)
                g.tensor_tensor(c3(kdec[0]), c3(cum[0])[:, :, P - 1:P].to_broadcast((P, NT, P)), c3(cum[0]), ALU.subtract).then_inc(S["pool_sub"], 1)
                g.wait_ge(S["cumulated"], h * 2 + 2)
                g.tensor_tensor(cum[1][:], cumb[:], cum[1][:], ALU.subtract).then_inc(S["pool_sub"], 1)
                g.wait_ge(S["pool_sub"], h * 3 + 2)
                g.tensor_tensor(c3(qdec[1], 0, SEQ), c3(cumb, CTX)[:, :, P - 1:P].to_broadcast((P, LT, P)), c3(cum[1], CTX), ALU.subtract).then_inc(S["pool_sub"], 1)
                for half in range(2):
                    g.wait_ge(S["s_done"], h * LT + half * HT)
                    for l, hl in enumerate(LEVELS):
                        nb = HN // (2 * hl)
                        view = lambda x: x.rearrange("p (b f n) -> p b f n", f=2, n=hl)
                        fwd, bwd = (view(cum[d][:, CTX + half * HN:CTX + (half + 1) * HN]) for d in range(2))
                        k4, q4 = view(wk[:, l, :]), view(wq[:, l, :])
                        mf = fwd[:, :, 0, hl - 1:hl].to_broadcast((P, nb, hl))
                        mb = bwd[:, :, 1, 0:1].to_broadcast((P, nb, hl))
                        for out, x, y in ((k4[:, :, 0], mf, fwd[:, :, 0]), (k4[:, :, 1], bwd[:, :, 1], mb),
                                          (q4[:, :, 0], mb, bwd[:, :, 0]), (q4[:, :, 1], fwd[:, :, 1], mf)):
                            g.tensor_tensor(out, x, y, ALU.subtract).then_inc(S["lev_sub"], 1)

        @block.vector
        def _(v):
            v.wait_ge(keep["lb_ready"], 2)
            c = Steps(v, S["bounds"])
            for n, (src, sign) in enumerate([(keep["lb"], 1.0), (keep["oml"], 1.0), (keep["oml"], -1.0)]):
                v.tensor_scalar(bound[:, :, :, n], src[:].rearrange("p (d h) -> p h d", d=2), sign, None, ALU.mult).then_inc(keep["bound_part"], 1)
            v.wait_ge(keep["bound_part"], 3)
            v.wait_ge(S["const_in"], 48)
            with v.Fori(0, HEADS) as h:
                c = Steps(v, S["dve"], h * STEPS)
                v.wait_ge(S["logf"], h * 2)
                v.tensor_copy(bnd[:], bound[:, bass.ds(h, 1), :, :].rearrange("p a d n -> p (a d) n")).then_inc(S["bounds"], 1)
                v.wait_ge(S["bounds"], h + 1)
                for j in range(2):
                    v.wait_ge(S["q_sig"], h * 2 + (j + 1))
                    v.tensor_tensor(q[:, j * 512:(j + 1) * 512], pj[j][:], sigq[:, j * 512:(j + 1) * 512], ALU.mult).then_inc(S["q_ready"], 1)
                v.wait_ge(S["logf"], h * 2 + 1)
                v.tensor_tensor_scan(cum[0][:], scan[:], cum[0][:], 0.0, ALU.mult, ALU.add).then_inc(S["cumulated"], 1)
                v.wait_ge(S["logf"], h * 2 + 2)
                v.tensor_tensor_scan(cumb[:], scan[:], cum[1][:], 0.0, ALU.mult, ALU.add).then_inc(S["cumulated"], 1)
                for d in range(2):
                    v.tensor_scalar(key[d][:], key[d][:], bnd[:, d, 2:3], bnd[:, d, 1:2], ALU.mult, ALU.add).then_inc(S["keys_ready"], 1)
                for g in range(2):
                    v.wait_ge(S["g_sig"], h * 2 + (g + 1))
                    v.tensor_tensor(gate[:, 4 * g:4 * g + 4, :], pj[(g + 1) % 2][:].rearrange("p (i n) -> p i n", i=4), sigg[:, 4 * g:4 * g + 4, :], ALU.mult).then_inc(S["gate_ready"], 1)
                v.wait_ge(S["gate_ready"], h * 2 + 2)
                c.link(v.tensor_tensor(gate[:], gate[:], nw[:].unsqueeze(1).to_broadcast((P, LT, P)), ALU.mult))
                v.wait_ge(S["keys_ready"], h * 2 + 2)
                v.wait_ge(S["q_ready"], h * 2 + 2)
                for n, (buf, by) in enumerate([(kdec[0], key[0]), (kdec[1], key[1]), (qdec[0], q), (qdec[1], q)]):
                    v.wait_ge(S["exped"], h * 6 + (n + 1))
                    v.tensor_tensor(buf[:], buf[:], by[:], ALU.mult).then_inc(S["dec_ready"], 1)

                def levels(half):
                    lo = half * HN
                    v.wait_ge(S["s_done"], h * LT + half * HT)
                    k0, k1 = (key[d][:, CTX + lo:CTX + lo + HN] for d in range(2))
                    c.did(v.tensor_tensor(wk[:, NL, :], k0, k1, ALU.add))
                    for l, hl in enumerate(LEVELS):
                        view = lambda x: x.rearrange("p (b f n) -> p b f n", f=2, n=hl)
                        k4 = view(wk[:, l, :])
                        v.wait_ge(S["lev_exp"], h * (4 * NL) + (half * 2 * NL + 2 * l + 1))
                        c.did(v.tensor_tensor(k4[:, :, 0], k4[:, :, 0], view(k0)[:, :, 0], ALU.mult))
                        c.did(v.tensor_tensor(k4[:, :, 1], k4[:, :, 1], view(k1)[:, :, 1], ALU.mult))
                        v.wait_ge(S["lev_exp"], h * (4 * NL) + (half * 2 * NL + 2 * l + 2))
                        x = v.tensor_tensor(wq[:, l, :], wq[:, l, :], q[:, lo:lo + HN], ALU.mult)
                        if l < NL - 1:
                            c.did(x)
                        else:
                            x.then_inc(S["lev_ready"], 1)

                def states():
                    v.wait_ge(S["exped"], h * 6 + 6)
                    v.wait_ge(S["o_done"], h * LT)
                    U = lambda i: ps[i // 4][:, (i % 4) * P:(i % 4 + 1) * P]
                    v.wait_ge(S["u_done"], h * 6 + 3)
                    c.link(v.tensor_copy(state[0][:, LT, :], U(0)))
                    c.link(v.scalar_tensor_tensor(state[0][:, 0, :], state[0][:, LT, :], total[:, 0, 1:2], U(1), ALU.mult, ALU.add))
                    for j in range(LT - 1):
                        c.link(v.scalar_tensor_tensor(state[0][:, j + 1, :], state[0][:, j, :], total[:, 0, CT + j:CT + j + 1], U(CT + j), ALU.mult, ALU.add))
                    v.wait_ge(S["u_done"], h * 6 + 6)
                    U = lambda i: ps[(3 + i // 4) % 4][:, (i % 4) * P:(i % 4 + 1) * P]
                    c.link(v.tensor_copy(state[1][:, LT, :], U(1)))
                    c.link(v.scalar_tensor_tensor(state[1][:, LT - 1, :], state[1][:, LT, :], total[:, 1, 0:1], U(0), ALU.mult, ALU.add))
                    for j in range(LT - 1, 0, -1):
                        c.link(v.scalar_tensor_tensor(state[1][:, j - 1, :], state[1][:, j, :], total[:, 1, CT + j:CT + j + 1], U(CT + j), ALU.mult, ALU.add))

                def pick(j):
                    v.wait_ge(S["s_done"], h * LT + (j + 1))
                    c.did(v.tensor_tensor(picked[:, 0:4, :], ps[2 * (j % 2)][:].rearrange("p (r n) -> p r n", r=4), masks[:, 0:4, :], ALU.mult))
                    c.link(v.tensor_tensor(picked[:, 4:NM, :], ps[2 * (j % 2) + 1][:, 0:(NM - 4) * P].rearrange("p (r n) -> p r n", n=P), masks[:, 4:NM, :], ALU.mult))
                    if j >= 2:
                        v.wait_ge(S["o_done"], h * LT + (j - 1))
                    v.tensor_reduce(st[j % 2][:], picked[:].rearrange("p r n -> p n r"), AX.X, ALU.add).then_inc(S["st_ready"], 1)
                    v.wait_ge(S["st_ready"], h * LT + (j + 1))
                    assert c.n == PICKED[j], (c.n, j)

                def finish(half):
                    sl = slice(half * HT, half * HT + HT)
                    v.wait_ge(S["squared"], h * LT + (half + 1) * HT)
                    v.tensor_scalar(ms[:, sl], ms[:, sl], 1.0 / P, EPS, ALU.mult, ALU.add).then_inc(S["ms_ready"], 1)
                    v.wait_ge(S["root_ready"], h * 2 + (half + 1))
                    c.link(v.reciprocal(ms[:, sl], ms[:, sl]))
                    for j in range(half * HT, half * HT + HT):
                        v.scalar_tensor_tensor(o[:, j, :], po[:, (j % HT) * P:(j % HT + 1) * P], ms[:, j:j + 1], gate[:, j, :], ALU.mult, ALU.mult).then_inc(S["o_ready"], 1)

                levels(0)
                states()
                assert c.n == STATES_AT, c.n
                for j in range(HT):
                    pick(j)
                levels(1)
                pick(HT)
                finish(0)
                for j in range(HT + 1, LT):
                    pick(j)
                finish(1)
                assert c.n == STEPS, c.n


def retention(nc, m, dram, keep):
    with ExitStack() as ctx:
        t = Machine(nc, ctx)
        vqk = t.sb("r_vqk", [P, NT, 256])
        raw_gate = t.sb("r_raw_gate", [P, LT, P])
        sig = t.sb("r_sig", [P, LT, P])
        gate = t.sb("r_gate", [P, LT, P])
        qk = t.sb("r_qk", [P, LT, P])
        rot = t.sb("r_rot", [P, 4, LT, 2, HALF])
        kd = t.sb("r_kd", [P, NT, P])
        qd = t.sb("r_qd", [P, LT, P])
        qT = t.sb("r_qT", [RDK, LT, P])
        kT = t.sb("r_kT", [RDK, LT, P])
        qdT = t.sb("r_qdT", [P, LT, P])
        state = t.sb("r_state", [P, LT + 1, P])
        st = t.sb("r_st", [P, LT, P])
        o = t.sb("r_o", [P, LT, P])
        sq = t.sb("r_sq", [P, P])
        ms = t.sb("r_ms", [P, LT])
        cos = t.sb("r_cos", [P, LT, HALF])
        sin = t.sb("r_sin", [P, LT, HALF])
        decay = t.sb("r_decay", [P, P])
        dcol = t.sb("r_dcol", [P, 5])
        tb = [t.ps(f"r_tb{i}") for i in range(2)]
        pu = [t.ps(f"r_pu{i}") for i in range(3)]
        po1 = t.ps("r_po1")
        po = [pu[2], po1]
        trig_in = t.sem("r_trig_in")
        decay_in = t.sem("r_decay_in")
        s_passed = t.sem("r_s_passed")
        vqk_in, gate_in = t.sem("r_vqk_in"), t.sem("r_gate_in")
        g_sig, gate_ready = t.sem("r_g_sig"), t.sem("r_gate_ready")
        dve = t.sem("r_dve")
        rotated = t.sem("r_rotated")
        decayed = t.sem("r_decayed")
        u_done = t.sem("r_u_done")
        turned, qT_ready, kT_ready, qdT_ready = t.sem("r_turned"), t.sem("r_qT_ready"), t.sem("r_kT_ready"), t.sem("r_qdT_ready")
        s_done, st_ready = t.sem("r_s_done"), t.sem("r_st_ready")
        o_done, squared, ms_ready, root_ready, o_ready, o_out = (t.sem("r_" + x) for x in ("o_done", "squared", "ms_ready", "root_ready", "o_ready", "o_out"))
        ident = keep["ident"]
        STATES_AT = 10 + 4 + 2 * (LT - 1)
        DVE_STEPS = STATES_AT + 1
        ctx.callback(t.clear)
        block = ctx.enter_context(nc.Block())

        @block.sync
        def _(sp):
            sp.dma_start(cos[:].rearrange("p a b -> p (a b)"), dram["cos"]).then_inc(trig_in, 16)
            sp.dma_start(sin[:].rearrange("p a b -> p (a b)"), dram["sin"]).then_inc(trig_in, 16)
            with sp.Fori(0, HEADS) as h:
                at_o, at_tasks = sp.snap(h * P), sp.snap(h * TASKS)
                sp.wait_ge(o_done, h * 2)
                alone(sp, s_passed)
                sp.dma_start(vqk[:], dram["projected"][bass.ds(at_tasks, NT), :, :].rearrange("n p c -> p n c")).then_inc(vqk_in, 16)
                sp.wait_ge(gate_ready, h * 2)
                alone(sp, s_passed)
                sp.dma_start(raw_gate[:].rearrange("p (n i) c -> p n (i c)", i=2), dram["projected"][bass.ds(at_tasks + NT, LT // 2), :, :].rearrange("n p c -> p n c")).then_inc(gate_in, 16)
                sp.wait_ge(st_ready, h * 2)
                alone(sp, s_passed)
                sp.dma_start(decay[:], dram["retdecay"][bass.ds(h, 1), :, :].rearrange("a s t -> (a s) t")).then_inc(decay_in, 16)
                sp.dma_start(dcol[:], dram["retcols"][bass.ds(h, 1), :, :].rearrange("a s t -> (a s) t")).then_inc(decay_in, 16)
                sp.wait_ge(o_ready, h * LT + LT)
                alone(sp, s_passed)
                sp.dma_start(dram["merged"].rearrange("(i p) n -> p i n", p=P)[:, :, bass.ds(at_o, P)], o[:]).then_inc(o_out, 16)
            sp.wait_ge(o_out, 16 * HEADS)

        @block.tensor
        def _(pe):
            with pe.Fori(0, HEADS) as h:
                for n in range(4):
                    src = qk if n < 2 else qd
                    pe.wait_ge(rotated if n < 2 else decayed, h + 1)
                    if n == 2:
                        pe.wait_ge(qT_ready, h * 2 + 1)
                        pe.wait_ge(kT_ready, h * 2 + 1)
                    if n == 3:
                        pe.wait_ge(qT_ready, h * 2 + 2)
                        pe.wait_ge(kT_ready, h * 2 + 2)
                    for i in range(4):
                        tt = pe.transpose(tb[n % 2][:, i * P:(i + 1) * P], src[:, 4 * (n % 2) + i, :], ident[:])
                    tt.then_inc(turned, 1)
                pe.wait_ge(decayed, h + 1)
                pe.wait_ge(vqk_in, h * 16 + 16)
                pe.wait_ge(o_ready, h * LT)
                for g in range(3):
                    for i in range(4 if g < 2 else 2):
                        mm = pe.matmul(pu[g][:, i * P:(i + 1) * P], kd[:, 4 * g + i, :], vqk[:, 4 * g + i, 0:P], start=True, stop=True)
                    mm.then_inc(u_done, 1)
                pe.wait_ge(dve, h * DVE_STEPS + STATES_AT)
                for g in range(2):
                    pe.wait_ge(qT_ready, h * 2 + (g + 1))
                    pe.wait_ge(kT_ready, h * 2 + (g + 1))
                    for i in range(4):
                        mm = pe.matmul(pu[g][:, i * P:(i + 1) * P], kT[:, 4 * g + i, :], qT[:, 4 * g + i, :], start=True, stop=True)
                    mm.then_inc(s_done, 1)
                for g in range(2):
                    pe.wait_ge(qdT_ready, h * 2 + (g + 1))
                    pe.wait_ge(st_ready, h * 2 + (g + 1))
                    for i in range(4):
                        j = 4 * g + i
                        pe.matmul(po[g][:, i * P:(i + 1) * P], st[:, j, :], vqk[:, CT + j, 0:P], start=True, stop=False)
                        mm = pe.matmul(po[g][:, i * P:(i + 1) * P], qdT[:, j, :], state[:, j, :], start=False, stop=True)
                    mm.then_inc(o_done, 1)

        @block.scalar
        def _(act):
            with act.Fori(0, HEADS) as h:
                act.wait_ge(gate_in, h * 16 + 16)
                act.wait_ge(gate_ready, h * 2)
                act.activation(sig[:], raw_gate[:], ACT.Sigmoid).then_inc(g_sig, 1)
                for g in range(2):
                    act.wait_ge(turned, h * 4 + (g + 1))
                    act.activation(qT[:, 4 * g:4 * g + 4, :], tb[g][0:RDK, :].rearrange("p (i n) -> p i n", i=4), ACT.Copy).then_inc(qT_ready, 1)
                for g in range(2):
                    act.wait_ge(turned, h * 4 + (g + 3))
                    act.activation(qdT[:, 4 * g:4 * g + 4, :], tb[g][:].rearrange("p (i n) -> p i n", i=4), ACT.Copy).then_inc(qdT_ready, 1)
                for g in range(2):
                    act.wait_ge(o_done, h * 2 + (g + 1))
                    for i in range(4):
                        j = 4 * g + i
                        if j:
                            act.wait_ge(squared, h * LT + j)
                        act.activation(sq[:], po[g][:, i * P:(i + 1) * P], ACT.Square, accum_out=ms[:, j:j + 1]).then_inc(squared, 1)
                act.wait_ge(ms_ready, h + 1)
                act.activation(ms[:], ms[:], ACT.Sqrt).then_inc(root_ready, 1)

        @block.vector
        def _(v):
            v.wait_ge(trig_in, 32)
            with v.Fori(0, HEADS) as h:
                c = Steps(v, dve, h * DVE_STEPS)
                v.wait_ge(vqk_in, h * 16 + 16)
                a = vqk[:, CT:NT, P:].rearrange("p i (q f d) -> p i q f d", q=2, f=2)
                q4 = qk[:].rearrange("p i (q f d) -> p i q f d", q=2, f=2)
                cb = cos[:].unsqueeze(2).to_broadcast((P, LT, 2, HALF))
                sb = sin[:].unsqueeze(2).to_broadcast((P, LT, 2, HALF))
                c.did(v.tensor_tensor(rot[:, 0], a[:, :, :, 0, :], cb, ALU.mult))
                c.did(v.tensor_tensor(rot[:, 1], a[:, :, :, 1, :], sb, ALU.mult))
                c.did(v.tensor_tensor(rot[:, 2], a[:, :, :, 0, :], sb, ALU.mult))
                c.link(v.tensor_tensor(rot[:, 3], a[:, :, :, 1, :], cb, ALU.mult))
                c.did(v.tensor_tensor(q4[:, :, :, 0, :], rot[:, 0], rot[:, 1], ALU.subtract))
                v.tensor_tensor(q4[:, :, :, 1, :], rot[:, 2], rot[:, 3], ALU.add).then_inc(rotated, 1)
                v.wait_ge(rotated, h + 1)
                c.wait()
                v.wait_ge(decay_in, h * 32 + 32)
                for b in range(2):
                    c.did(v.tensor_scalar(kd[:, 0:CT, b * RDK:(b + 1) * RDK], vqk[:, 0:CT, 192:256], dcol[:, 2 + b:3 + b], None, ALU.mult))
                    c.did(v.tensor_scalar(kd[:, CT:, b * RDK:(b + 1) * RDK], qk[:, :, RDK:], dcol[:, 2 + b:3 + b], None, ALU.mult))
                    if b == 0:
                        c.did(v.tensor_scalar(qd[:, :, 0:RDK], qk[:, :, 0:RDK], dcol[:, 0:1], None, ALU.mult))
                v.tensor_scalar(qd[:, :, RDK:], qk[:, :, 0:RDK], dcol[:, 1:2], None, ALU.mult).then_inc(decayed, 1)
                for g in range(2):
                    v.wait_ge(turned, h * 4 + (g + 1))
                    v.tensor_copy(kT[:, 4 * g:4 * g + 4, :], tb[g][RDK:, :].rearrange("p (i n) -> p i n", i=4)).then_inc(kT_ready, 1)
                v.wait_ge(g_sig, h + 1)
                v.tensor_tensor(gate[:], raw_gate[:], sig[:], ALU.mult).then_inc(gate_ready, 2)
                v.wait_ge(u_done, h * 3 + 3)
                U = lambda b, i: pu[i // 4][b * RDK:(b + 1) * RDK, (i % 4) * P:(i % 4 + 1) * P]
                S = lambda b, j: state[b * RDK:(b + 1) * RDK, j, :]
                g0, g1 = dcol[0:RDK, 4:5], dcol[RDK:, 4:5]
                c.did(v.tensor_copy(S(0, LT), U(0, 0)))
                c.link(v.tensor_copy(S(1, LT), U(1, 1)))
                c.did(v.scalar_tensor_tensor(S(0, 0), S(0, LT), g0, U(0, 1), ALU.mult, ALU.add))
                c.link(v.scalar_tensor_tensor(S(1, LT - 1), S(1, LT), g1, U(1, 0), ALU.mult, ALU.add))
                for j in range(LT - 1):
                    n = LT - 1 - j
                    c.did(v.scalar_tensor_tensor(S(0, j + 1), S(0, j), g0, U(0, CT + j), ALU.mult, ALU.add))
                    c.link(v.scalar_tensor_tensor(S(1, n - 1), S(1, n), g1, U(1, CT + n), ALU.mult, ALU.add))
                assert c.n == STATES_AT
                for g in range(2):
                    v.wait_ge(s_done, h * 2 + (g + 1))
                    v.tensor_tensor(st[:, 4 * g:4 * g + 4, :], pu[g][:].rearrange("p (i n) -> p i n", i=4), decay[:].unsqueeze(1).to_broadcast((P, 4, P)), ALU.mult).then_inc(st_ready, 1)
                v.wait_ge(squared, h * LT + LT)
                v.tensor_scalar(ms[:], ms[:], 1.0 / P, EPS, ALU.mult, ALU.add).then_inc(ms_ready, 1)
                v.wait_ge(root_ready, h + 1)
                c.link(v.reciprocal(ms[:], ms[:]))
                v.wait_ge(o_out, h * 16)
                for j in range(LT):
                    v.scalar_tensor_tensor(o[:, j, :], po[j // 4][:, (j % 4) * P:(j % 4 + 1) * P], ms[:, j:j + 1], gate[:, j, :], ALU.mult, ALU.mult).then_inc(o_ready, 1)
                assert c.n == DVE_STEPS


def route(nc, m, dram, keep):
    with ExitStack() as ctx:
        t = Machine(nc, ctx)
        g1, g2 = t.sb("o_g1", [P, D]), t.sb("o_g2", [P, D])
        scale, shift = t.sb("o_scale", [P, D]), t.sb("o_shift", [P, D])
        fw = t.sb("o_fw", [P, D])
        rw = t.sb("o_rw", [P, KT, NE])
        rb = t.sb("o_rb", [P, NE])
        b2 = t.sb("o_b2", [NE, D])
        earlier = t.sb("o_earlier", [P, P])
        tokens = t.sb("o_tokens", [P, LT])
        experts = t.sb("o_experts", [P, NE])
        base = t.sb("o_base", [P, NE])
        ones = t.sb("o_ones", [P, P])
        mt = [t.sb(f"o_mt{j}", [P, D]) for j in range(2)]
        x = [t.sb(f"o_x{j}", [P, D]) for j in range(2)]
        mT = [t.sb(f"o_mT{j}", [P, KT, P]) for j in range(2)]
        h_ = t.sb("o_h", [P, LT, D])
        sq = t.sb("o_sq", [P, D])
        ms = [t.sb(f"o_ms{j}", [P, 1]) for j in range(2)]
        vv = [t.sb(f"o_v{j}", [P, D]) for j in range(2)]
        vT = t.sb("o_vT", [P, KT, P])
        n_parts = t.sb("o_n_parts", [NE, 1])
        lg = t.sb("o_lg", [P, LT, NE])
        top = t.sb("o_top", [P, LT, 8])
        topi = t.sb("o_topi", [P, LT, 8], U32)
        topf = t.sb("o_topf", [P, LT * TOPK])
        ex = t.sb("o_ex", [P, LT, TOPK])
        den = t.sb("o_den", [P, LT])
        pairs = t.sb("o_pairs", [P, LT, TOPK, 2])
        hot = t.sb("o_hot", [P, LT * TOPK, NE])
        pick = t.sb("o_pick", [P, LT * TOPK, NE])
        sel = t.sb("o_sel", [P, LT, NE])
        seen = t.sb("o_seen", [P, LT + 1, NE])
        dense = t.sb("o_dense", [P, LT, NE])
        denseT = t.sb("o_denseT", [NE, LT, P])
        place = t.sb("o_place", [P, LT, NE])
        dest = t.sb("o_dest", [P, LT * TOPK])
        desti = t.sb("o_desti", [P, LT * TOPK], U32)
        cnt = t.sb("o_cnt", [NE, 2])
        more = t.sb("o_more", [NE, 3, PARTS])
        units = t.sb("o_units", [NE, 4, UNITS])
        mine = t.sb("o_mine", [NE, PARTS, UNITS])
        iota = t.sb("o_iota", [NE, UNITS + 1 + 2 * PARTS])
        tb = [t.ps(f"o_tb{i}") for i in range(2)]
        py = [t.ps(f"o_py{j}", [P, 2, 512]) for j in range(2)]
        pl, pp = t.ps("o_pl"), t.ps("o_pp")
        names = """w_in late_in const_in dve turned mT_ready y_done h_ready squared ms_ready root_ready v_ready
        vT_ready logits_done lg_ready top_ready exped sel_ready placed_done dense_ready denseT_done denseT_ready bias_done out_ready
        sum_out dest_ready scattered seen_ready counted unit_step units_done s_passed""".split()
        S = {n: t.sem("o_" + n) for n in names}
        merged_in, x_in, v_out = ([t.sem(f"o_{n}{j}") for j in range(2)] for n in ("merged_in", "x_in", "v_out"))
        ident = keep["ident"]
        W = [keep["slots"][i][:].rearrange("p (k n) -> p k n", k=KT) for i in range(4)]
        ctx.callback(t.clear)
        block = ctx.enter_context(nc.Block())
        NCONST = 9
        STEPS = 2 * 3

        @block.sync
        def _(sp):
            wo = dram["w_out"][0].rearrange("(k p) n -> p k n", p=P)
            for j in range(4):
                sp.dma_start(W[j], wo[:, :, j * 256:(j + 1) * 256]).then_inc(S["w_in"], 16)
            sp.dma_start(rw[:], dram["router_w"][0].rearrange("(k p) e -> p k e", p=P)).then_inc(S["w_in"], 16)
            for n, dst in enumerate((g1, shift, scale, g2)):
                sp.dma_start(dst[:], dram["ada_rows"][:, n * D:(n + 1) * D].to_broadcast((P, D))).then_inc(S["const_in"], 16)
            sp.dma_start(fw[:], dram["norm_ffn_w"].to_broadcast((P, D))).then_inc(S["const_in"], 16)
            sp.dma_start(rb[:], dram["router_b"].to_broadcast((P, NE))).then_inc(S["const_in"], 16)
            sp.dma_start(b2[:], dram["b2"][0]).then_inc(S["late_in"], 16)
            sp.dma_start(earlier[:], dram["earlier"]).then_inc(S["late_in"], 16)
            sp.dma_start(tokens[:], dram["tokens"]).then_inc(S["const_in"], 16)
            sp.dma_start(experts[:], dram["experts"]).then_inc(S["const_in"], 16)
            sp.dma_start(iota[:], dram["unit_ids"]).then_inc(S["const_in"], 16)
            with sp.Fori(0, LT // 2) as t_:
                at = [sp.snap(t_ * (2 * P) + j * P) for j in range(2)]
                for j in range(2):
                    sp.wait_ge(S["turned"], t_ * 8)
                    alone(sp, S["s_passed"])
                    sp.wait_ge(S["h_ready"], t_ * 2)
                    alone(sp, S["s_passed"])
                    sp.dma_start(mt[j][:], dram["merged"][bass.ds(at[j], P), :]).then_inc(merged_in[j], 16)
                    sp.dma_start(x[j][:], dram["x"][0][bass.ds(at[j], P), :]).then_inc(x_in[j], 16)
                for j in range(2):
                    sp.wait_ge(S["v_ready"], t_ * 2 + (j + 1))
                    alone(sp, S["s_passed"])
                    sp.dma_start(dram["v_rows"][bass.ds(at[j], P), :], vv[j][:]).then_inc(v_out[j], 16)
            for i in range(LT):
                sp.wait_ge(S["out_ready"], i + 1)
                sp.dma_start(dram["sum"][i * P:(i + 1) * P, :], h_[:, i, :]).then_inc(S["sum_out"], 16)
            for j in range(2):
                sp.wait_ge(v_out[j], 8 * LT)
            sp.wait_ge(S["sum_out"], 16 * LT)

        @block.tensor
        def _(pe):
            pe.wait_ge(S["w_in"], 16 * 5)
            with pe.Fori(0, LT // 2) as t_:
                for j in range(2):
                    pe.wait_ge(merged_in[j], t_ * 16 + 16)
                    for n in range(2):
                        if j:
                            pe.wait_ge(S["mT_ready"], t_ * 4 + (n + 1))
                        else:
                            pe.wait_ge(S["vT_ready"], t_ * 4)
                        for k in range(4):
                            tt = pe.transpose(tb[n][:, k * P:(k + 1) * P], mt[j][:, (4 * n + k) * P:(4 * n + k + 1) * P], ident[:])
                        tt.then_inc(S["turned"], 1)
                    pe.wait_ge(S["mT_ready"], t_ * 4 + (2 * j + 2))
                    pe.wait_ge(S["h_ready"], t_ * 2)
                    for c in range(4):
                        for k in range(KT):
                            mm = pe.matmul(py[j][:, c // 2, (c % 2) * 256:(c % 2 + 1) * 256], mT[j][:, k, :], W[c][:, k, :], start=(k == 0), stop=(k == KT - 1))
                    mm.then_inc(S["y_done"], 1)
                for j in range(2):
                    pe.wait_ge(S["v_ready"], t_ * 2 + (j + 1))
                    for n in range(2):
                        if j:
                            pe.wait_ge(S["vT_ready"], t_ * 4 + (n + 1))
                        for k in range(4):
                            tt = pe.transpose(tb[n][:, k * P:(k + 1) * P], vv[j][:, (4 * n + k) * P:(4 * n + k + 1) * P], ident[:])
                        tt.then_inc(S["turned"], 1)
                    pe.wait_ge(S["vT_ready"], t_ * 4 + (2 * j + 2))
                    pe.wait_ge(S["lg_ready"], t_ * 2 + j)
                    for k in range(KT):
                        mm = pe.matmul(pl[:, 0:NE], vT[:, k, :], rw[:, k, :], start=(k == 0), stop=(k == KT - 1))
                    mm.then_inc(S["logits_done"], 1)
            pe.wait_ge(S["late_in"], 16 * 2)
            pe.wait_ge(S["sel_ready"], 1)
            pe.wait_ge(S["seen_ready"], 1 + LT)
            pe.matmul(pp[:, 0:LT * NE], earlier[:], sel[:].rearrange("p i e -> p (i e)"), start=True, stop=False)
            pe.matmul(pp[:, 0:LT * NE], ones[:], seen[:, 0:LT, :].rearrange("p i e -> p (i e)"), start=False, stop=True).then_inc(S["placed_done"], 1)
            pe.wait_ge(S["dense_ready"], 1)
            for i in range(LT):
                tt = pe.transpose(tb[i // 4][0:NE, (i % 4) * P:(i % 4 + 1) * P], dense[:, i, :], ident[:])
            tt.then_inc(S["denseT_done"], 1)
            pe.wait_ge(S["denseT_ready"], 2)
            for i in range(LT):
                if i >= 2:
                    pe.wait_ge(S["out_ready"], i - 1)
                for n in range(2):
                    mm = pe.matmul(py[i % 2][:, n, :], denseT[:, i, :], b2[:, n * 512:(n + 1) * 512], start=True, stop=True)
                mm.then_inc(S["bias_done"], 1)
            pe.matmul(pl[0:NE, 0:1], seen[:, LT, :], ones[:, 0:1], start=True, stop=True).then_inc(S["counted"], 1)
            pe.wait_ge(S["unit_step"], 1)
            pe.matmul(pl[0:NE, 0:1], earlier[0:NE, 0:NE], n_parts[:], start=True, stop=True).then_inc(S["counted"], 1)
            pe.wait_ge(S["unit_step"], 2)
            pe.matmul(pl[0:1, 0:4 * UNITS], ones[0:NE, 0:1], units[:].rearrange("e a u -> e (a u)"), start=True, stop=True).then_inc(S["counted"], 1)

        @block.scalar
        def _(act):
            with act.Fori(0, LT // 2) as t_:
                def root(j):
                    act.wait_ge(S["h_ready"], t_ * 2 + (j + 1))
                    act.wait_ge(S["squared"], t_ * 2 + j)
                    act.activation(sq[:], h_[:, bass.ds(t_ * 2 + j, 1), :].rearrange("p a n -> p (a n)"), ACT.Square, accum_out=ms[j][:]).then_inc(S["squared"], 1)
                    act.wait_ge(S["ms_ready"], t_ * 2 + (j + 1))
                    act.activation(ms[j][:], ms[j][:], ACT.Sqrt).then_inc(S["root_ready"], 1)

                def turned(j, what, to, ready):
                    for n in range(2):
                        act.wait_ge(S["turned"], t_ * 8 + (4 * what + 2 * j + n + 1))
                        if what:
                            act.wait_ge(S["logits_done"], t_ * 2 + j)
                        act.activation(to[:, 4 * n:4 * n + 4, :], tb[n][:].rearrange("p (k n) -> p k n", k=4), ACT.Copy).then_inc(S[ready], 1)

                turned(0, 0, mT[0], "mT_ready")
                turned(1, 0, mT[1], "mT_ready")
                root(0)
                turned(0, 1, vT, "vT_ready")
                root(1)
                turned(1, 1, vT, "vT_ready")
            act.wait_ge(S["top_ready"], 1)
            act.activation(ex[:], ex[:], ACT.Exp).then_inc(S["exped"], 1)
            act.wait_ge(S["denseT_done"], 1)
            for n in range(2):
                act.activation(denseT[:, 4 * n:4 * n + 4, :], tb[n][0:NE, :].rearrange("p (i n) -> p i n", i=4), ACT.Copy).then_inc(S["denseT_ready"], 1)

        @block.vector
        def _(v):
            v.memset(ones[:], 1.0).then_inc(S["units_done"], 1)
            v.memset(seen[:, 0, :], 0.0).then_inc(S["seen_ready"], 1)
            v.wait_ge(S["const_in"], 16 * NCONST)
            c = Steps(v, S["dve"])
            c.did(v.tensor_scalar(base[:], experts[:], float(SEQ), None, ALU.mult))
            c.link(v.scalar_tensor_tensor(scale[:], scale[:], 1.0, fw[:], ALU.add, ALU.mult))
            with v.Fori(0, LT // 2) as t_:
                c = Steps(v, S["dve"], t_ * STEPS + 2)
                for j in range(2):
                    h = h_[:, bass.ds(t_ * 2 + j, 1), :].rearrange("p a n -> p (a n)")
                    v.wait_ge(S["y_done"], t_ * 2 + (j + 1))
                    v.wait_ge(x_in[j], t_ * 16 + 16)
                    c.link(v.tensor_tensor(h, py[j][:].rearrange("p a n -> p (a n)"), g1[:], ALU.mult))
                    v.tensor_tensor(h, h, x[j][:], ALU.add).then_inc(S["h_ready"], 1)
                    v.wait_ge(S["squared"], t_ * 2 + (j + 1))
                    v.tensor_scalar(ms[j][:], ms[j][:], 1.0 / D, EPS, ALU.mult, ALU.add).then_inc(S["ms_ready"], 1)
                    v.wait_ge(S["root_ready"], t_ * 2 + (j + 1))
                    c.link(v.reciprocal(ms[j][:], ms[j][:]))
                    v.wait_ge(v_out[j], t_ * 16)
                    v.wait_ge(S["turned"], t_ * 8)
                    c.link(v.scalar_tensor_tensor(vv[j][:], h, ms[j][:], scale[:], ALU.mult, ALU.mult))
                    v.tensor_tensor(vv[j][:], vv[j][:], shift[:], ALU.add).then_inc(S["v_ready"], 1)
                for j in range(2):
                    v.wait_ge(S["logits_done"], t_ * 2 + (j + 1))
                    v.tensor_tensor(lg[:, bass.ds(t_ * 2 + j, 1), :].rearrange("p a e -> p (a e)"), pl[:, 0:NE], rb[:], ALU.add).then_inc(S["lg_ready"], 1)
                assert c.n == STEPS, c.n
            c = Steps(v, S["dve"], LT // 2 * STEPS + 2)
            v.wait_ge(S["lg_ready"], LT)
            for i in range(LT):
                c.did(v.max(out=top[:, i, :], in_=lg[:, i, :]))
            c.wait()
            for i in range(LT):
                c.did(v.max_index(out=topi[:, i, :], in_max=top[:, i, :], in_values=lg[:, i, :]))
            v.tensor_tensor(ex[:], top[:, :, 0:TOPK], top[:, :, 0:1].to_broadcast((P, LT, TOPK)), ALU.subtract).then_inc(S["top_ready"], 1)
            c.wait()
            c.link(v.tensor_copy(topf[:].rearrange("p (i k) -> p i k", k=TOPK), topi[:, :, 0:TOPK]))
            shape = (P, LT * TOPK, NE)
            by_tile = lambda a: a.rearrange("p (i k) e -> p i e k", k=TOPK)
            c.link(v.tensor_tensor(hot[:], experts[:].unsqueeze(1).to_broadcast(shape), topf[:].unsqueeze(2).to_broadcast(shape), ALU.is_equal))
            v.tensor_reduce(sel[:], by_tile(hot[:]), AX.X, ALU.add).then_inc(S["sel_ready"], 1)
            v.wait_ge(S["sel_ready"], 1)
            for i in range(LT):
                v.wait_ge(S["seen_ready"], i + 1)
                v.tensor_tensor(seen[:, i + 1, :], seen[:, i, :], sel[:, i, :], ALU.add).then_inc(S["seen_ready"], 1)
            v.wait_ge(S["exped"], 1)
            c.link(v.tensor_reduce(den[:], ex[:], AX.X, ALU.add))
            c.link(v.reciprocal(den[:], den[:]))
            c.did(v.tensor_copy(pairs[:, :, :, 0], tokens[:].unsqueeze(2).to_broadcast((P, LT, TOPK))))
            c.link(v.tensor_tensor(ex[:], ex[:], den[:].unsqueeze(2).to_broadcast((P, LT, TOPK)), ALU.mult))
            gates = ex[:].rearrange("p i k -> p (i k)")
            c.did(v.tensor_copy(pairs[:, :, :, 1], ex[:]))
            c.link(v.tensor_tensor(pick[:], hot[:], gates.unsqueeze(2).to_broadcast(shape), ALU.mult))
            v.tensor_reduce(dense[:], by_tile(pick[:]), AX.X, ALU.add).then_inc(S["dense_ready"], 1)
            v.wait_ge(S["placed_done"], 1)
            v.wait_ge(S["dense_ready"], 1)
            c.link(v.tensor_tensor(place[:], pp[:, 0:LT * NE].rearrange("p (i e) -> p i e", i=LT), base[:].unsqueeze(1).to_broadcast((P, LT, NE)), ALU.add))
            c.link(v.tensor_tensor(pick[:].rearrange("p (i k) e -> p i k e", k=TOPK), hot[:].rearrange("p (i k) e -> p i k e", k=TOPK),
                                   place[:].unsqueeze(2).to_broadcast((P, LT, TOPK, NE)), ALU.mult))
            c.link(v.tensor_reduce(dest[:], pick[:], AX.X, ALU.add))
            v.tensor_copy(desti[:], dest[:]).then_inc(S["dest_ready"], 1)
            for i in range(LT):
                v.wait_ge(S["bias_done"], i + 1)
                c.link(v.tensor_tensor(mt[i % 2][:], py[i % 2][:].rearrange("p a n -> p (a n)"), g2[:], ALU.mult))
                v.tensor_tensor(h_[:, i, :], h_[:, i, :], mt[i % 2][:], ALU.add).then_inc(S["out_ready"], 1)
            ids = iota[:, UNITS:UNITS + 1]
            begin, begin_all = iota[:, UNITS + 1:UNITS + 1 + PARTS], iota[:, UNITS + 1 + PARTS:]
            v.wait_ge(S["counted"], 1)
            c.link(v.tensor_copy(cnt[:, 0:1], pl[0:NE, 0:1]))
            c.link(v.tensor_tensor(more[:, 1, :], cnt[:, 0:1].to_broadcast((NE, PARTS)), begin, ALU.subtract))
            c.link(v.tensor_scalar(more[:, 0, :], more[:, 1, :], 0.0, None, ALU.is_gt))
            v.tensor_reduce(n_parts[:], more[:, 0, :], AX.X, ALU.add).then_inc(S["unit_step"], 1)
            v.wait_ge(S["unit_step"], 1)
            v.wait_ge(S["counted"], 2)
            c.link(v.tensor_copy(cnt[:, 1:2], pl[0:NE, 0:1]))
            c.link(v.tensor_tensor(more[:, 2, :], cnt[:, 1:2].to_broadcast((NE, PARTS)), iota[:, 0:PARTS], ALU.add))
            for j in range(PARTS):
                c.did(v.tensor_scalar(mine[:, j, :], iota[:, 0:UNITS], more[:, 2, j:j + 1], more[:, 0, j:j + 1], ALU.is_equal, ALU.mult))
            c.wait()
            c.link(v.tensor_reduce(keep["own"][0:NE], mine[:].rearrange("e j u -> e u j"), AX.X, ALU.add))
            c.did(v.tensor_copy(keep["own"][NE:], keep["own"][0:NE]))
            c.did(v.tensor_scalar(units[:, 0, :], keep["own"][0:NE], ids, None, ALU.mult))
            c.did(v.tensor_scalar(units[:, 2, :], iota[:, 0:UNITS], 0.0, n_parts[:], ALU.is_equal, ALU.mult))
            c.did(v.tensor_scalar(units[:, 1, :], mine[:, 0, :], more[:, 1, 0:1], None, ALU.mult))
            c.link(v.tensor_scalar(units[:, 3, :], mine[:, 0, :], begin_all[:, 0:1], None, ALU.mult))
            for j in range(1, PARTS):
                c.did(v.scalar_tensor_tensor(units[:, 1, :], mine[:, j, :], more[:, 1, j:j + 1], units[:, 1, :], ALU.mult, ALU.add))
                c.link(v.scalar_tensor_tensor(units[:, 3, :], mine[:, j, :], begin_all[:, j:j + 1], units[:, 3, :], ALU.mult, ALU.add))
            v.sem_inc(S["unit_step"], 1)
            v.wait_ge(S["counted"], 3)
            v.tensor_copy(keep["units"][:], pl[0:1, 0:4 * UNITS]).then_inc(S["units_done"], 1)
            v.wait_ge(S["units_done"], 2)

        @block.gpsimd
        def _(g):
            g.wait_ge(keep["emptied"], 32)
            g.wait_ge(S["dest_ready"], 1)
            for n in range(LT * TOPK):
                g.indirect_dma_start(dram["lists"], bass.IndirectOffsetOnAxis(ap=desti[:, n:n + 1], axis=0),
                                     pairs[:, n // TOPK, n % TOPK, :], None).then_inc(S["scattered"], 16)
            g.wait_ge(S["scattered"], 16 * TOPK * LT)


def experts(nc, m, dram, keep):
    with ExitStack() as ctx:
        t = Machine(nc, ctx)
        NB = CAP // P
        PIECES, RING = 12, 4
        KH = KT // 2
        more = [t.sb_twice(f"e_slot{i}", [P, WSLOT]) for i in range(SLOTS, PIECES)]
        raw = keep["slots"] + [x[0] for x in more]
        wlo = keep["slots_r"] + [x[1] for x in more]
        whi = [t.sb(f"e_whi{i}", [P, WSLOT], F32R) for i in range(RING)]
        xhi, xlo = t.sb("e_xhi", [P, KT, CAP], F32R), t.sb("e_xlo", [P, KT, CAP], F32R)
        ahi, alo = t.sb("e_ahi", [P, KT, CAP], F32R), t.sb("e_alo", [P, KT, CAP], F32R)
        xg = [t.sb(f"e_xg{i}", [P, D]) for i in range(NB)]
        yo = t.sb("e_yo", [P, NB, D])
        glu, lin, sig = (t.sb("e_" + n, [P, NB, 256]) for n in ("glu", "lin", "sig"))
        act_rows = [t.sb(f"e_act{i}", [P, NB, 256]) for i in range(2)]
        g2 = t.sb("e_g2", [P, D])
        spark = t.sb("e_spark", [1, 1])
        b1 = t.sb("e_b1", [2 * NE, 2 * D], F32R)
        pick = t.sb("e_pick", [2 * NE, P], F32R)
        lists = t.sb("e_lists", [P, NB, 2])
        idx_next = t.sb("e_idx_next", [P, NB], U32)
        idx_mid, gate_mid = t.sb("e_idx_mid", [P, NB], U32), t.sb("e_gate_mid", [P, NB])
        idx_now = t.sb("e_idx_now", [P, NB], U32)
        hb = [t.ps(f"e_hb{i}", [P, NB, 512]) for i in range(2)]
        yb = [t.ps("e_yb", [P, NB, 512]), hb[1]]
        tb = [t.ps(f"e_tb{i}") for i in range(2)]
        names = """const_in set b1_high b1_ready lists_in mid_ready next_ready now_ready pick_ready gates_ready whi_made wlo_dve wlo_pool
        piece_done glu_ready hid_taken sig_made lin_ready act_ready turned hi_made lo_made y_taken scattered
        g_passed a_passed s_passed""".split()
        S = {n: t.sem("e_" + n) for n in names}
        w_in = [t.sem(f"e_w_in{i}") for i in range(PIECES)]
        gath = [t.sem(f"e_gath{i}") for i in range(NB)]
        ident, U, own = keep["ident"], keep["units"], keep["own"]
        FIRST, GROUPS = 4, 8
        ACT_GROUP, ROW_GROUP = [0, 1, 2, 3], [4, 5, 6, 7]
        ctx.callback(t.clear)
        block = ctx.enter_context(nc.Block())

        def units_of(e):
            return e.snap(e.value_load(U[0:1, 2 * UNITS:2 * UNITS + 1], min_val=1, max_val=UNITS - 1))

        def expert_of(e, u):
            return e.value_load(U[0:1, bass.ds(u, 1)], min_val=0, max_val=NE - 1)

        def count_of(e, u):
            return e.value_load(U[0:1, bass.ds(u + UNITS, 1)], min_val=0, max_val=SEQ)

        def by_pool(i):
            return i % 3 == 2

        def wait_rest(e, i, u):
            if by_pool(i):
                e.wait_ge(S["wlo_pool"], u * (PIECES // 3) + (i + 1) // 3)
            else:
                e.wait_ge(S["wlo_dve"], u * (PIECES - PIECES // 3) + (i + 1 - (i + 1) // 3))

        def rest(e, i, u, done):
            e.wait_ge(S["whi_made"], u * PIECES + (i + 1))
            e.tensor_tensor(wlo[i % PIECES][:], raw[i % PIECES][:], whi[i % RING][:].bitcast(F32), ALU.subtract).then_inc(done, 1)

        @block.sync
        def _(sp):
            sp.dma_start(g2[:], dram["ada_rows"][:, 3 * D:].to_broadcast((P, D))).then_inc(S["const_in"], 16)
            for i in range(2):
                sp.dma_start(yo[i * NE:(i + 1) * NE].rearrange("p b n -> p (b n)"), dram["b1"][0]).then_inc(S["const_in"], 16)

            def load(i, e):
                w = (dram["w1"] if i < 8 else dram["w2"])[0][bass.ds(e, 1), :, :].rearrange("a (k p) n -> p (a k) n", p=P)[:, i % 2 * KH:(i % 2 + 1) * KH, :]
                to = raw[i][:].rearrange("p (k n) -> p k n", k=KH)
                if i < 8:
                    for f in range(2):
                        col = f * D + i // 2 * 256
                        sp.dma_start(to[:, :, f * 256:(f + 1) * 256], w[:, :, col:col + 256]).then_inc(w_in[i], 16)
                else:
                    col = (i // 2 - 4) * 512
                    sp.dma_start(to, w[:, :, col:col + 512]).then_inc(w_in[i], 32)

            n_units = units_of(sp)
            e0 = expert_of(sp, 0)
            for i in range(PIECES):
                load(i, e0)
            with sp.Fori(0, n_units) as u:
                en = expert_of(sp, u + 1)
                for i in range(PIECES):
                    sp.wait_ge(S["piece_done"], u * PIECES + (i + 1))
                    alone(sp, S["s_passed"])
                    load(i, en)
            for i in range(PIECES):
                sp.wait_ge(w_in[i], n_units * 32 + 32)
                alone(sp, S["s_passed"])

        @block.gpsimd
        def _(g):
            g.wait_ge(S["set"], NB)

            def load_lists(u):
                at = g.value_load(U[0:1, bass.ds(u + 3 * UNITS, 1)], min_val=0, max_val=NE * SEQ - CAP)
                g.dma_start(lists[:], dram["lists"][bass.ds(at, CAP), :].rearrange("(b p) c -> p b c", p=P)).then_inc(S["lists_in"], 16)

            def gather(b):
                g.indirect_dma_start(xg[b][:], None, dram["v_rows"], bass.IndirectOffsetOnAxis(ap=idx_next[:, b:b + 1], axis=0),
                                     bounds_check=SEQ - 1, oob_is_err=False).then_inc(gath[b], 16)

            n_units = units_of(g)
            load_lists(0)
            g.wait_ge(S["next_ready"], 1)
            for b in range(NB):
                gather(b)
            for i in range(RING):
                if by_pool(i):
                    rest(g, i, 0, S["wlo_pool"])
            with g.Fori(0, n_units) as u:
                g.wait_ge(S["mid_ready"], u + 1)
                alone(g, S["g_passed"])
                load_lists(u + 1)
                pieces = [i for i in range(RING, PIECES + RING) if by_pool(i)]
                rest(g, pieces[0], u, S["wlo_pool"])
                g.wait_ge(S["next_ready"], u + 2)
                g.wait_ge(S["turned"], u * GROUPS + FIRST)
                alone(g, S["g_passed"])
                for b in range(NB):
                    gather(b)
                for i in pieces[1:]:
                    rest(g, i, u, S["wlo_pool"])
                cnt = count_of(g, u)
                g.wait_ge(S["scattered"], u * (16 * NB))
                g.wait_ge(S["y_taken"], u * 2 + 2)
                g.wait_ge(S["now_ready"], u + 1)
                alone(g, S["g_passed"])

                def scatter(nb):
                    for b in range(nb):
                        n = 1 if b < nb - 1 else 1 + NB - nb
                        g.indirect_dma_start(dram["sum"], bass.IndirectOffsetOnAxis(ap=idx_now[:, b:b + 1], axis=0), yo[:, b, :], None,
                                             compute_op=ALU.add).then_inc(S["scattered"], 16 * n)

                with g.If(cnt > P):
                    scatter(2)
                with g.Else():
                    scatter(1)
            g.wait_ge(S["scattered"], n_units * (16 * NB))
            alone(g, S["g_passed"])

        def by_size(e, cnt, body):
            with e.If(cnt > P):
                body(2)
            with e.Else():
                body(1)

        @block.tensor
        def _(pe):
            n_units = units_of(pe)

            def turn_rows(g, base, loads):
                r = g - ROW_GROUP[0] if base is not None else g
                b, hf = r // 2, r % 2
                if hf == 0:
                    pe.wait_ge(gath[b], loads)
                if base is not None:
                    pe.wait_ge(S["lo_made"], base + (g - 1))
                elif g >= 2:
                    pe.wait_ge(S["lo_made"], g - 1)
                for k in range(4):
                    tt = pe.transpose(tb[g % 2][:, k * P:(k + 1) * P], xg[b][:, (4 * hf + k) * P:(4 * hf + k + 1) * P], ident[:])
                tt.then_inc(S["turned"], 1)

            for g in range(FIRST):
                turn_rows(g, None, 16)
            pe.wait_ge(S["b1_ready"], 1)
            with pe.Fori(0, n_units) as u:
                cnt = count_of(pe, u)
                base = u * GROUPS + FIRST

                def turn_act(p, nb):
                    g = ACT_GROUP[p]
                    pe.wait_ge(S["act_ready"], u * 4 + (p + 1))
                    pe.wait_ge(S["lo_made"], base + (g - 1))
                    for b in range(nb):
                        for q in range(2):
                            tt = pe.transpose(tb[g % 2][:, (2 * b + q) * P:(2 * b + q + 1) * P], act_rows[p % 2][:, b, q * P:(q + 1) * P], ident[:])
                    tt.then_inc(S["turned"], 1)

                def products(out, hi, lo, nb, i):
                    wait_rest(pe, i, u)
                    wh, wl = whi[i % RING][:], wlo[i][:]
                    for b in range(nb):
                        c = slice(b * P, (b + 1) * P)
                        for k in range(KH):
                            w, kk = slice(k * 512, (k + 1) * 512), i % 2 * KH + k
                            pe.matmul(out[:, b, :], hi[:, kk, c], wh[:, w], start=(i >= 8 and kk == 0), stop=False)
                            pe.matmul(out[:, b, :], hi[:, kk, c], wl[:, w], start=False, stop=False)
                            mm = pe.matmul(out[:, b, :], lo[:, kk, c], wh[:, w], start=False, stop=(kk == KT - 1))
                    mm.then_inc(S["piece_done"], 1)

                def body(nb):
                    pe.wait_ge(S["pick_ready"], u + 1)
                    for p in range(4):
                        if p == 0:
                            pe.wait_ge(S["lo_made"], base)
                            pe.wait_ge(S["hid_taken"], u * 4)
                        elif p == 1:
                            pe.wait_ge(S["y_taken"], u * 2)
                        else:
                            pe.wait_ge(S["hid_taken"], u * 4 + (p - 1))
                        out = hb[p % 2]
                        for b in range(nb):
                            pe.matmul(out[:, b, :], pick[:], b1[:].rearrange("e (f n) -> e f n", f=2)[:, :, p * 256:(p + 1) * 256], start=True, stop=False)
                        products(out, xhi, xlo, nb, 2 * p)
                        products(out, xhi, xlo, nb, 2 * p + 1)
                        if 1 <= p < 3:
                            turn_act(p - 1, nb)
                    pe.wait_ge(S["lo_made"], base + (ACT_GROUP[1] + 1))
                    products(yb[0], ahi, alo, nb, 8)
                    turn_act(2, nb)
                    turn_act(3, nb)
                    turn_rows(ROW_GROUP[0], base, u * 16 + 32)
                    pe.wait_ge(S["lo_made"], base + (ACT_GROUP[3] + 1))
                    products(yb[0], ahi, alo, nb, 9)
                    turn_rows(ROW_GROUP[1], base, u * 16 + 32)
                    turn_rows(ROW_GROUP[2], base, u * 16 + 32)
                    products(yb[1], ahi, alo, nb, 10)
                    turn_rows(ROW_GROUP[3], base, u * 16 + 32)
                    products(yb[1], ahi, alo, nb, 11)

                by_size(pe, cnt, body)

        @block.scalar
        def _(act):
            act.wait_ge(S["const_in"], 48)
            act.activation(b1[:], yo[0:2 * NE].rearrange("p b n -> p (b n)"), ACT.Copy).then_inc(S["b1_high"], 1)
            n_units = units_of(act)

            def high(i, u, ahead=True):
                act.wait_ge(w_in[i % PIECES], (u + i // PIECES) * 32 + 32)
                if ahead:
                    act.wait_ge(S["piece_done"], u * PIECES + (i - RING + 1))
                act.activation(whi[i % RING][:], raw[i % PIECES][:], ACT.Copy).then_inc(S["whi_made"], 1)

            def high_rows(r, parity, count):
                act.wait_ge(S["turned"], count)
                b, hf = r // 2, r % 2
                act.activation(xhi[:, 4 * hf:4 * hf + 4, b * P:(b + 1) * P], tb[parity][:].rearrange("p (k n) -> p k n", k=4), ACT.Copy).then_inc(S["hi_made"], 1)

            for r in range(FIRST):
                high_rows(r, r % 2, r + 1)
            for i in range(RING):
                high(i, 0, ahead=False)
            with act.Fori(0, n_units) as u:
                cnt = count_of(act, u)
                base = u * GROUPS + FIRST

                def high_act(p, nb):
                    g = ACT_GROUP[p]
                    act.wait_ge(S["turned"], base + (g + 1))
                    act.activation(ahi[:, 2 * p:2 * p + 2, 0:nb * P].rearrange("p q (b n) -> p b q n", b=nb),
                                   tb[g % 2][:, 0:nb * 256].rearrange("p (b q n) -> p b q n", b=nb, q=2), ACT.Copy).then_inc(S["hi_made"], 1)

                def body(nb):
                    act.wait_ge(S["a_passed"], u)
                    act.activation(spark[:], ident[0:1, 0:1], ACT.Sigmoid).then_inc(S["a_passed"], 1)
                    for p in range(4):
                        high(2 * p + RING, u)
                        act.wait_ge(S["glu_ready"], u * 4 + (p + 1))
                        act.activation(sig[:, 0:nb], glu[:, 0:nb], ACT.Sigmoid, scale=1.702).then_inc(S["sig_made"], 1)
                        if 1 <= p < 3:
                            high_act(p - 1, nb)
                        high(2 * p + RING + 1, u)
                    rows = lambda r: high_rows(r, ROW_GROUP[r] % 2, base + (ROW_GROUP[r] + 1))
                    high_act(2, nb)
                    high_act(3, nb)
                    rows(0)
                    high(8 + RING, u)
                    rows(1)
                    rows(2)
                    high(9 + RING, u)
                    rows(3)
                    high(10 + RING, u)
                    high(11 + RING, u)

                by_size(act, cnt, body)

        @block.vector
        def _(v):
            for x in xg:
                v.memset(x[:], 0.0).then_inc(S["set"], 1)
            v.wait_ge(S["b1_high"], 1)
            lo_rows = slice(NE, 2 * NE)
            v.tensor_tensor(b1[lo_rows], yo[lo_rows].rearrange("p b n -> p (b n)"), b1[lo_rows].bitcast(F32), ALU.subtract).then_inc(S["b1_ready"], 1)
            n_units = units_of(v)

            def next_index(loads):
                v.wait_ge(S["lists_in"], loads)
                v.tensor_copy(idx_next[:], lists[:, :, 0]).then_inc(S["next_ready"], 1)

            def low_rows(r, parity, count):
                v.wait_ge(S["hi_made"], count)
                b, hf = r // 2, r % 2
                to = (slice(None), slice(4 * hf, 4 * hf + 4), slice(b * P, (b + 1) * P))
                v.tensor_tensor(xlo[to], tb[parity][:].rearrange("p (k n) -> p k n", k=4), xhi[to].bitcast(F32), ALU.subtract).then_inc(S["lo_made"], 1)

            next_index(16)
            for r in range(FIRST):
                low_rows(r, r % 2, r + 1)
            for i in range(RING):
                if not by_pool(i):
                    rest(v, i, 0, S["wlo_dve"])
            v.tensor_copy(pick[:], own[:, 0:1].to_broadcast((2 * NE, P))).then_inc(S["pick_ready"], 1)
            with v.Fori(0, n_units) as u:
                cnt = count_of(v, u)
                base = u * GROUPS + FIRST
                v.wait_ge(S["next_ready"], u + 1)
                v.wait_ge(S["now_ready"], u)
                v.wait_ge(S["y_taken"], u * 2)
                v.tensor_copy(gate_mid[:], lists[:, :, 1]).then_inc(S["gates_ready"], 1)
                v.tensor_copy(idx_mid[:], idx_next[:]).then_inc(S["mid_ready"], 1)

                def low_act(p, nb):
                    g = ACT_GROUP[p]
                    v.wait_ge(S["hi_made"], base + (g + 1))
                    to = lambda x: x[:, 2 * p:2 * p + 2, 0:nb * P].rearrange("p q (b n) -> p b q n", b=nb)
                    v.tensor_tensor(to(alo), tb[g % 2][:, 0:nb * 256].rearrange("p (b q n) -> p b q n", b=nb, q=2), to(ahi).bitcast(F32),
                                    ALU.subtract).then_inc(S["lo_made"], 1)

                def rest_ahead(i):
                    if not by_pool(i + RING):
                        rest(v, i + RING, u, S["wlo_dve"])

                def body(nb):
                    for p in range(4):
                        g_, l_, s_ = glu[:, 0:nb], lin[:, 0:nb], sig[:, 0:nb]
                        h = hb[p % 2][:, 0:nb]
                        n = u * 4 + (p + 1)
                        rest_ahead(2 * p)
                        v.wait_ge(S["piece_done"], u * PIECES + (2 * p + 2))
                        v.tensor_scalar(g_, h[:, :, 0:256], LIMIT, None, ALU.min).then_inc(S["glu_ready"], 1)
                        v.tensor_scalar(l_, h[:, :, 256:512], LIMIT, -LIMIT, ALU.min, ALU.max).then_inc(S["hid_taken"], 1)
                        v.wait_ge(S["hid_taken"], n)
                        v.wait_ge(S["glu_ready"], n)
                        v.scalar_tensor_tensor(l_, l_, 1.0, g_, ALU.add, ALU.mult).then_inc(S["lin_ready"], 1)
                        v.wait_ge(S["lin_ready"], n)
                        v.wait_ge(S["sig_made"], n)
                        v.tensor_tensor(act_rows[p % 2][:, 0:nb], l_, s_, ALU.mult).then_inc(S["act_ready"], 1)
                        v.wait_ge(S["act_ready"], n)
                        if p == 0:
                            next_index(u * 16 + 32)
                        if 1 <= p < 3:
                            low_act(p - 1, nb)
                        rest_ahead(2 * p + 1)
                    rows = lambda r: low_rows(r, ROW_GROUP[r] % 2, base + (ROW_GROUP[r] + 1))

                    def take(j):
                        v.wait_ge(S["piece_done"], u * PIECES + (10 + 2 * j))
                        for b in range(nb):
                            x = v.scalar_tensor_tensor(yo[:, b, j * 512:(j + 1) * 512], yb[j][:, b, :], gate_mid[:, b:b + 1], g2[:, j * 512:(j + 1) * 512], ALU.mult, ALU.mult)
                        x.then_inc(S["y_taken"], 1)

                    v.tensor_copy(pick[:], own[:, bass.ds(u + 1, 1)].to_broadcast((2 * NE, P))).then_inc(S["pick_ready"], 1)
                    low_act(2, nb)
                    low_act(3, nb)
                    rows(0)
                    rest_ahead(8)
                    v.wait_ge(S["scattered"], u * (16 * NB))
                    v.wait_ge(S["mid_ready"], u + 1)
                    v.tensor_copy(idx_now[:], idx_mid[:]).then_inc(S["now_ready"], 1)
                    v.wait_ge(S["gates_ready"], u + 1)
                    rows(1)
                    rows(2)
                    take(0)
                    rest_ahead(9)
                    rows(3)
                    rest_ahead(10)
                    take(1)
                    rest_ahead(11)

                by_size(v, cnt, body)


def finish(nc, m, dram, keep):
    with ExitStack() as ctx:
        t = Machine(nc, ctx)
        x = t.sb("f_x", [P, LT, D])
        sq = t.sb("f_sq", [P, D])
        nw = t.sb("f_nw", [P, D])
        ms = t.sb("f_ms", [P, LT])
        w_in, squared, ms_ready, root_ready, inv_ready, ready, out = (t.sem("f_" + n) for n in ("w_in", "squared", "ms_ready", "root_ready", "inv_ready", "ready", "out"))
        x_in = [t.sem(f"f_x_in{i}") for i in range(LT)]
        ctx.callback(t.clear)
        block = ctx.enter_context(nc.Block())

        @block.sync
        def _(sp):
            for i in range(LT):
                sp.dma_start(x[:, i, :], dram["sum"][i * P:(i + 1) * P, :]).then_inc(x_in[i], 16)
            sp.dma_start(nw[:], dram["norm_final_w"].rearrange("(a n) -> a n", a=1).to_broadcast((P, D))).then_inc(w_in, 16)
            for i in range(LT):
                sp.wait_ge(ready, i + 1)
                sp.dma_start(dram["out"][0, i * P:(i + 1) * P, :], x[:, i, :]).then_inc(out, 16)
            sp.wait_ge(out, 16 * LT)

        @block.scalar
        def _(act):
            for i in range(LT):
                act.wait_ge(x_in[i], 16)
                if i:
                    act.wait_ge(squared, i)
                act.activation(sq[:], x[:, i, :], ACT.Square, accum_out=ms[:, i:i + 1]).then_inc(squared, 1)
            for i in range(LT):
                act.wait_ge(ms_ready, i + 1)
                act.activation(ms[:, i:i + 1], ms[:, i:i + 1], ACT.Sqrt).then_inc(root_ready, 1)

        @block.vector
        def _(v):
            v.wait_ge(w_in, 16)
            for i in range(LT):
                r = ms[:, i:i + 1]
                v.wait_ge(squared, i + 1)
                v.tensor_scalar(r, r, 1.0 / D, EPS, ALU.mult, ALU.add).then_inc(ms_ready, 1)
            for i in range(LT):
                r = ms[:, i:i + 1]
                v.wait_ge(root_ready, i + 1)
                v.reciprocal(r, r).then_inc(inv_ready, 1)
                v.wait_ge(inv_ready, i + 1)
                v.scalar_tensor_tensor(x[:, i, :], x[:, i, :], r, nw[:], ALU.mult, ALU.mult).then_inc(ready, 1)


IN = ["x", "c", "ctx", "c_ctx", "w_ada", "b_ada", "norm_mix_w", "norm_ffn_w", "w_in", "w_out", "hg_lb",
      "hg_norm_w", "router_w", "router_b", "w1", "b1", "w2", "b2", "norm_final_w"]


def build(nc, dram, stages=99):
    with ExitStack() as ctx:
        m = Machine(nc, ctx)
        dram["ada_rows"] = nc.dram_tensor("ada_rows", [1, 4 * D], F32, kind="Internal").ap()
        dram["v_rows"] = nc.dram_tensor("v_rows", [SEQ, D], F32, kind="Internal").ap()
        dram["sum"] = nc.dram_tensor("sum", [SEQ + CAP, D], F32, kind="Internal").ap()
        dram["lists"] = nc.dram_tensor("lists", [NE * SEQ, 2], F32, kind="Internal").ap()
        dram["projected"] = nc.dram_tensor("projected", [HEADS * TASKS, P, 256], F32, kind="Internal").ap()
        dram["merged"] = nc.dram_tensor("merged", [SEQ, D], F32, kind="Internal").ap()
        slots = [m.sb_twice(f"slot{i}", [P, WSLOT]) for i in range(SLOTS)]
        keep = dict(
            slots=[x[0] for x in slots], slots_r=[x[1] for x in slots],
            landed=[m.sem(f"landed{i}") for i in range(SLOTS)], released=[m.sem(f"released{i}") for i in range(SLOTS)],
            ident=m.sb("ident", [P, P]), const_in=m.sem("const_in"),
            lb=m.sb("lb", [P, 8]), oml=m.sb("oml", [P, 8]), lb_ready=m.sem("lb_ready"), emptied=m.sem("emptied"), bound_part=m.sem("bound_part"), u_ready=m.sem("u_ready"),
        )
        with ExitStack() as mix:
            keep["uT"] = Machine(nc, mix).sb("uT", [P, KT, N])
            modulate(nc, m, dram, keep)
            if stages >= 1:
                hgrn2(nc, m, dram, keep)
        if stages >= 2:
            retention(nc, m, dram, keep)
        keep["units"] = m.sb("units", [1, 4 * UNITS], I32)
        keep["own"] = m.sb("own", [2 * NE, UNITS])
        if stages >= 3:
            route(nc, m, dram, keep)
        if stages >= 4:
            experts(nc, m, dram, keep)
            finish(nc, m, dram, keep)


def kernel(**inputs):
    import concourse.bacc as bacc
    from concourse.bass_utils import run_bass_kernel_spmd

    nc = bacc.Bacc("TRN2", target_bir_lowering=False, num_devices=1)
    arrays, dram = {}, {}
    for prefix, names, source in (("in_", IN, inputs), ("c_", None, constants())):
        for name in names or source:
            a = np.ascontiguousarray(source[name])
            arrays[prefix + name] = a
            dram[name] = nc.dram_tensor(prefix + name, list(a.shape), mybir.dt.from_np(a.dtype), kind="ExternalInput").ap()
    dram["out"] = nc.dram_tensor("out", [1, SEQ, D], F32, kind="ExternalOutput").ap()
    build(nc, dram)
    r = run_bass_kernel_spmd(nc, [arrays], core_ids=[0])
    return r.results[0]["out"]
```
